# Optimizing a Trainium2 kernel written in Bass

```python
import math
import jax
import jax.numpy as jnp
from jax import lax
import numpy as np
import jax, jax.numpy as jnp

D_MODEL = 1024
BATCH = 1
SEQ = 256
DEPTH = 2

GRID_W = 64
CTX_LEN = 256
N_MIXERS = 4
HEAD_DIM = 64
ROPE_BASE = 10000.0
RMS_EPS = 1e-6
D_FF = ((8 * D_MODEL // 3 + 255) // 256) * 256
N_MOD = 6

DA_HEADS = D_MODEL // (2 * HEAD_DIM)
DA_VDIM = 2 * HEAD_DIM
Q_BLOCK = 128

SC_WIDTH = 3

WA_HEADS = D_MODEL // HEAD_DIM
WA_KV_HEADS = 4
WINDOW = 128
W_BLOCK = WINDOW

HG_EXPAND = 128
HG_HEADS = D_MODEL // HG_EXPAND
HG_DK = HG_EXPAND
HG_DV = D_MODEL // HG_HEADS
HG_FDIM = HG_HEADS * HG_DK
CHUNK = 64


def n_layers_of(mixer):
    return len(range(mixer, DEPTH, N_MIXERS))

def rmsnorm(x, g):
    x32 = x.astype(jnp.float32)
    y = x32 * lax.rsqrt(jnp.mean(x32 * x32, axis=-1, keepdims=True) + RMS_EPS)
    return y.astype(x.dtype) * g

def modulate(x, shift, scale):
    return x * (1.0 + scale) + shift

def swiglu(t, w_in, w_out):
    a, b = jnp.split(t @ w_in, 2, axis=-1)
    return (jax.nn.silu(a) * b) @ w_out

def rope_tables(n_tokens):
    rows = n_tokens // GRID_W
    row = jnp.repeat(jnp.arange(rows), GRID_W).astype(jnp.float32)
    col = jnp.tile(jnp.arange(GRID_W), rows).astype(jnp.float32)
    half = HEAD_DIM // 2
    inv_freq = 1.0 / (ROPE_BASE ** (jnp.arange(0, half, 2, dtype=jnp.float32) / half))
    ang = jnp.concatenate([row[:, None] * inv_freq, col[:, None] * inv_freq], axis=-1)
    return jnp.cos(ang), jnp.sin(ang)

def apply_rope_2d(x, cos, sin):
    n_mid = x.ndim - 3
    qd = HEAD_DIM // 4
    bshape = (cos.shape[0],) + (1,) * n_mid + (2, qd)
    cs, sn = cos.reshape(bshape), sin.reshape(bshape)
    xs = x.reshape(x.shape[:-1] + (2, 2, qd))
    x1, x2 = xs[..., 0, :], xs[..., 1, :]
    out = jnp.stack([x1 * cs - x2 * sn, x2 * cs + x1 * sn], axis=-2)
    return out.reshape(x.shape)

def sink_softmax(scores, sink):
    m = sink
    for s in scores:
        m = jnp.maximum(m, jnp.max(s, axis=-1, keepdims=True))
    es = [jnp.exp(s - m) for s in scores]
    den = jnp.exp(sink - m)
    for e in es:
        den = den + jnp.sum(e, axis=-1, keepdims=True)
    return [e / den for e in es]

def diff_attention(h, hc, wqkv, lam, subln_g, wo, cos, sin, layer_idx, need_ctx):
    B, L, _ = h.shape
    lam_init = 0.8 - 0.6 * math.exp(-0.3 * layer_idx)
    lam32 = lam.astype(jnp.float32)
    lam_full = (jnp.exp(jnp.sum(lam32[0] * lam32[1]))
                - jnp.exp(jnp.sum(lam32[2] * lam32[3])) + lam_init)
    scale = HEAD_DIM ** -0.5

    def project(t):
        n = t.shape[1]
        q, k, v = jnp.split(t @ wqkv, 3, axis=-1)
        return (q.reshape(B, n, DA_HEADS, 2, HEAD_DIM),
                k.reshape(B, n, DA_HEADS, 2, HEAD_DIM),
                v.reshape(B, n, DA_HEADS, DA_VDIM))

    def attend(qb, kk, vv):
        s = jnp.einsum('bqhmd,bkhmd->bhmqk', qb, kk).astype(jnp.float32) * scale
        p = jax.nn.softmax(s, axis=-1)
        p = p[:, :, 0] - lam_full * p[:, :, 1]
        return jnp.einsum('bhqk,bkhe->bqhe', p.astype(vv.dtype), vv)

    def readout(o):
        n = o.shape[1]
        o = rmsnorm(o, subln_g) * (1.0 - lam_init)
        return o.reshape(B, n, D_MODEL) @ wo

    q, k, v = project(h)
    q, k = apply_rope_2d(q, cos, sin), apply_rope_2d(k, cos, sin)
    qc, kc, vc = project(hc)
    k_all = jnp.concatenate([kc, k], axis=1)
    v_all = jnp.concatenate([vc, v], axis=1)
    nb = L // Q_BLOCK
    q_blocks = jnp.moveaxis(q.reshape(B, nb, Q_BLOCK, DA_HEADS, 2, HEAD_DIM), 1, 0)
    o = lax.map(lambda qb: attend(qb, k_all, v_all), q_blocks)
    o = jnp.moveaxis(o, 0, 1).reshape(B, L, DA_HEADS, DA_VDIM)
    y = readout(o)
    yc = readout(attend(qc, kc, vc)) if need_ctx else None
    return yc, y

def short_conv(h, hc, w_in, conv_w, w_out, need_ctx):
    pad = SC_WIDTH // 2

    def run(t):
        n = t.shape[1]
        b_gate, c_gate, u = jnp.split(t @ w_in, 3, axis=-1)
        z = c_gate * u
        zp = jnp.pad(z, ((0, 0), (pad, pad), (0, 0)))
        conv = conv_w[0] * zp[:, 0:n]
        for j in range(1, SC_WIDTH):
            conv = conv + conv_w[j] * zp[:, j:j + n]
        return (b_gate * conv) @ w_out

    y = run(h)
    yc = run(hc) if need_ctx else None
    return yc, y

def window_attention(h, hc, wqkv, sinks, wo, cos, sin, need_ctx):
    B, L, _ = h.shape
    G, R = WA_KV_HEADS, WA_HEADS // WA_KV_HEADS
    scale = HEAD_DIM ** -0.5
    qw, kw = WA_HEADS * HEAD_DIM, WA_KV_HEADS * HEAD_DIM

    def project(t):
        n = t.shape[1]
        qkv = t @ wqkv
        q = qkv[..., :qw].reshape(B, n, G, R, HEAD_DIM)
        k = qkv[..., qw:qw + kw].reshape(B, n, G, HEAD_DIM)
        v = qkv[..., qw + kw:].reshape(B, n, G, HEAD_DIM)
        return q, k, v

    sink = sinks.reshape(G, R).astype(jnp.float32)
    q, k, v = project(h)
    q, k = apply_rope_2d(q, cos, sin), apply_rope_2d(k, cos, sin)
    qc, kc, vc = project(hc)

    nb = L // W_BLOCK
    qb = q.reshape(B, nb, W_BLOCK, G, R, HEAD_DIM)

    def band(a):
        ab = jnp.pad(a.reshape(B, nb, W_BLOCK, G, HEAD_DIM), ((0, 0), (1, 1), (0, 0), (0, 0), (0, 0)))
        return jnp.concatenate([ab[:, :-2], ab[:, 1:-1], ab[:, 2:]], axis=2)

    kb, vb = band(k), band(v)
    q_pos = jnp.arange(nb)[:, None] * W_BLOCK + jnp.arange(W_BLOCK)[None, :]
    k_pos = (jnp.arange(nb)[:, None] - 1) * W_BLOCK + jnp.arange(3 * W_BLOCK)[None, :]
    rel = k_pos[:, None, :] - q_pos[:, :, None]
    valid = (jnp.abs(rel) <= WINDOW) & (k_pos[:, None, :] >= 0) & (k_pos[:, None, :] < L)

    s_win = jnp.einsum('bnqgrd,bnkgd->bngrqk', qb, kb).astype(jnp.float32) * scale
    s_win = jnp.where(valid[None, :, None, None], s_win, -jnp.inf)
    s_ctx = jnp.einsum('bnqgrd,bcgd->bngrqc', qb, kc).astype(jnp.float32) * scale
    p_ctx, p_win = sink_softmax([s_ctx, s_win], sink[None, None, :, :, None, None])
    o = (jnp.einsum('bngrqc,bcgd->bnqgrd', p_ctx.astype(vc.dtype), vc)
         + jnp.einsum('bngrqk,bnkgd->bnqgrd', p_win.astype(vb.dtype), vb))
    y = o.reshape(B, L, D_MODEL) @ wo

    yc = None
    if need_ctx:
        n = hc.shape[1]
        s_c = jnp.einsum('bqgrd,bcgd->bgrqc', qc, kc).astype(jnp.float32) * scale
        (p_c,) = sink_softmax([s_c], sink[None, :, :, None, None])
        oc = jnp.einsum('bgrqc,bcgd->bqgrd', p_c.astype(vc.dtype), vc)
        yc = oc.reshape(B, n, D_MODEL) @ wo
    return yc, y

def gla_scan(q, k, v, logf, s0, with_output):
    B, NH, T, _ = q.shape
    nc = T // CHUNK

    def chunks(a):
        return jnp.moveaxis(a.astype(jnp.float32).reshape(B, NH, nc, CHUNK, a.shape[-1]), 2, 0)

    tri = jnp.tril(jnp.ones((CHUNK, CHUNK), dtype=bool))[:, :, None]

    def step(S, xs):
        qc, kc, vc, gc = xs
        b = jnp.cumsum(gc, axis=2)
        b_end = b[:, :, -1:, :]
        S_next = (jnp.exp(b_end)[:, :, 0, :, None] * S
                  + jnp.einsum('bhsk,bhsv->bhkv', kc * jnp.exp(b_end - b), vc))
        if not with_output:
            return S_next, None
        rel = jnp.where(tri, b[:, :, :, None, :] - b[:, :, None, :, :], -jnp.inf)
        att = jnp.sum(qc[:, :, :, None, :] * kc[:, :, None, :, :] * jnp.exp(rel), axis=-1)
        o = att @ vc + jnp.einsum('bhtk,bhkv->bhtv', qc * jnp.exp(b), S)
        return S_next, o

    S_fin, o = lax.scan(step, s0, (chunks(q), chunks(k), chunks(v), chunks(logf)))
    if not with_output:
        return S_fin, None
    return S_fin, jnp.moveaxis(o, 0, 2).reshape(B, NH, T, v.shape[-1])

def hgrn2(h, hc, w_in, lb_param, gnorm_g, wo, layer_idx, need_ctx):
    B = h.shape[0]
    H = HG_HEADS
    p = jax.nn.softmax(lb_param.astype(jnp.float32), axis=1)
    lb = (jnp.cumsum(p, axis=1) - p[:, :1])[:, layer_idx][:, None, None, :]

    def gates(t):
        q, f_fw, f_bw, i_in, og = jnp.split(t @ w_in, 5, axis=-1)
        q = jax.nn.silu(q)
        f_pre = jnp.stack([f_fw, f_bw], axis=0).astype(jnp.float32)
        logf = jnp.logaddexp(jnp.log(lb), jnp.log1p(-lb) + jax.nn.log_sigmoid(f_pre))
        k = -jnp.expm1(logf)
        return q, k, i_in, logf, og

    def to_heads(a):
        return a.reshape(a.shape[0], a.shape[1], H, -1).transpose(0, 2, 1, 3)

    def both(a_fw, a_bw):
        return jnp.concatenate([to_heads(a_fw), jnp.flip(to_heads(a_bw), axis=2)], axis=1)

    def merge(o):
        return (o[:, :H] + jnp.flip(o[:, H:], axis=2)).transpose(0, 2, 1, 3)

    def readout(o, og):
        n = o.shape[1]
        o = rmsnorm(o.astype(h.dtype), gnorm_g) * jax.nn.silu(og).reshape(B, n, H, HG_DV)
        return o.reshape(B, n, D_MODEL) @ wo

    qc, kc, vc, gc, ogc = gates(hc)
    s0 = jnp.zeros((B, 2 * H, HG_DK, HG_DV), jnp.float32)
    S_ctx, o_ctx = gla_scan(both(qc, qc), both(kc[0], kc[1]), both(vc, vc), both(gc[0], gc[1]),
                            s0, need_ctx)
    q, k, v, g, og = gates(h)
    _, o = gla_scan(both(q, q), both(k[0], k[1]), both(v, v), both(g[0], g[1]), S_ctx, True)
    y = readout(merge(o), og)
    yc = readout(merge(o_ctx), ogc) if need_ctx else None
    return yc, y

def first_inputs(seed: int = 0) -> dict:
    key = jax.random.key(seed)
    keys = jax.random.split(key, 32)
    counter = [0]

    def nrm(shape, scale):
        k = keys[counter[0]]
        counter[0] += 1
        return jax.random.normal(k, shape, jnp.float32) * scale

    D, F = D_MODEL, D_FF
    nA, nB, nC, nD = n_layers_of(0), n_layers_of(1), n_layers_of(2), n_layers_of(3)
    wa_cols = (WA_HEADS + 2 * WA_KV_HEADS) * HEAD_DIM
    return {
        'x': nrm((BATCH, SEQ, D), 1.0),
        'c': nrm((BATCH, D), 1.0),
        'ctx': nrm((BATCH, CTX_LEN, D), 1.0),
        'c_ctx': nrm((D,), 1.0),
        'ada_w': nrm((DEPTH, D, N_MOD * D), 0.5 * D ** -0.5),
        'ada_b': nrm((DEPTH, N_MOD * D), 0.02),
        'norm1_g': 1.0 + nrm((DEPTH, D), 0.02),
        'norm2_g': 1.0 + nrm((DEPTH, D), 0.02),
        'ffn_w_in': nrm((DEPTH, D, 2 * F), D ** -0.5),
        'ffn_w_out': nrm((DEPTH, F, D), F ** -0.5),
        'final_g': 1.0 + nrm((D,), 0.02),
        'da_wqkv': nrm((nA, D, 3 * D), D ** -0.5),
        'da_lambda': nrm((nA, 4, HEAD_DIM), 0.1),
        'da_subln_g': 1.0 + nrm((nA, DA_VDIM), 0.02),
        'da_wo': nrm((nA, D, D), D ** -0.5),
        'sc_w_in': nrm((nB, D, 3 * D), D ** -0.5),
        'sc_conv_w': nrm((nB, SC_WIDTH, D), SC_WIDTH ** -0.5),
        'sc_w_out': nrm((nB, D, D), D ** -0.5),
        'wa_wqkv': nrm((nC, D, wa_cols), D ** -0.5),
        'wa_sinks': nrm((nC, WA_HEADS), 0.5),
        'wa_wo': nrm((nC, WA_HEADS * HEAD_DIM, D), D ** -0.5),
        'hg_w_in': nrm((nD, D, 5 * D), D ** -0.5),
        'hg_lb': nrm((2, DEPTH, HG_FDIM), 0.1),
        'hg_gnorm_g': 1.0 + nrm((nD, HG_DV), 0.02),
        'hg_wo': nrm((nD, D, D), D ** -0.5),
    }

def first_block(x, c, ctx, c_ctx, ada_w, ada_b, norm1_g, norm2_g, ffn_w_in, ffn_w_out, final_g,
              da_wqkv, da_lambda, da_subln_g, da_wo, sc_w_in, sc_conv_w, sc_w_out,
              wa_wqkv, wa_sinks, wa_wo, hg_w_in, hg_lb, hg_gnorm_g, hg_wo):
    B, L, _ = x.shape
    cos, sin = rope_tables(L)
    cos, sin = cos.astype(x.dtype), sin.astype(x.dtype)
    silu_c = jax.nn.silu(c)
    silu_cc = jax.nn.silu(c_ctx)[None, :]
    for i in range(DEPTH):
        mixer, slot = i % N_MIXERS, i // N_MIXERS
        need_ctx = i < DEPTH - 1
        mod = (silu_c @ ada_w[i] + ada_b[i])[:, None, :]
        mod_c = (silu_cc @ ada_w[i] + ada_b[i])[:, None, :]
        sh1, sc1, g1, sh2, sc2, g2 = jnp.split(mod, N_MOD, axis=-1)
        csh1, csc1, cg1, csh2, csc2, cg2 = jnp.split(mod_c, N_MOD, axis=-1)
        h = modulate(rmsnorm(x, norm1_g[i]), sh1, sc1)
        hc = modulate(rmsnorm(ctx, norm1_g[i]), csh1, csc1)
        if mixer == 0:
            yc, y = diff_attention(h, hc, da_wqkv[slot], da_lambda[slot], da_subln_g[slot],
                                   da_wo[slot], cos, sin, i, need_ctx)
        elif mixer == 1:
            yc, y = short_conv(h, hc, sc_w_in[slot], sc_conv_w[slot], sc_w_out[slot], need_ctx)
        elif mixer == 2:
            yc, y = window_attention(h, hc, wa_wqkv[slot], wa_sinks[slot], wa_wo[slot],
                                     cos, sin, need_ctx)
        else:
            yc, y = hgrn2(h, hc, hg_w_in[slot], hg_lb, hg_gnorm_g[slot], hg_wo[slot], i, need_ctx)
        x = x + g1 * y
        x = x + g2 * swiglu(modulate(rmsnorm(x, norm2_g[i]), sh2, sc2), ffn_w_in[i], ffn_w_out[i])
        if need_ctx:
            ctx = ctx + cg1 * yc
            ctx = ctx + cg2 * swiglu(modulate(rmsnorm(ctx, norm2_g[i]), csh2, csc2),
                                     ffn_w_in[i], ffn_w_out[i])
    return rmsnorm(x, final_g)


DEPTH_2 = 1

SSD_EXPAND = 2
D_SSD = SSD_EXPAND * D_MODEL
SSD_HEADDIM = 64
SSD_HEADS = D_SSD // SSD_HEADDIM
SSD_GROUPS = 8
SSD_STATE = 128
SSD_CONV = 4
SSD_CHUNK = 128
D_XBC = D_SSD + 2 * SSD_GROUPS * SSD_STATE
POOL_WINDOWS = (2, 4, 8, 16)
POOL_GROUPS = len(POOL_WINDOWS)
D_POOL = D_MODEL
POOL_GDIM = D_POOL // POOL_GROUPS
N_BRANCHES = 2
SPLIT_OFFSETS = (D_SSD, D_SSD + D_XBC, D_SSD + D_XBC + SSD_HEADS, D_SSD + D_XBC + SSD_HEADS + D_POOL)
D_IN_PROJ = D_SSD + D_XBC + SSD_HEADS + D_POOL + N_BRANCHES * D_MODEL
N_EXPERTS = 64
TOP_K = 8
N_EXPERT_GROUPS = 8
EXPERTS_PER_GROUP = N_EXPERTS // N_EXPERT_GROUPS
TOPK_GROUPS = 4
D_EXPERT = 256
D_SHARED = 256
ROUTED_SCALE = 2.5
MOE_BLOCK = 128
N_ADA = 6
EPS = 1e-6


def rmsnorm_2(x, g):
    xf = x.astype(jnp.float32)
    inv = lax.rsqrt(jnp.mean(xf * xf, axis=-1, keepdims=True) + EPS)
    return (xf * inv * g.astype(jnp.float32)).astype(x.dtype)

def modulate_2(x, shift, scale):
    return x * (1 + scale[:, None, :]) + shift[:, None, :]

def causal_dwconv(x, w, b):
    K, C = w.shape
    y = lax.conv_general_dilated(x, w[:, None, :].astype(x.dtype), window_strides=(1,),
                                 padding=[(K - 1, 0)], dimension_numbers=('NWC', 'WIO', 'NWC'),
                                 feature_group_count=C)
    return y + b

def segsum_exp(a):
    Q = a.shape[-1]
    cs = jnp.cumsum(a, axis=-1)
    diff = cs[..., :, None] - cs[..., None, :]
    mask = jnp.tril(jnp.ones((Q, Q), dtype=bool))
    return jnp.where(mask, jnp.exp(jnp.where(mask, diff, 0.0)), 0.0)

def ssd_chunked(xh, dt, A, Bm, Cm):
    Bsz, S, H, P = xh.shape
    G, N = Bm.shape[-2:]
    R = H // G
    Q = SSD_CHUNK
    nc = S // Q
    x = (xh * dt[..., None]).reshape(Bsz, nc, Q, G, R, P)
    a = (dt * A).reshape(Bsz, nc, Q, G, R).transpose(0, 1, 3, 4, 2)
    Bc = Bm.reshape(Bsz, nc, Q, G, N)
    Cc = Cm.reshape(Bsz, nc, Q, G, N)
    a_cs = jnp.cumsum(a, axis=-1)
    L = segsum_exp(a)
    CB = jnp.einsum('bclgn,bcsgn->bcgls', Cc, Bc)
    y_diag = jnp.einsum('bcgls,bcgrls,bcsgrp->bclgrp', CB, L, x)
    decay_states = jnp.exp(a_cs[..., -1:] - a_cs)
    states = jnp.einsum('bclgn,bcgrl,bclgrp->bcgrpn', Bc, decay_states, x)
    chunk_decay = jnp.exp(a_cs[..., -1])

    def step(carry, inp):
        st, dec = inp
        return carry * dec[..., None, None] + st, carry

    init = jnp.zeros(states.shape[:1] + states.shape[2:], states.dtype)
    _, prev = lax.scan(step, init, (jnp.moveaxis(states, 1, 0), jnp.moveaxis(chunk_decay, 1, 0)))
    prev = jnp.moveaxis(prev, 0, 1)
    y_off = jnp.einsum('bclgn,bcgrpn,bcgrl->bclgrp', Cc, prev, jnp.exp(a_cs))
    return (y_diag + y_off).reshape(Bsz, S, H, P)

def ssd_branch(z, xbc, dt_raw, conv_w, conv_b, dt_bias, A_log, D_skip, norm_g):
    xbc = jax.nn.silu(causal_dwconv(xbc, conv_w, conv_b))
    Bsz, S, _ = xbc.shape
    GN = SSD_GROUPS * SSD_STATE
    xs = xbc[..., :D_SSD].reshape(Bsz, S, SSD_HEADS, SSD_HEADDIM)
    Bm = xbc[..., D_SSD:D_SSD + GN].reshape(Bsz, S, SSD_GROUPS, SSD_STATE)
    Cm = xbc[..., D_SSD + GN:].reshape(Bsz, S, SSD_GROUPS, SSD_STATE)
    dt = jax.nn.softplus((dt_raw + dt_bias).astype(jnp.float32))
    A = -jnp.exp(A_log.astype(jnp.float32))
    y = ssd_chunked(xs, dt, A, Bm, Cm) + D_skip[:, None] * xs
    y = y.reshape(Bsz, S, D_SSD) * jax.nn.silu(z)
    y = rmsnorm_2(y.reshape(Bsz, S, SSD_GROUPS, D_SSD // SSD_GROUPS), norm_g.reshape(SSD_GROUPS, -1))
    return y.reshape(Bsz, S, D_SSD)

def pool_branch(xp, pool_w, pool_scale):
    Bsz, S, _ = xp.shape
    xg = xp.reshape(Bsz, S, POOL_GROUPS, POOL_GDIM).astype(jnp.float32)
    csp = jnp.pad(jnp.cumsum(xg, axis=1), ((0, 0), (1, 0), (0, 0), (0, 0)))
    pos = jnp.arange(1, S + 1, dtype=jnp.float32)
    outs = []
    for gi, w in enumerate(POOL_WINDOWS):
        c_g = csp[:, :, gi]
        lower = jnp.concatenate([jnp.zeros((Bsz, w - 1, POOL_GDIM), c_g.dtype), c_g[:, :S + 1 - w]], axis=1)
        mean = (c_g[:, 1:] - lower) / jnp.minimum(pos, w)[None, :, None]
        outs.append(mean - xg[:, :, gi])
    pooled = jnp.stack(outs, axis=2).astype(xp.dtype)
    mixed = jnp.einsum('bsgc,gcd->bsgd', pooled, pool_w)
    return mixed.reshape(Bsz, S, D_POOL) * pool_scale

def moe_ffn(u, w_router, router_bias, we_gate, we_up, we_down, ws_gate, ws_up, ws_down):
    Bsz, S, D = u.shape
    N = Bsz * S
    uf = u.reshape(N, D)
    scores = jax.nn.sigmoid((uf @ w_router).astype(jnp.float32))
    choice = scores + router_bias.astype(jnp.float32)
    grp = choice.reshape(N, N_EXPERT_GROUPS, EXPERTS_PER_GROUP)
    grp_score = lax.top_k(grp, 2)[0].sum(-1)
    _, top_grp = lax.top_k(grp_score, TOPK_GROUPS)
    grp_mask = jnp.any(top_grp[:, :, None] == jnp.arange(N_EXPERT_GROUPS)[None, None, :], axis=1)
    masked = jnp.where(jnp.repeat(grp_mask, EXPERTS_PER_GROUP, axis=1), choice, -jnp.inf)
    _, top_e = lax.top_k(masked, TOP_K)
    wts = jnp.take_along_axis(scores, top_e, axis=1)
    wts = wts / jnp.sum(wts, axis=-1, keepdims=True) * ROUTED_SCALE
    NK = N * TOP_K
    e_flat = top_e.reshape(NK).astype(jnp.int32)
    tok_flat = jnp.arange(NK, dtype=jnp.int32) // TOP_K
    order = jnp.argsort(e_flat)
    e_sorted = e_flat[order]
    counts = jax.ops.segment_sum(jnp.ones((NK,), jnp.int32), e_flat, num_segments=N_EXPERTS)
    padded = (counts + MOE_BLOCK - 1) // MOE_BLOCK * MOE_BLOCK
    starts = jnp.cumsum(counts) - counts
    pends = jnp.cumsum(padded)
    pstarts = pends - padded
    dest = pstarts[e_sorted] + jnp.arange(NK, dtype=jnp.int32) - starts[e_sorted]
    n_blocks = -(-NK // MOE_BLOCK) + N_EXPERTS
    n_slots = n_blocks * MOE_BLOCK
    slot_tok = jnp.full((n_slots,), N, jnp.int32).at[dest].set(tok_flat[order])
    slot_w = jnp.zeros((n_slots,), u.dtype).at[dest].set(wts.reshape(NK)[order].astype(u.dtype))
    block_e = jnp.minimum(jnp.searchsorted(pends, jnp.arange(n_blocks, dtype=jnp.int32) * MOE_BLOCK, side='right'),
                          N_EXPERTS - 1).astype(jnp.int32)
    u_pad = jnp.concatenate([uf, jnp.zeros((1, D), uf.dtype)], axis=0)

    def expert_block(args):
        toks, ws, e = args
        xb = u_pad[toks]
        hid = jax.nn.silu(xb @ we_gate[e]) * (xb @ we_up[e])
        return (hid @ we_down[e]) * ws[:, None]

    y_slots = lax.map(expert_block, (slot_tok.reshape(n_blocks, MOE_BLOCK),
                                     slot_w.reshape(n_blocks, MOE_BLOCK), block_e))
    routed = jax.ops.segment_sum(y_slots.reshape(n_slots, D), slot_tok, num_segments=N + 1)[:N]
    shared = (jax.nn.silu(uf @ ws_gate) * (uf @ ws_up)) @ ws_down
    return (routed + shared).reshape(Bsz, S, D)

def second_inputs(seed: int = 0) -> dict:
    key = jax.random.key(seed)
    ks = jax.random.split(key, 32)
    f32 = jnp.float32

    def nrm(k, shape, scale):
        return jax.random.normal(k, shape, f32) * scale

    dt0 = jnp.exp(jax.random.uniform(ks[8], (DEPTH_2, SSD_HEADS), f32, math.log(1e-3), math.log(1e-1)))
    return {
        'x': nrm(ks[0], (BATCH, SEQ, D_MODEL), 1.0),
        'c': nrm(ks[1], (BATCH, D_MODEL), 1.0),
        'w_ada': nrm(ks[2], (DEPTH_2, D_MODEL, N_ADA * D_MODEL), 0.5 * D_MODEL ** -0.5),
        'b_ada': nrm(ks[3], (DEPTH_2, N_ADA * D_MODEL), 0.02),
        'norm_mix_g': 1.0 + nrm(ks[4], (DEPTH_2, D_MODEL), 0.02),
        'w_in': nrm(ks[5], (DEPTH_2, D_MODEL, D_IN_PROJ), D_MODEL ** -0.5),
        'conv_w': nrm(ks[6], (DEPTH_2, SSD_CONV, D_XBC), SSD_CONV ** -0.5),
        'conv_b': nrm(ks[7], (DEPTH_2, D_XBC), 0.02),
        'dt_bias': dt0 + jnp.log(-jnp.expm1(-dt0)),
        'A_log': jnp.log(jax.random.uniform(ks[9], (DEPTH_2, SSD_HEADS), f32, 1.0, 16.0)),
        'D_skip': 1.0 + nrm(ks[10], (DEPTH_2, SSD_HEADS), 0.02),
        'ssd_norm_g': 1.0 + nrm(ks[11], (DEPTH_2, D_SSD), 0.02),
        'pool_w': nrm(ks[12], (DEPTH_2, POOL_GROUPS, POOL_GDIM, POOL_GDIM), POOL_GDIM ** -0.5),
        'pool_scale': 1.0 + nrm(ks[13], (DEPTH_2, D_POOL), 0.02),
        'w_br_ssd': nrm(ks[14], (DEPTH_2, D_SSD, D_MODEL), D_SSD ** -0.5),
        'w_br_pool': nrm(ks[15], (DEPTH_2, D_POOL, D_MODEL), D_POOL ** -0.5),
        'w_out': nrm(ks[16], (DEPTH_2, D_MODEL, D_MODEL), D_MODEL ** -0.5),
        'norm_ffn_g': 1.0 + nrm(ks[17], (DEPTH_2, D_MODEL), 0.02),
        'w_router': nrm(ks[18], (DEPTH_2, D_MODEL, N_EXPERTS), D_MODEL ** -0.5),
        'router_bias': nrm(ks[19], (DEPTH_2, N_EXPERTS), 0.01),
        'we_gate': nrm(ks[20], (DEPTH_2, N_EXPERTS, D_MODEL, D_EXPERT), D_MODEL ** -0.5),
        'we_up': nrm(ks[21], (DEPTH_2, N_EXPERTS, D_MODEL, D_EXPERT), D_MODEL ** -0.5),
        'we_down': nrm(ks[22], (DEPTH_2, N_EXPERTS, D_EXPERT, D_MODEL), D_EXPERT ** -0.5),
        'ws_gate': nrm(ks[23], (DEPTH_2, D_MODEL, D_SHARED), D_MODEL ** -0.5),
        'ws_up': nrm(ks[24], (DEPTH_2, D_MODEL, D_SHARED), D_MODEL ** -0.5),
        'ws_down': nrm(ks[25], (DEPTH_2, D_SHARED, D_MODEL), D_SHARED ** -0.5),
        'final_norm_g': 1.0 + nrm(ks[26], (D_MODEL,), 0.02),
    }

def second_block(x, c, w_ada, b_ada, norm_mix_g, w_in, conv_w, conv_b, dt_bias, A_log, D_skip, ssd_norm_g,
              pool_w, pool_scale, w_br_ssd, w_br_pool, w_out, norm_ffn_g, w_router, router_bias,
              we_gate, we_up, we_down, ws_gate, ws_up, ws_down, final_norm_g):
    h = x
    c_act = jax.nn.silu(c)
    for l in range(DEPTH_2):
        mod = c_act @ w_ada[l] + b_ada[l]
        sh1, sc1, g1, sh2, sc2, g2 = jnp.split(mod, N_ADA, axis=-1)
        u = modulate_2(rmsnorm_2(h, norm_mix_g[l]), sh1, sc1)
        proj = u @ w_in[l]
        z, xbc, dt_raw, xp, gts = jnp.split(proj, SPLIT_OFFSETS, axis=-1)
        y_ssd = ssd_branch(z, xbc, dt_raw, conv_w[l], conv_b[l], dt_bias[l], A_log[l], D_skip[l],
                           ssd_norm_g[l]) @ w_br_ssd[l]
        y_pool = pool_branch(xp, pool_w[l], pool_scale[l]) @ w_br_pool[l]
        g_ssd, g_pool = jnp.split(jax.nn.sigmoid(gts), N_BRANCHES, axis=-1)
        mixed = (g_ssd * y_ssd + g_pool * y_pool) @ w_out[l]
        h = h + g1[:, None, :] * mixed
        u2 = modulate_2(rmsnorm_2(h, norm_ffn_g[l]), sh2, sc2)
        h = h + g2[:, None, :] * moe_ffn(u2, w_router[l], router_bias[l], we_gate[l], we_up[l], we_down[l],
                                         ws_gate[l], ws_up[l], ws_down[l])
    return rmsnorm_2(h, final_norm_g)


def setup_inputs(seed=0):
    out = dict(first_inputs(seed))
    for name, value in second_inputs(seed + 1).items():
        if name != "x":
            out[name + "_2"] = value
    return out


def reference(
    x, c, ctx, c_ctx, ada_w, ada_b, norm1_g, norm2_g, ffn_w_in, ffn_w_out, final_g, da_wqkv,
    da_lambda, da_subln_g, da_wo, sc_w_in, sc_conv_w, sc_w_out, wa_wqkv, wa_sinks, wa_wo,
    hg_w_in, hg_lb, hg_gnorm_g, hg_wo, c_2, w_ada_2, b_ada_2, norm_mix_g_2, w_in_2, conv_w_2,
    conv_b_2, dt_bias_2, A_log_2, D_skip_2, ssd_norm_g_2, pool_w_2, pool_scale_2, w_br_ssd_2,
    w_br_pool_2, w_out_2, norm_ffn_g_2, w_router_2, router_bias_2, we_gate_2, we_up_2,
    we_down_2, ws_gate_2, ws_up_2, ws_down_2, final_norm_g_2,
):
    x = first_block(
        x, c, ctx, c_ctx, ada_w, ada_b, norm1_g, norm2_g, ffn_w_in, ffn_w_out, final_g, da_wqkv,
        da_lambda, da_subln_g, da_wo, sc_w_in, sc_conv_w, sc_w_out, wa_wqkv, wa_sinks, wa_wo,
        hg_w_in, hg_lb, hg_gnorm_g, hg_wo,
    )
    return second_block(
        x, c_2, w_ada_2, b_ada_2, norm_mix_g_2, w_in_2, conv_w_2, conv_b_2, dt_bias_2, A_log_2,
        D_skip_2, ssd_norm_g_2, pool_w_2, pool_scale_2, w_br_ssd_2, w_br_pool_2, w_out_2,
        norm_ffn_g_2, w_router_2, router_bias_2, we_gate_2, we_up_2, we_down_2, ws_gate_2,
        ws_up_2, ws_down_2, final_norm_g_2,
    )


_drawn_inputs = setup_inputs


def setup_inputs(seed=0):
    import zlib

    import numpy as np

    out = dict(_drawn_inputs(seed))
    spreads = {}
    factors = {'norm2_g': 2.961,
     'da_subln_g': 3.337,
     'norm_mix_g_2': 4.364,
     'conv_b_2': 27.408,
     'D_skip_2': 48.008,
     'ssd_norm_g_2': 39.874,
     'pool_scale_2': 12.378,
     'final_norm_g_2': 7.665,
     'norm_ffn_g_2': 5.221,
     'router_bias_2': 3.98}
    for name, (base, spread) in spreads.items():
        noise = np.random.default_rng([zlib.crc32(name.encode()), seed]).standard_normal(out[name].shape)
        drawn = base * np.exp(spread * noise) if base else spread * noise
        out[name] = jnp.asarray(drawn.astype(out[name].dtype))
    for name, factor in factors.items():
        out[name] = (out[name] * factor).astype(out[name].dtype)
    return out
```

```python
import math
from contextlib import ExitStack

import numpy as np
import concourse.bass as bass
import concourse.mybir as mybir

F32 = mybir.dt.float32
F32R = mybir.dt.float32r
ALU = mybir.AluOpType
ACT = mybir.ActivationFunctionType
AX = mybir.AxisListType.X

P = 128
T = 256
D = 1024
KD = D // P
FF = 2816
KF = FF // P
NE = 64
EPS = 1e-6
BIG = 1e30

SMALLS = {}
CONSTS = {}


def _layout(table, parts):
    at = 0
    for name, n in parts:
        table[name] = (at, n)
        at += n
    return at


N_SMALL = _layout(SMALLS, [
    ("c", 8), ("c_ctx", 8), ("c_2", 8), ("ada_b0", 48), ("ada_b1", 48), ("b_ada_2", 48),
    ("norm1_g0", 8), ("norm1_g1", 8), ("norm2_g0", 8), ("norm2_g1", 8), ("final_g", 8),
    ("subln", 1), ("sc_conv", 24), ("norm_mix", 8), ("conv_w", 128), ("conv_b", 32),
    ("dskip", 16), ("ssd_g", 16), ("pool_scale", 8), ("norm_ffn", 8), ("final_g2", 8),
    ("dt_bias", 32), ("a_log", 32), ("router_bias", 64), ("lam", 256),
])
N_CONST = _layout(CONSTS, [("ident", P), ("triu", P), ("cos", T), ("sin", T), ("invw", 64)])


class Engine:

    def __init__(self, sem):
        self.sem = sem
        self.count = 0
        self.todo = []
        self.seen = {}

    def wait(self, *tokens):
        for tok in tokens:
            if tok is None:
                continue
            sem, value = tok
            if self.seen.get(sem.name, 0) < value:
                self.seen[sem.name] = value
                self.todo.append(lambda e, s=sem, v=value: e.wait_ge(s, v))

    def op(self, fn, *waits):
        self.wait(*waits)
        self.count += 1
        self.todo.append(lambda e: fn(e).then_inc(self.sem, 1))
        return (self.sem, self.count)

    def quiet(self, fn, *waits):
        self.wait(*waits)
        self.todo.append(fn)

    def run(self, e):
        for fn in self.todo:
            fn(e)


def program(nc, I, out, plan):
    ctx = ExitStack()
    with ctx:
        def sb(name, shape, dt=F32):
            return ctx.enter_context(nc.sbuf_tensor(name, shape, dt))

        def sem(name):
            return ctx.enter_context(nc.semaphore(name))

        banks = [ctx.enter_context(nc.psum_tensor(f"bank{i}", [P, 512], F32)) for i in range(8)]
        pe, act, dve, pool, sp = (Engine(sem(f"s_{n}")) for n in ("pe", "act", "dve", "pool", "sp"))

        NRAW = 3
        NSPLIT = 2
        raw = [sb(f"raw{i}", [P, 2048]) for i in range(NRAW)]
        whi = [sb(f"whi{i}", [P, 2048], F32R) for i in range(NSPLIT)]
        wlo = [sb(f"wlo{i}", [P, 2048], F32R) for i in range(NSPLIT)]
        RR = sb("RR", [P, 15360], F32R)
        small = sb("small", [P, N_SMALL])
        const = sb("const", [P, N_CONST])
        ones_d = sb("ones_d", [P, P])
        ones_h = sb("ones_h", [P, P])
        ones_1 = sb("ones_1", [P, 1])
        ones_g = sb("ones_g", [P, P])
        xT = sb("xT", [P, KD, T])
        nsq = sb("nsq", [P, KD, T])
        nr = sb("nr", [P, T])
        vecs = sb("vecs", [P, 392])
        arena = sb("arena", [P, 12480])
        work = sb("work", [P, 4096])

        def sm(name, a=0, b=None):
            o, n = SMALLS[name]
            return small[:, o + a:o + (n if b is None else b)]

        def cn(name, a=0, b=None):
            o, n = CONSTS[name]
            return const[:, o + a:o + (n if b is None else b)]

        ident, triu = cn("ident"), cn("triu")

        def ar(at, *shape):
            n = int(np.prod(shape))
            v = arena[:, at:at + n]
            if len(shape) == 2:
                v = v.rearrange("p (a b) -> p a b", a=shape[0])
            elif len(shape) == 3:
                v = v.rearrange("p (a b c) -> p a b c", a=shape[0], b=shape[1])
            return v

        class Pair:

            def __init__(self, at, nk, w):
                n = nk * w
                self.hi = RR[:, at:at + n].rearrange("p (k w) -> p k w", k=nk)
                self.lo = RR[:, at + n:at + 2 * n].rearrange("p (k w) -> p k w", k=nk)

            def part(self, a, b):
                q = Pair.__new__(Pair)
                q.hi, q.lo = self.hi[:, :, a:b], self.lo[:, :, a:b]
                return q

            def at(self, k):
                return self.hi[:, k, :], self.lo[:, k, :]

        free = [None] * 8
        turn = [0]
        active = [list(range(8))]

        def bank():
            b = active[0][turn[0] % len(active[0])]
            turn[0] += 1
            pe.wait(free[b])
            free[b] = None
            return b

        raw_sem = [sem(f"s_raw{i}") for i in range(NRAW)]
        raw_count = [0] * NRAW
        raw_free = [()] * NRAW
        split_free = [None] * NSPLIT
        n_loaded = [0]
        n_split = [0]
        n_taken = [0]
        order = []
        ready = {}

        def source(spec):
            name, lead, k0, k1, c0, c1 = spec[:6]
            w = I[name] if lead is None else I[name][lead]
            if name == "pool_w_2":
                return w.rearrange("g (k p) n -> p (g k) n", p=P)
            return w[k0 * P:k1 * P, c0:c1].rearrange("(k p) n -> p k n", p=P)

        def fetch(spec):
            i = n_loaded[0] % NRAW
            n_loaded[0] += 1
            k0, k1, c0, c1 = spec[2:6]
            v = raw[i][:, 0:(k1 - k0) * (c1 - c0)].rearrange("p (k n) -> p k n", k=k1 - k0)
            sp.wait(*raw_free[i])
            sp.quiet(lambda e: e.dma_start(v, source(spec)).then_inc(raw_sem[i], 16))
            raw_count[i] += 16
            return i, v, (raw_sem[i], raw_count[i])

        def prepare(n):
            spec = plan[n]
            i, v, tok = fetch(spec)
            if spec[6] == "raw":
                ready[n] = (i, v, tok)
                return
            k, w = spec[3] - spec[2], spec[5] - spec[4]
            q = n_split[0] % NSPLIT
            n_split[0] += 1
            hi = whi[q][:, 0:k * w].rearrange("p (k n) -> p k n", k=k)
            lo = wlo[q][:, 0:k * w].rearrange("p (k n) -> p k n", k=k)
            toks = []
            h = (k + 1) // 2
            for a, b in ((0, h), (h, k)):
                t = act.op(lambda e, a=a, b=b: e.activation(hi[:, a:b, :], v[:, a:b, :], ACT.Copy), tok, split_free[q])
                t2 = dve.op(lambda e, a=a, b=b: e.tensor_tensor(lo[:, a:b, :], v[:, a:b, :], hi[:, a:b, :].bitcast(F32),
                                                                ALU.subtract), t, tok, split_free[q])
                toks += [t2] * (b - a)
            raw_free[i] = (t, t2)
            ready[n] = (q, hi, lo, toks)

        def tile(name, lead, k0, k1, c0, c1, kind="split"):
            spec = (name, lead, k0, k1, c0, c1, kind)
            n = n_taken[0]
            n_taken[0] += 1
            order.append(spec)
            if plan is None:
                v = raw[0][:, 0:(k1 - k0) * (c1 - c0)].rearrange("p (k n) -> p k n", k=k1 - k0)
                return (0, v, None) if kind == "raw" else (0, v, v, [None] * (k1 - k0))
            assert plan[n] == spec
            for m in range(n, min(n + AHEAD + 1, len(plan))):
                if m not in ready:
                    prepare(m)
            return ready.pop(n) if n in ready else None

        AHEAD = 1
        def mm(o, lhsT, rhs, start, stop, **kw):
            pe.quiet(lambda e: e.matmul(o, lhsT, rhs, start=start, stop=stop, **kw))

        def mm_end(o, lhsT, rhs, start, stop, **kw):
            return pe.op(lambda e: e.matmul(o, lhsT, rhs, start=start, stop=stop, **kw))

        def chain(o, pairs, first=True, last=True):
            tok = None
            for i, (l, r, *w) in enumerate(pairs):
                pe.wait(*w)
                tok = (mm_end if i == len(pairs) - 1 else mm)(
                    o, l, r, first and i == 0, last and i == len(pairs) - 1)
            return tok

        def products(w, x, *tok):
            (wh, wl), (xh, xl) = w, x
            return [(wh, xh, *tok), (wh, xl), (wl, xh)]

        def split_into(pair, src, *waits):
            toks = []
            nk = src.shape[1]
            step = max(1, 512 // src.shape[2])
            for k in range(0, nk, step):
                e_ = min(k + step, nk)
                t = act.op(lambda e, k=k, e_=e_: e.activation(pair.hi[:, k:e_, :], src[:, k:e_, :], ACT.Copy), *waits)
                t = dve.op(lambda e, k=k, e_=e_: e.tensor_tensor(pair.lo[:, k:e_, :], src[:, k:e_, :],
                                                                 pair.hi[:, k:e_, :].bitcast(F32), ALU.subtract), t, *waits)
                toks += [t] * (e_ - k)
            return toks

        s_in = sem("s_in")
        s_x = sem("s_x")
        s_cx = sem("s_cx")
        ctxT = ar(6144, KD, T)
        act.quiet(lambda e: e.dma_start(small[:, :], I["small"]).then_inc(s_in, 16))
        act.quiet(lambda e: e.dma_start(const[:, :], I["const"]).then_inc(s_in, 16))
        act.quiet(lambda e: e.dma_start(xT[:, :, :], I["xT"].rearrange("(k p) t -> p k t", p=P)).then_inc(s_x, 16))
        act.quiet(lambda e: e.dma_start(ctxT, I["ctxT"].rearrange("(k p) t -> p k t", p=P)).then_inc(s_cx, 16))
        t_in, t_x, t_cx = (s_in, 32), (s_x, 16), (s_cx, 16)
        t_ones = [pool.op(lambda e, m=m, v=v: e.memset(m[:, :], v))
                  for m, v in ((ones_1, 1.0), (ones_d, 1.0 / D), (ones_g, 1.0 / 256), (ones_h, 1.0 / P))]

        vec_at = [0]

        def vec(n):
            v = vecs[:, vec_at[0]:vec_at[0] + n]
            vec_at[0] += n
            assert vec_at[0] <= 392
            return v

        def silu_into(dst, src, *waits):
            return act.op(lambda e: e.activation(dst, src, ACT.Silu), *waits)

        cs3 = vec(24)
        t_c = silu_into(cs3, small[:, 0:24], t_in)
        c2s = cs3[:, 16:24]

        ada_acc = [ar(11520 + i * 256, 256) for i in range(2)]
        ada_used = [None, None]
        n_ada = [0]

        def ada(name, lead, c0, c1, conds, dst, bias):
            def step(i, toks):
                r, v, tok = tile(name, lead, 0, KD, c0 + i * P, c0 + (i + 2) * P, "raw")
                b = bank()
                done = []
                for n, cond in enumerate(conds):
                    eng = dve
                    q = n_ada[0] % 2
                    n_ada[0] += 1
                    acc = ada_acc[q]
                    t = eng.op(lambda e, acc=acc, cond=cond: e.tensor_scalar(acc[:, :], v[:, 0, :], cond[:, 0:1], None,
                                                                             ALU.mult), tok, t_c, ada_used[q])
                    for k in range(1, KD):
                        t = eng.op(lambda e, k=k, acc=acc, cond=cond: e.scalar_tensor_tensor(
                            out=acc[:, :], in0=v[:, k, :], scalar=cond[:, k:k + 1], in1=acc[:, :],
                            op0=ALU.mult, op1=ALU.add), t)
                    done.append(t)
                    pe.wait(t, t_ones[3])
                    for j in range(2):
                        t = mm_end(banks[b][:, 2 * n + j:2 * n + j + 1], acc[:, j * P:(j + 1) * P], ones_1[:, 0:1], True, True)
                    ada_used[q] = t
                raw_free[r] = tuple(done)
                for n in range(len(conds)):
                    o, src = dst[:, i:i + 2, n], banks[b][:, 2 * n:2 * n + 2]
                    free[b] = dve.op(lambda e, o=o, src=src: e.tensor_tensor(o, src, bias[:, i:i + 2], ALU.add), t, t_in)
                toks.append(free[b])

            toks = []
            return [lambda i=i: step(i, toks) for i in range(0, (c1 - c0) // P, 2)], toks

        behind = []

        def one_behind():
            if behind:
                behind.pop(0)()

        def all_behind():
            while behind:
                one_behind()

        def scale_vec(dst, g, sc, *waits):
            return dve.op(lambda e: e.scalar_tensor_tensor(out=dst, in0=sc, scalar=1.0, in1=g,
                                                           op0=ALU.add, op1=ALU.mult), *waits)

        def rsqrt(v, y, u, *waits):
            t = act.op(lambda e: e.activation(y, v, ACT.Ln), *waits)
            t = act.op(lambda e: e.activation(y, y, ACT.Exp, scale=-0.5), t)
            t = dve.op(lambda e: e.scalar_tensor_tensor(out=u, in0=v, scalar=-0.5, in1=y, op0=ALU.mult, op1=ALU.mult), t)
            t = dve.op(lambda e: e.tensor_tensor(u, u, y, ALU.mult), t)
            return dve.op(lambda e: e.scalar_tensor_tensor(out=y, in0=u, scalar=1.5, in1=y, op0=ALU.add, op1=ALU.mult), t)

        def mean_sq(o, ones, nk, sq, *waits):
            pe.wait(t_ones[3], *waits)
            b = bank()
            t = chain(banks[b][:, 0:T], [(ones[:, :], sq[:, k, :]) for k in range(nk)])
            free[b] = dve.op(lambda e: e.tensor_scalar(o, banks[b][:, 0:T], EPS, None, ALU.add), t)
            return free[b]

        def norm_mod(src, a, sh, dst, *waits):
            t = act.op(lambda e: e.activation(nsq[:, :, :], src, ACT.Square), *waits)
            t = mean_sq(nsq[:, 0, :], ones_d, KD, nsq, t)
            t = rsqrt(nsq[:, 0, :], nr[:, :], nsq[:, 1, :], t)
            o = nsq if dst is None or isinstance(dst, Pair) else dst
            toks = []
            rb = nr[:, :].rearrange("p (o t) -> p o t", o=1).to_broadcast([P, 2, T])
            for k in range(0, KD, 2):
                t1 = dve.op(lambda e, k=k: e.tensor_tensor(nsq[:, k:k + 2, :], src[:, k:k + 2, :], rb, ALU.mult), t)
                for j in (k, k + 1):
                    if sh is None:
                        t2 = dve.op(lambda e, j=j: e.tensor_scalar(o[:, j, :], nsq[:, j, :], a[:, j:j + 1], None,
                                                                   ALU.mult), t1)
                    else:
                        t2 = dve.op(lambda e, j=j: e.tensor_scalar(o[:, j, :], nsq[:, j, :], a[:, j:j + 1],
                                                                   sh[:, j:j + 1], ALU.mult, ALU.add), t1)
                if isinstance(dst, Pair):
                    q = Pair.__new__(Pair)
                    q.hi, q.lo = dst.hi[:, k:k + 2, :], dst.lo[:, k:k + 2, :]
                    toks += split_into(q, nsq[:, k:k + 2, :], t2)
                else:
                    toks += [t2, t2]
            return toks

        def project(name, lead, x, nk, consume, waits, c0=0, n=D):
            for cc in range(0, n, 256):
                bs = [bank(), bank()]
                for k0 in range(0, nk, KD):
                    k1 = min(k0 + KD, nk)
                    q, hi, lo, tw = tile(name, lead, k0, k1, c0 + cc, c0 + cc + 256)
                    for j in range(2):
                        pairs = []
                        for k in range(k0, k1):
                            cs = slice(j * P, (j + 1) * P)
                            pe_w = (tw[k - k0], waits[k])
                            pairs += products((hi[:, k - k0, cs], lo[:, k - k0, cs]), x.at(k), *pe_w)
                        t = chain(banks[bs[j]][:, 0:T], pairs, first=k0 == 0, last=k1 == nk)
                        if k1 == nk:
                            if j == 1:
                                split_free[q] = t
                            consume(cc // P + j, bs[j], t)
                    split_free[q] = t

        def add_gated(g):
            toks = []

            def consume(n, b, t):
                t = dve.op(lambda e: e.scalar_tensor_tensor(out=xT[:, n, :], in0=banks[b][:, 0:T],
                                                            scalar=g[:, n:n + 1], in1=xT[:, n, :],
                                                            op0=ALU.mult, op1=ALU.add), t)
                free[b] = t
                toks.append(t)
            return consume, toks

        gate_tmp = [work[:, i * 512:(i + 1) * 512] for i in range(4)]
        gate_used = [None] * 4
        n_gate = [0]

        def gated(pair, k, a, b, t_a, t_b, extra=None):
            i = n_gate[0] % 4
            n_gate[0] += 1
            n = a.shape[1]
            tmp = gate_tmp[i][:, 0:n * T].rearrange("p (x y) -> p x y", x=n)
            ta = act.op(lambda e: e.activation(tmp, a, ACT.Silu), t_a, gate_used[i])

            def finish(b, t_b):
                tb = dve.op(lambda e: e.tensor_tensor(tmp, b, tmp, ALU.mult), ta, t_b)
                t = tb
                if extra is not None:
                    t = dve.op(lambda e: e.tensor_tensor(tmp, tmp, extra[0], ALU.mult), tb, extra[1])
                q = Pair.__new__(Pair)
                q.hi, q.lo = pair.hi[:, k:k + n, :], pair.lo[:, k:k + n, :]
                toks = split_into(q, tmp, t)
                gate_used[i] = toks[-1]
                return tb, toks
            return ta, finish

        def ffn(layer, h, t_h, consume):
            hid = Pair(4096, KF, T)
            toks = []
            for c in range(FF // 256):
                fin = []
                for half in range(2):
                    q, hi, lo, tw = tile("ffn_w_in", layer, 0, KD, half * FF + c * 256, half * FF + c * 256 + 256)
                    for j in range(2):
                        b = bank()
                        pairs = []
                        for k in range(KD):
                            cs = slice(j * P, (j + 1) * P)
                            pairs += products((hi[:, k, cs], lo[:, k, cs]), h.at(k), tw[k], t_h[k])
                        t = chain(banks[b][:, 0:T], pairs)
                        ps = banks[b][:, 0:T].rearrange("p (o t) -> p o t", o=1)
                        if half == 0:
                            free[b], f = gated(hid, 2 * c + j, ps, None, t, None)
                            fin.append(f)
                        else:
                            free[b], tk = fin[j](ps, t)
                            toks += tk
                    split_free[q] = t
                one_behind()
            project("ffn_w_out", layer, hid, KF, consume, toks)

        mod0 = vec(32).rearrange("p (b n) -> p b n", n=2)
        steps, toks = ada("ada_w", 0, 0, 2048, [cs3[:, 0:8], cs3[:, 8:16]], mod0, sm("ada_b0", 0, 16))
        behind += steps
        all_behind()
        t_mod = toks[-1]
        sh_x, sh_c = vec(8), vec(8)
        a_x, a_c = vec(8), vec(8)
        t1 = dve.op(lambda e: e.tensor_copy(sh_x, mod0[:, 0:8, 0]), t_mod)
        t2 = dve.op(lambda e: e.tensor_copy(sh_c, mod0[:, 0:8, 1]), t_mod)
        t3 = scale_vec(a_x, sm("norm1_g0"), mod0[:, 8:16, 0], t_mod)
        t4 = scale_vec(a_c, sm("norm1_g0"), mod0[:, 8:16, 1], t_mod)
        dve.wait(t4)
        hcat = Pair(0, KD, 512)
        t_hx = norm_mod(xT[:, :, :], a_x, sh_x, hcat.part(256, 512), t_x)
        t_hc = norm_mod(ctxT, a_c, sh_c, hcat.part(0, 256), t_cx, t_hx[-1])

        qT = ar(0, KD, T)
        kT = ar(2048, KD, 512)
        vv = ar(6144, 4, 1024)
        pT = [work[:, i * 1024:(i + 1) * 1024].rearrange("p (k q) -> p k q", k=4) for i in range(2)]
        oT = nsq[:, :, :]
        pexp = [[work[:, 2048 + i * 1024 + m * 512:2560 + i * 1024 + m * 512] for m in range(2)] for i in range(2)]
        pcomb = [ar(10240 + i * 512, 512) for i in range(2)]
        SWAP = [i ^ 16 for i in range(32)]
        rt = [work[:, i * 512:i * 512 + 256] for i in range(4)]
        ru = [work[:, i * 512 + 256:i * 512 + 512] for i in range(4)]
        rt_used = [None] * 4
        n_rope = [0]

        def rope(dst, src, t):
            i = n_rope[0] % 4
            n_rope[0] += 1
            a, b = rt[i], ru[i]
            t0 = act.op(lambda e: e.activation(a, src, ACT.Copy), t, rt_used[i])
            t1 = dve.op(lambda e: e.stream_shuffle(b, a, SWAP), t0)
            t1 = dve.op(lambda e: e.tensor_tensor(b, b, cn("sin"), ALU.mult), t1)
            t2 = dve.op(lambda e: e.tensor_tensor(a, a, cn("cos"), ALU.mult), t1)
            t3 = dve.op(lambda e: e.tensor_tensor(dst, a, b, ALU.add), t2)
            rt_used[i] = t3
            return t0, t3

        t_q = {}

        def take_q(n, b, t):
            free[b], t_q[n] = rope(qT[:, n, :], banks[b][:, 0:T], t)

        project("da_wqkv", None, hcat.part(256, 512), KD, take_q, t_hx)
        t_k = {}
        for cc in range(0, D, 256):
            q, hi, lo, tw = tile("da_wqkv", None, 0, KD, D + cc, D + cc + 256)
            for j in range(2):
                n = cc // P + j
                b = bank()
                pairs = []
                for k in range(KD):
                    cs = slice(j * P, (j + 1) * P)
                    pairs += products((hi[:, k, cs], lo[:, k, cs]), hcat.at(k), tw[k], t_hc[k])
                t = chain(banks[b][:, :], pairs)
                if j == 1:
                    split_free[q] = t
                tc = act.op(lambda e, b=b, n=n: e.activation(kT[:, n, 0:256], banks[b][:, 0:256], ACT.Copy), t)
                free[b], t_k[n] = rope(kT[:, n, 256:512], banks[b][:, 256:512], t)
        t_v = None
        for cc in range(0, D, 256):
            q, hi, lo, tw = tile("da_wqkv", None, 0, KD, 2 * D + cc, 2 * D + cc + 256)
            for m in range(4):
                b = bank()
                pairs = []
                for k in range(KD):
                    xh, xl = hcat.hi[:, k, m * P:(m + 1) * P], hcat.lo[:, k, m * P:(m + 1) * P]
                    pairs += products((xh, xl), (hi[:, k, :], lo[:, k, :]), tw[k], t_hc[k])
                t = chain(banks[b][:, 0:256], pairs)
                t_v = act.op(lambda e, b=b, m=m, cc=cc: e.activation(vv[:, m, cc:cc + 256], banks[b][:, 0:256], ACT.Copy), t)
                free[b] = t_v
            split_free[q] = t

        lam2 = vec(2)
        lamx = vec(2)
        lamn = vec(1)
        lp = ar(11264, 128).rearrange("p (a d) -> p a d", a=2)
        l4 = sm("lam").rearrange("p (a b d) -> p a b d", a=2, b=2)
        t = dve.op(lambda e: e.tensor_tensor(lp, l4[:, :, 0, :], l4[:, :, 1, :], ALU.mult), t_in)
        t = dve.op(lambda e: e.tensor_reduce(lam2, lp, AX, ALU.add), t)
        t = act.op(lambda e: e.activation(lamx, lam2, ACT.Exp), t)
        LAM_INIT = 0.8 - 0.6 * math.exp(-0.3 * 0)
        t = dve.op(lambda e: e.tensor_tensor(lamn, lamx[:, 1:2], lamx[:, 0:1], ALU.subtract), t)
        t_lam = dve.op(lambda e: e.tensor_scalar(lamn, lamn, -LAM_INIT, None, ALU.add), t)
        sub_g = vec(1)
        t_subg = dve.op(lambda e: e.tensor_scalar(sub_g, sm("subln"), 1.0 - LAM_INIT, None, ALU.mult), t_in)

        SCALE = 64 ** -0.5
        stat = vec(64)
        pe.wait(t_v)
        act.wait(t_k[7])
        t_o = {}
        units = [(h, qb) for h in range(8) for qb in range(2)]
        comb_tok = {}
        comb_free = [None, None]
        pT_free = [None, None]
        evac_tok = {}

        modr0 = vec(32)
        steps, toks0 = ada("ada_w", 0, 2048, 6144, [cs3[:, 0:8]],
                           modr0.rearrange("p (b n) -> p b n", n=1), sm("ada_b0", 16, 48))
        behind += steps

        def scores(u):
            h, qb = units[u]
            pe.wait(t_q[h], t_k[h])
            st = stat[:, (u % 4) * 8:(u % 4) * 8 + 8]
            ends = []
            for m in range(2):
                b = bank()
                t = mm_end(banks[b][:, :], qT[m * 64:m * 64 + 64, h, qb * P:qb * P + P],
                           kT[m * 64:m * 64 + 64, h, :], True, True)
                t = dve.op(lambda e, b=b, m=m: e.tensor_reduce(st[:, m:m + 1], banks[b][:, :], AX, ALU.max), t)
                t = dve.op(lambda e, m=m: e.tensor_scalar(st[:, 2 + m:3 + m], st[:, m:m + 1], -SCALE, None, ALU.mult), t)
                t = act.op(lambda e, b=b, m=m: e.activation(pexp[u % 2][m], banks[b][:, :], ACT.Exp,
                                                            bias=st[:, 2 + m:3 + m], scale=SCALE,
                                                            accum_out=st[:, 4 + m:5 + m]), t, comb_free[u % 2])
                free[b] = t
                ends.append(t)
            return ends

        def combine(u, ends):
            st = stat[:, (u % 4) * 8:(u % 4) * 8 + 8]
            t = dve.op(lambda e: e.reciprocal(st[:, 6:8], st[:, 4:6]), *ends)
            t1 = dve.op(lambda e: e.tensor_tensor(st[:, 7:8], st[:, 7:8], lamn, ALU.mult), t, t_lam)
            t2 = dve.op(lambda e: e.tensor_scalar(pexp[u % 2][0], pexp[u % 2][0], st[:, 6:7], None, ALU.mult), t)
            comb_tok[u] = dve.op(lambda e: e.scalar_tensor_tensor(
                out=pcomb[u % 2], in0=pexp[u % 2][1], scalar=st[:, 7:8], in1=pexp[u % 2][0],
                op0=ALU.mult, op1=ALU.add), t1, t2, evac_tok.get(("tr", u - 2)))
            comb_free[u % 2] = comb_tok[u]

        def turn_p(u):
            h, qb = units[u]
            pe.wait(comb_tok[u], t_in)
            b = bank()
            for kt in range(4):
                o = banks[b][:, kt * P:(kt + 1) * P]
                i = pcomb[u % 2][:, kt * P:(kt + 1) * P]
                if kt < 3:
                    pe.quiet(lambda e, o=o, i=i: e.transpose(o, i, ident))
                else:
                    t = pe.op(lambda e, o=o, i=i: e.transpose(o, i, ident))
            evac_tok[("tr", u)] = t
            t = act.op(lambda e: e.activation(pT[h % 2][:, :, qb * P:qb * P + P],
                                              banks[b][:, :].rearrange("p (k q) -> p k q", k=4), ACT.Copy),
                       t, pT_free[h % 2])
            free[b] = t
            evac_tok[u] = t

        def pv(h):
            pe.wait(evac_tok[2 * h], evac_tok[2 * h + 1])
            b = bank()
            t = chain(banks[b][:, 0:T], [(vv[:, kt, h * P:(h + 1) * P], pT[h % 2][:, kt, :]) for kt in range(4)])
            pT_free[h % 2] = t
            t_o[h] = act.op(lambda e: e.activation(oT[:, h, :], banks[b][:, 0:T], ACT.Copy), t)
            free[b] = t_o[h]

        for u in range(len(units) + 2):
            if u < len(units):
                ends = scores(u)
                combine(u, ends)
            if u >= 1 and u - 1 < len(units):
                turn_p(u - 1)
            if u >= 2 and u % 2 == 1 and (u - 3) // 2 >= 0:
                pv((u - 3) // 2)
            one_behind()

        all_behind()
        t_modr = toks0[-1]
        g1, sh2, sc2, g2 = (modr0[:, i * 8:i * 8 + 8] for i in range(4))
        a2 = vec(8)
        t_a2 = scale_vec(a2, sm("norm2_g0"), sc2, t_modr)

        osq = ar(0, KD, T)
        ors = ar(2048, KD, T)
        oru = ar(4096, KD, T)
        on = Pair(8192, KD, T)
        t = act.op(lambda e: e.activation(osq, oT, ACT.Square), t_o[7])
        for h in range(8):
            tm = mean_sq(osq[:, h, :], ones_h, 1, osq[:, h:h + 1, :], t)
        t = rsqrt(osq, ors, oru, tm)
        t_on = []
        for h in range(0, 8, 2):
            t1 = dve.op(lambda e, h=h: e.scalar_tensor_tensor(out=ors[:, h:h + 2, :], in0=oT[:, h:h + 2, :], scalar=sub_g,
                                                              in1=ors[:, h:h + 2, :], op0=ALU.mult, op1=ALU.mult),
                        t, t_subg)
            q = Pair.__new__(Pair)
            q.hi, q.lo = on.hi[:, h:h + 2, :], on.lo[:, h:h + 2, :]
            t_on += split_into(q, ors[:, h:h + 2, :], t1)
        consume, t_res = add_gated(g1)
        dve.wait(t_modr)
        project("da_wo", None, on, KD, consume, t_on)

        modr1 = vec(48)
        steps, toks1 = ada("ada_w", 1, 0, 6144, [cs3[:, 0:8]],
                           modr1.rearrange("p (b n) -> p b n", n=1), sm("ada_b1"))
        behind += steps
        h = Pair(0, KD, T)
        t_h = norm_mod(xT[:, :, :], a2, sh2, h, t_res[-1], t_a2)
        consume, t_res = add_gated(g2)
        ffn(0, h, t_h, consume)

        all_behind()
        t_mod = toks1[-1]
        sh1, sc1, g1b, sh2b, sc2b, g2b = (modr1[:, i * 8:i * 8 + 8] for i in range(6))
        a1b, a2b = vec(8), vec(8)
        t_a = scale_vec(a1b, sm("norm1_g1"), sc1, t_mod)
        t_a2 = scale_vec(a2b, sm("norm2_g1"), sc2b, t_mod)
        modr2 = vec(48)
        steps, toks2 = ada("w_ada_2", None, 0, 6144, [c2s],
                           modr2.rearrange("p (b n) -> p b n", n=1), sm("b_ada_2"))
        behind += steps
        t_h = norm_mod(xT[:, :, :], a1b, sh1, h, t_res[-1], t_a)
        zp = ar(0, KD, 258)
        cv = ar(2064, KD, T)
        bzf = ar(4112, KD, T)
        bz = Pair(4096, KD, T)
        t_z0 = dve.op(lambda e: e.memset(zp[:, :, 0:1], 0.0), t_res[-1])
        t_z0 = dve.op(lambda e: e.memset(zp[:, :, 257:258], 0.0), t_res[-1])
        t_cv = {}
        scw = sm("sc_conv")
        t_cg = {}

        def take_cgate(n, b, t):
            free[b] = t_cg[n] = act.op(lambda e: e.activation(bzf[:, n, :], banks[b][:, 0:T], ACT.Copy), t, t_res[-1])

        def take_u(n, b, t):
            t = dve.op(lambda e: e.tensor_tensor(zp[:, n, 1:257], banks[b][:, 0:T], bzf[:, n, :], ALU.mult), t, t_cg[n])
            free[b] = t
            t = dve.op(lambda e: e.tensor_scalar(cv[:, n, :], zp[:, n, 0:256], scw[:, n:n + 1], None,
                                                 ALU.mult), t, t_z0)
            for q in range(1, 3):
                t = dve.op(lambda e, q=q: e.scalar_tensor_tensor(
                    out=cv[:, n, :], in0=zp[:, n, q:q + 256], scalar=scw[:, q * 8 + n:q * 8 + n + 1],
                    in1=cv[:, n, :], op0=ALU.mult, op1=ALU.add), t)
            t_cv[n] = t

        t_bz = []

        def take_b(n, b, t):
            t = dve.op(lambda e: e.tensor_tensor(bzf[:, n, :], banks[b][:, 0:T], cv[:, n, :], ALU.mult), t, t_cv[n])
            free[b] = t
            q = Pair.__new__(Pair)
            q.hi, q.lo = bz.hi[:, n:n + 1, :], bz.lo[:, n:n + 1, :]
            t_bz.extend(split_into(q, bzf[:, n:n + 1, :], t))

        project("sc_w_in", None, h, KD, take_cgate, t_h, D)
        project("sc_w_in", None, h, KD, take_u, t_h, 2 * D)
        project("sc_w_in", None, h, KD, take_b, t_h, 0)
        consume, t_res = add_gated(g1b)
        project("sc_w_out", None, bz, KD, consume, t_bz)
        t_h = norm_mod(xT[:, :, :], a2b, sh2b, h, t_res[-1], t_a2)
        consume, t_res = add_gated(g2b)
        ffn(1, h, t_h, consume)

        all_behind()
        t_mod = toks2[-1]
        sh1, sc1, g1c, sh2c, sc2c, g2c = (modr2[:, i * 8:i * 8 + 8] for i in range(6))
        a1c, a2c = vec(8), vec(8)
        t_a = scale_vec(a1c, sm("norm_mix"), sc1, t_mod)
        t_a2 = scale_vec(a2c, sm("norm_ffn"), sc2c, t_mod)
        t = norm_mod(xT[:, :, :], sm("final_g"), None, xT[:, :, :], t_res[-1])
        t_h = norm_mod(xT[:, :, :], a1c, sh1, h, t[-1], t_a)

        DTC, XPC, GTC = 6144, 6176, 7200
        xbc = ar(0, 32, T)
        xdt = ar(8192, 2, 2048)
        lt = ar(12288, 192)

        r, vdt, tok = tile("w_in_2", None, 0, KD, DTC, DTC + 32, "raw")
        pe.wait(tok, t_h[-1])
        b = bank()
        for m in range(2):
            t = chain(banks[b][:, m * 32:m * 32 + 32], [(nsq[:, k, m * P:(m + 1) * P], vdt[:, k, :]) for k in range(KD)])
        raw_free[r] = (t,)
        u_, dt_, a_ = (lt[:, i * 64:i * 64 + 64] for i in range(3))
        e_, w_, q_ = (nr[:, i * 64:i * 64 + 64] for i in range(3))
        b3 = lambda v: v.rearrange("p (c h) -> p c h", c=2)
        bc = lambda v: v.rearrange("p (o h) -> p o h", o=1).to_broadcast([P, 2, 32])
        pb = banks[b][:, 0:64].rearrange("p (c h) -> p c h", c=2)
        t = dve.op(lambda e: e.tensor_tensor(b3(u_), pb, bc(sm("dt_bias")), ALU.add), t)
        free[b] = t
        t = dve.op(lambda e: e.scalar_tensor_tensor(out=e_, in0=u_, scalar=-1.0, in1=u_, op0=ALU.mult, op1=ALU.max), t)
        t = act.op(lambda e: e.activation(e_, e_, ACT.Exp, scale=-1.0), t)
        t = dve.op(lambda e: e.tensor_scalar(w_, e_, 1.0, None, ALU.add), t)
        t = act.op(lambda e: e.activation(q_, w_, ACT.Ln), t)
        t = dve.op(lambda e: e.tensor_scalar(dt_, w_, 1.0, None, ALU.is_equal), t)
        t = dve.op(lambda e: e.tensor_tensor(q_, q_, dt_, ALU.add), t)
        t = dve.op(lambda e: e.scalar_tensor_tensor(out=w_, in0=w_, scalar=-1.0, in1=dt_, op0=ALU.add, op1=ALU.add), t)
        t = dve.op(lambda e: e.reciprocal(w_, w_), t)
        t = dve.op(lambda e: e.tensor_tensor(q_, q_, w_, ALU.mult), t)
        t = dve.op(lambda e: e.tensor_tensor(q_, q_, e_, ALU.mult), t)
        t_dt = dve.op(lambda e: e.scalar_tensor_tensor(out=dt_, in0=u_, scalar=0.0, in1=q_, op0=ALU.max, op1=ALU.add), t)
        A_ = vec(32)
        t = act.op(lambda e: e.activation(A_, sm("a_log"), ACT.Exp))
        t = dve.op(lambda e: e.tensor_scalar(A_, A_, -1.0, None, ALU.mult), t)
        t_av = dve.op(lambda e: e.tensor_tensor(b3(a_), b3(dt_), bc(A_), ALU.mult), t, t_dt)

        praw = [work[:, i * 1024:i * 1024 + 259] for i in range(4)]
        pacc = [work[:, i * 1024 + 260:i * 1024 + 516] for i in range(4)]
        ptmp = [work[:, i * 1024 + 516:i * 1024 + 772] for i in range(4)]
        t_pad = [dve.op(lambda e, i=i: e.memset(praw[i][:, 0:3], 0.0), t_h[-1]) for i in range(4)]
        p_used = [t_pad[3]] * 4
        cw, cb = sm("conv_w"), sm("conv_b")
        t_xbc = {}

        def take_xbc(n, b, t):
            i = n % 4
            raw, acc = praw[i], pacc[i]
            t = act.op(lambda e: e.activation(raw[:, 3:259], banks[b][:, 0:T], ACT.Copy), t, p_used[i])
            free[b] = t
            t = dve.op(lambda e: e.tensor_scalar(acc, raw[:, 0:256], cw[:, n:n + 1], cb[:, n:n + 1],
                                                 ALU.mult, ALU.add), t)
            for q in range(1, 4):
                t = dve.op(lambda e, q=q: e.scalar_tensor_tensor(
                    out=acc, in0=raw[:, q:q + 256], scalar=cw[:, q * 32 + n:q * 32 + n + 1], in1=acc,
                    op0=ALU.mult, op1=ALU.add), t)
            p_used[i] = t_xbc[n] = silu_into(xbc[:, n, :], acc, t)

        project("w_in_2", None, h, KD, take_xbc, t_h, 2048, 4096)

        cs_ = u_
        b = bank()
        pe.wait(t_av)
        for c in range(2):
            t = mm_end(banks[b][:, c * 32:c * 32 + 32], triu, a_[:, c * 32:c * 32 + 32], True, True)
        t_cs = act.op(lambda e, b=b: e.activation(cs_, banks[b][:, 0:64], ACT.Copy), t)
        free[b] = t_cs

        nsf = nsq[:, :, :].rearrange("p k t -> p (k t)")
        Bt = nsf[:, 0:1024].rearrange("p (g n) -> p g n", g=8)
        t_xdt = {}
        for c in range(2):
            for q in range(4):
                b = bank()
                for j in range(4):
                    n = 4 * q + j
                    pe.wait(t_xbc[n])
                    o, i = banks[b][:, j * P:(j + 1) * P], xbc[:, n, c * P:(c + 1) * P]
                    t = pe.op(lambda e, o=o, i=i: e.transpose(o, i, ident))
                src = banks[b][:, :].rearrange("p (h d) -> p h d", d=64)
                dst = xdt[:, c, q * 512:(q + 1) * 512].rearrange("p (h d) -> p h d", d=64)
                dtb = dt_[:, c * 32 + q * 8:c * 32 + q * 8 + 8].rearrange("p (h o) -> p h o", o=1).to_broadcast([P, 8, 64])
                t_xdt[c, q] = dve.op(lambda e, src=src, dst=dst, dtb=dtb: e.tensor_tensor(dst, src, dtb, ALU.mult),
                                     t, t_dt)
                free[b] = t_xdt[c, q]
        for q in range(2):
            b = bank()
            for j in range(4):
                g = 4 * q + j
                pe.wait(t_xbc[16 + g])
                o, i = banks[b][:, j * P:(j + 1) * P], xbc[:, 16 + g, 0:P]
                t = pe.op(lambda e, o=o, i=i: e.transpose(o, i, ident))
            t_Bt = act.op(lambda e, b=b, q=q: e.activation(
                Bt[:, 4 * q:4 * q + 4, :], banks[b][:, :].rearrange("p (g n) -> p g n", g=4), ACT.Copy), t)
            free[b] = t_Bt

        Rs = [work[:, i * 2048:i * 2048 + 512].rearrange("p (r l) -> p r l", r=4) for i in range(2)]
        Ex = [work[:, i * 2048 + 512:i * 2048 + 1024].rearrange("p (r l) -> p r l", r=4) for i in range(2)]
        Ce = [work[:, i * 2048 + 1024:i * 2048 + 1536].rearrange("p (r l) -> p r l", r=4) for i in range(2)]
        CBm = [work[:, i * 2048 + 1536:i * 2048 + 1664] for i in range(2)]
        xdec = [work[:, i * 2048 + 1664:i * 2048 + 1920] for i in range(2)]
        dec = vec(8)
        Sg = [nsf[:, 1024 + i * 256:1280 + i * 256] for i in range(2)]
        buf_free = [list(p_used), list(p_used)]
        sg_free = [None, None]
        y_tok = {}
        dsk = sm("dskip")

        def decays(u):
            g, c = divmod(u, 2)
            i = u % 2
            b = bank()
            for r in range(4):
                h = c * 32 + 4 * g + r
                t = mm_end(banks[b][:, r * P:(r + 1) * P], a_[:, h:h + 1].to_broadcast([P, P]), triu, True, True)
            tR = act.op(lambda e: e.activation(Rs[i], banks[b][:, :].rearrange("p (r l) -> p r l", r=4), ACT.Copy),
                        t, *buf_free[i])
            free[b] = tR
            pe.wait(t_xbc[16 + g], t_xbc[24 + g])
            b2 = bank()
            t = mm_end(banks[b2][:, 0:P], xbc[:, 16 + g, c * P:(c + 1) * P], xbc[:, 24 + g, c * P:(c + 1) * P], True, True)
            tCB = dve.op(lambda e: e.tensor_tensor(CBm[i], banks[b2][:, 0:P], triu, ALU.mult), t, *buf_free[i])
            free[b2] = tCB
            if c == 0:
                h0 = 4 * g
                d4 = dec[:, 4 * (g % 2):4 * (g % 2) + 4]
                t = dve.op(lambda e: e.tensor_tensor(d4, Rs[i][:, :, 127], cs_[:, h0:h0 + 4], ALU.subtract), tR, t_cs)
                t = act.op(lambda e: e.activation(d4, d4, ACT.Exp), t)
                xv = xdt[:, 0, h0 * 64:h0 * 64 + 256].rearrange("p (r d) -> p r d", r=4)
                db = d4.rearrange("p (r o) -> p r o", o=1).to_broadcast([P, 4, 64])
                xd = xdec[i].rearrange("p (r d) -> p r d", r=4)
                tX = dve.op(lambda e: e.tensor_tensor(xd, xv, db, ALU.mult), t, t_xdt[0, g // 2])
                tC = None
            else:
                t = act.op(lambda e: e.activation(Ce[i], Rs[i], ACT.Exp), tR)
                cb_ = xbc[:, 24 + g, P:2 * P].rearrange("p (o l) -> p o l", o=1).to_broadcast([P, 4, P])
                tC = dve.op(lambda e: e.tensor_tensor(Ce[i], Ce[i], cb_, ALU.mult), t)
                tX = None
            for r in range(4):
                h = c * 32 + 4 * g + r
                t = dve.op(lambda e, r=r, h=h: e.tensor_scalar(Ex[i][:, r, :], Rs[i][:, r, :], cs_[:, h:h + 1], 0.0,
                                                               ALU.subtract, ALU.min), tR, t_cs)
            t = act.op(lambda e: e.activation(Ex[i], Ex[i], ACT.Exp), t)
            mb = CBm[i].rearrange("p (o l) -> p o l", o=1).to_broadcast([P, 4, P])
            tE = dve.op(lambda e: e.tensor_tensor(Ex[i], Ex[i], mb, ALU.mult), t, tCB)
            return tE, tX, tC

        y_bank = {}

        def outputs(u, toks):
            g, c = divmod(u, 2)
            i = u % 2
            tE, tX, tC = toks
            if c == 0:
                y_bank[g] = (bank(), bank())
                bs = bank()
                pe.wait(tX, t_Bt)
                t = mm_end(banks[bs][:, 0:256], Bt[:, g, :], xdec[i], True, True)
                t_S = act.op(lambda e: e.activation(Sg[g % 2], banks[bs][:, 0:256], ACT.Copy), t, sg_free[g % 2])
                free[bs] = t_S
                y_tok["S", g] = t_S
            pe.wait(tE, t_xdt[c, g // 2], tC, y_tok["S", g] if c else None)
            for r in range(4):
                bk = banks[y_bank[g][r // 2]]
                o = bk[64 * (r % 2):64 * (r % 2) + 64, c * P:(c + 1) * P]
                h = 4 * g + r
                t = mm_end(o, xdt[:, c, h * 64:h * 64 + 64], Ex[i][:, r, :], True, c == 0)
                if c:
                    t = mm_end(o, Sg[g % 2][:, r * 64:r * 64 + 64], Ce[i][:, r, :], False, True)
            buf_free[i] = [t]
            if c:
                sg_free[g % 2] = t
                for j in range(2):
                    n = 2 * g + j
                    bb = y_bank[g][j]
                    free[bb] = y_tok[n] = dve.op(lambda e, n=n, bb=bb: e.scalar_tensor_tensor(
                        out=xbc[:, n, :], in0=xbc[:, n, :], scalar=dsk[:, n:n + 1], in1=banks[bb][:, 0:T],
                        op0=ALU.mult, op1=ALU.add), t)

        prev = None
        for u in range(17):
            cur = decays(u) if u < 16 else None
            if prev is not None:
                outputs(u - 1, prev)
            prev = cur

        t_scan = y_tok[15]
        yf = xbc[:, 0:16, :]
        zt = [work[:, i * 256:i * 256 + 256] for i in range(2)]
        zt_used = [t_scan, t_scan]

        def take_z(n, b, t):
            i = n % 2
            free[b] = t = act.op(lambda e: e.activation(zt[i], banks[b][:, 0:T], ACT.Silu), t, zt_used[i])
            zt_used[i] = y_tok[n] = dve.op(lambda e: e.tensor_tensor(yf[:, n, :], yf[:, n, :], zt[i], ALU.mult), t)

        project("w_in_2", None, h, KD, take_z, t_h, 0, 2048)
        ysq = ar(4096, 16, T)
        gv_ = nsq[:, :, :]
        gy_ = ar(8192, 8, T)
        gu_ = ar(10240, 8, T)
        gg = sm("ssd_g")
        yT = Pair(4096, 16, T)

        def group_norm():
            for g in range(8):
                t = act.op(lambda e, g=g: e.activation(ysq[:, 2 * g:2 * g + 2, :], yf[:, 2 * g:2 * g + 2, :], ACT.Square),
                           y_tok[2 * g + 1])
                tm = mean_sq(gv_[:, g, :], ones_g, 2, ysq[:, 2 * g:2 * g + 2, :], t)
            t = rsqrt(gv_, gy_, gu_, tm)
            toks = []
            for n in range(0, 16, 2):
                for j in (n, n + 1):
                    t2 = dve.op(lambda e, j=j: e.scalar_tensor_tensor(out=yf[:, j, :], in0=yf[:, j, :],
                                                                      scalar=gg[:, j:j + 1], in1=gy_[:, j // 2, :],
                                                                      op0=ALU.mult, op1=ALU.mult), t)
                q = Pair.__new__(Pair)
                q.hi, q.lo = yT.hi[:, n:n + 2, :], yT.lo[:, n:n + 2, :]
                toks += split_into(q, yf[:, n:n + 2, :], t2)
            return toks

        t_y = group_norm()

        pp = [work[:, 512 + i * 1024:512 + i * 1024 + 272] for i in range(2)]
        pq = [[work[:, 512 + i * 1024 + 272:512 + i * 1024 + 544], work[:, 512 + i * 1024 + 544:512 + i * 1024 + 816]]
              for i in range(2)]
        pooled = ar(4096, KD, T)
        mixf = ar(6144, KD, T)
        mixp = Pair(0, KD, T)
        pz = [pool.op(lambda e, i=i: e.memset(pp[i][:, 0:16], 0.0), t_scan) for i in range(2)]
        pp_used = [pz[1], pz[1]]
        t_pool = {}

        def take_xp(n, b, t):
            i = n % 2
            t = act.op(lambda e: e.activation(pp[i][:, 16:272], banks[b][:, 0:T], ACT.Copy), t, pp_used[i])
            free[b] = t
            src, w, q = pp[i], 1, 0
            for step in range(n // 2 + 1):
                dst = pq[i][q]
                t = pool.op(lambda e, src=src, dst=dst, w=w: e.tensor_tensor(
                    dst[:, 2 * w:272], src[:, 2 * w:272], src[:, w:272 - w], ALU.add), t)
                src, w, q = dst, 2 * w, 1 - q
            g = n // 2
            iw = cn("invw", g * 16, g * 16 + 16)
            dst = pq[i][q]
            t0 = pool.op(lambda e: e.tensor_tensor(dst[:, 16:32], src[:, 16:32], iw, ALU.mult), t)
            t = pool.op(lambda e: e.tensor_scalar(dst[:, 32:272], src[:, 32:272], 0.5 ** (g + 1), None, ALU.mult), t)
            t = pool.op(lambda e: e.tensor_tensor(pooled[:, n, :], dst[:, 16:272], pp[i][:, 16:272], ALU.subtract),
                        t0, t, t_y[-1])
            pp_used[i] = t_pool[n] = t

        project("w_in_2", None, h, KD, take_xp, t_h, XPC, 1024)

        gts = ar(8192, 16, T)
        t_gt = {}

        def take_gt(n, b, t):
            v = gts[:, n, :]
            free[b] = t_gt[n] = act.op(lambda e: e.activation(v, banks[b][:, 0:T], ACT.Sigmoid), t, t_y[-1])

        project("w_in_2", None, h, KD, take_gt, t_h, GTC, 2048)

 
        r, vp, tok = tile("pool_w_2", None, 0, 8, 0, 256, "raw")
        pe.wait(tok)
        psc = sm("pool_scale")
        t_mx = []
        for n in range(8):
            g, j = divmod(n, 2)
            pe.wait(t_pool[2 * g], t_pool[2 * g + 1])
            b = bank()
            t = chain(banks[b][:, 0:T], [(vp[:, 2 * g + k, j * P:(j + 1) * P], pooled[:, 2 * g + k, :]) for k in range(2)])
            t1 = dve.op(lambda e, n=n, b=b: e.tensor_scalar(mixf[:, n, :], banks[b][:, 0:T], psc[:, n:n + 1], None,
                                                            ALU.mult), t)
            free[b] = t1
            q = Pair.__new__(Pair)
            q.hi, q.lo = mixp.hi[:, n:n + 1, :], mixp.lo[:, n:n + 1, :]
            t_mx += split_into(q, mixf[:, n:n + 1, :], t1)
        raw_free[r] = (t,)

        t_m1 = {}

        def take_ssd(n, b, t):
            free[b] = t_m1[n] = dve.op(lambda e: e.tensor_tensor(gts[:, n, :], banks[b][:, 0:T], gts[:, n, :], ALU.mult),
                                       t, t_gt[n])

        project("w_br_ssd_2", None, yT, 16, take_ssd, t_y)
        t_m2 = []
        mix = Pair(4096, KD, T)

        def take_pool(n, b, t):
            t = dve.op(lambda e: e.tensor_tensor(gts[:, 8 + n, :], banks[b][:, 0:T], gts[:, 8 + n, :], ALU.mult),
                       t, t_gt[8 + n])
            free[b] = t
            t = dve.op(lambda e: e.tensor_tensor(gts[:, n, :], gts[:, n, :], gts[:, 8 + n, :], ALU.add), t, t_m1[n])
            q = Pair.__new__(Pair)
            q.hi, q.lo = mix.hi[:, n:n + 1, :], mix.lo[:, n:n + 1, :]
            t_m2.extend(split_into(q, gts[:, n:n + 1, :], t))

        project("w_br_pool_2", None, mixp, KD, take_pool, t_mx)
        consume, t_res = add_gated(g1c)
        project("w_out_2", None, mix, KD, consume, t_m2)

        t_u = norm_mod(xT[:, :, :], a2c, sh2c, h, t_res[-1], t_a2)
        r, vr, tok = tile("w_router_2", None, 0, KD, 0, 64, "raw")
        pe.wait(tok, t_u[-1])
        wT = ar(1024, T)[0:64, :]
        b = bank()
        for m in range(2):
            t = chain(banks[b][:, m * 64:m * 64 + 64], [(nsq[:, k, m * P:(m + 1) * P], vr[:, k, :]) for k in range(KD)])
        raw_free[r] = (t,)
        lg = banks[b][:, 0:128]
        scs = ar(0, 128)
        cho = ar(128, 128)
        msk = ar(256, 128)
        m8 = ar(384, 2, 64)
        gsc = ar(512, 16)
        gv = ar(528, 16)
        rpl = ar(544, 128)
        gmk = ar(672, 16)
        top = ar(688, 16)
        den = ar(704, 2)
        wts = ar(706, 128)
        three = lambda v, a: v.rearrange("p (a b) -> p a b", a=a)
        t = act.op(lambda e: e.activation(scs, lg, ACT.Exp, scale=-1.0), t)
        free[b] = t
        t = dve.op(lambda e: e.tensor_scalar(scs, scs, 1.0, None, ALU.add), t)
        t = dve.op(lambda e: e.reciprocal(scs, scs), t)
        rb = sm("router_bias").rearrange("p (o n) -> p o n", o=1).to_broadcast([P, 2, 64])
        t = dve.op(lambda e: e.tensor_tensor(three(cho, 2), three(scs, 2), rb, ALU.add), t)
        bw = bank()

        def route(m, t):
            cm = cho[:, m * 64:m * 64 + 64]
            sm_ = scs[:, m * 64:m * 64 + 64]
            mk = msk[:, m * 64:m * 64 + 64]
            wm = wts[:, m * 64:m * 64 + 64]
            for g in range(8):
                tg = dve.op(lambda e, g=g: e.max(m8[:, m, g * 8:g * 8 + 8], cm[:, g * 8:g * 8 + 8]), t)
            m3 = three(m8[:, m, :], 8)
            gs, gvm, gmm, tp = (v[:, m * 8:m * 8 + 8] for v in (gsc, gv, gmk, top))
            t2 = dve.op(lambda e: e.tensor_tensor(gs, m3[:, :, 0], m3[:, :, 1], ALU.add), tg)
            t2 = dve.op(lambda e: e.max(gvm, gs), t2)
            t2 = dve.op(lambda e: e.memset(gvm[:, 4:8], BIG), t2)
            t2 = dve.op(lambda e: e.match_replace(gmm, gvm, gs, -BIG), t2)
            t2 = dve.op(lambda e: e.tensor_tensor(gmm, gmm, gs, ALU.not_equal), t2)
            gb = gmm.rearrange("p (g o) -> p g o", o=1).to_broadcast([P, 8, 8])
            t3 = dve.op(lambda e: e.tensor_scalar(gs, gmm, 1.0, BIG, ALU.subtract, ALU.mult), t2)
            t2 = dve.op(lambda e: e.tensor_tensor(three(mk, 8), three(cm, 8), gb, ALU.mult), t2)
            gsb = gs.rearrange("p (g o) -> p g o", o=1).to_broadcast([P, 8, 8])
            t2 = dve.op(lambda e: e.tensor_tensor(three(mk, 8), three(mk, 8), gsb, ALU.add), t2, t3)
            t2 = dve.op(lambda e: e.max(tp, mk), t2)
            rp = rpl[:, m * 64:m * 64 + 64]
            t2 = dve.op(lambda e: e.match_replace(rp, tp, mk, -3e30), t2)
            t2 = dve.op(lambda e: e.tensor_tensor(rp, rp, mk, ALU.not_equal), t2)
            t2 = dve.op(lambda e: e.tensor_tensor(wm, rp, sm_, ALU.mult), t2)
            dm = den[:, m:m + 1]
            t2 = dve.op(lambda e: e.tensor_reduce(dm, wm, AX, ALU.add), t2)
            t2 = dve.op(lambda e: e.reciprocal(dm, dm), t2)
            t2 = dve.op(lambda e: e.tensor_scalar(wm, wm, dm, 2.5, ALU.mult, ALU.mult), t2)
            pe.wait(t2)
            return pe.op(lambda e: e.transpose(banks[bw][0:64, m * P:(m + 1) * P], wm, ident))

        t_wt = [route(m, t) for m in range(2)]
        t_wT = act.op(lambda e: e.activation(wT, banks[bw][0:64, 0:T], ACT.Copy), t_wt[1])
        free[bw] = t_wT

        for b in range(4, 8):
            pe.wait(free[b])
        active[0] = [0, 1, 2, 3]
        hidE = [Pair(4096 + i * 1024, 2, T) for i in range(2)]
        wrow = [ar(1280 + i * 256, T) for i in range(2)]
        hid_used = [t_res[-1], t_res[-1]]
        wrow_used = [None, None]
        acc = [banks[4 + n // 2][:, (n % 2) * T:(n % 2) * T + T] for n in range(8)]

        def expert_in(i):
            q = i % 2
            extra = None
            names = ("ws_gate_2", "ws_up_2") if i == 0 else ("we_gate_2", "we_up_2")
            lead = None if i == 0 else i - 1
            if i:
                bw = bank()
                pe.wait(t_wT)
                t = mm_end(banks[bw][:, 0:T], ident[0:64, lead:lead + 1].to_broadcast([64, P]), wT, True, True)
                t = act.op(lambda e: e.activation(wrow[q], banks[bw][:, 0:T], ACT.Copy), t, wrow_used[q])
                free[bw] = t
                extra = (wrow[q].rearrange("p (o t) -> p o t", o=1).to_broadcast([P, 2, T]), t)
            fin = None
            for name in names:
                sq, hi, lo, tw = tile(name, lead, 0, KD, 0, 256)
                b = bank()
                for j in range(2):
                    pairs = []
                    for k in range(KD):
                        cs = slice(j * P, (j + 1) * P)
                        pairs += products((hi[:, k, cs], lo[:, k, cs]), h.at(k), tw[k], t_u[k])
                    t = chain(banks[b][:, j * T:(j + 1) * T], pairs)
                split_free[sq] = t
                ps = three(banks[b][:, :], 2)
                if fin is None:
                    act.wait(hid_used[q])
                    dve.wait(hid_used[q])
                    free[b], fin = gated(hidE[q], 0, ps, None, t, None, extra)
                else:
                    free[b], toks = fin(ps, t)
            wrow_used[q] = toks[-1]
            return toks

        def expert_out(i, t_hid, first, last):
            q = i % 2
            sq, hi, lo, tw = tile("ws_down_2" if i == 0 else "we_down_2", None if i == 0 else i - 1, 0, 2, 0, 1024)
            todo = []
            for n in range(8):
                for k in range(2):
                    cs = slice(n * P, (n + 1) * P)
                    for m, (l, x, *w) in enumerate(products((hi[:, k, cs], lo[:, k, cs]), hidE[q].at(k), tw[k], t_hid[k])):
                        todo.append((acc[n], l, x, first and k == 0 and m == 0 and n % 2 == 0,
                                     last and k == 1 and m == 2, w))
            for o, l, x, st, en, w in todo:
                pe.wait(*w)
                fn = lambda e, o=o, l=l, x=x, st=st, en=en: e.matmul(o, l, x, start=st, stop=en, skip_group_check=True)
                if o is todo[-1][0] and (o, l, x, st, en, w) == todo[-1]:
                    t = pe.op(fn)
                else:
                    pe.quiet(fn)
            split_free[sq] = t
            hid_used[q] = t
            return t

        prev = None
        for i in range(NE + 2):
            cur = expert_in(i) if i <= NE else None
            if prev is not None:
                t_acc = expert_out(i - 1, prev, i == 1, i == NE + 1)
            prev = cur

        for n in range(8):
            t = dve.op(lambda e, n=n: e.scalar_tensor_tensor(out=xT[:, n, :], in0=acc[n], scalar=g2c[:, n:n + 1],
                                                             in1=xT[:, n, :], op0=ALU.mult, op1=ALU.add), t_acc)
        t = norm_mod(xT[:, :, :], sm("final_g2"), None, None, t)[-1]
        s_out = sem("s_out")
        sp.quiet(lambda e: e.dma_start(out.rearrange("(k p) t -> p k t", p=P), nsq[:, :, :]).then_inc(s_out, 16), t)
        sp.wait((s_out, 16))
        if plan is None:
            return order

        block = ctx.enter_context(nc.Block())
        block.sync(sp.run)
        block.scalar(act.run)
        block.vector(dve.run)
        block.gpsimd(pool.run)
        block.tensor(pe.run)


def _cols(v):
    return np.ascontiguousarray(v.reshape(-1, P).T)


def _constants():
    f = np.float32
    tok = np.arange(T)
    inv = (1.0 / (f(10000.0) ** (np.arange(0, 32, 2, dtype=f) / f(32)))).astype(f)
    ang = np.concatenate([(tok // 64).astype(f)[:, None] * inv, (tok % 64).astype(f)[:, None] * inv], axis=-1)
    d = np.arange(P) % 64
    idx = (d // 32) * 16 + d % 16
    sign = np.where(d % 32 < 16, -1.0, 1.0).astype(f)
    cos = np.cos(ang).astype(f)[:, idx].T
    sin = np.sin(ang).astype(f)[:, idx].T * sign[:, None]
    invw = np.stack([1.0 / np.minimum(tok + 1, w) for w in (2, 4, 8, 16)]).astype(f)[:, 0:16].reshape(1, -1)
    return np.concatenate([np.eye(P, dtype=f), np.triu(np.ones((P, P), f)), cos, sin,
                           np.broadcast_to(invw, (P, 64))], axis=1).astype(f)


def kernel(**inputs):
    import concourse.bacc as bacc
    from concourse.bass_utils import run_bass_kernel_spmd

    a = {k: np.asarray(v) for k, v in inputs.items()}
    row = lambda v: np.broadcast_to(v.reshape(1, -1), (P, v.size))
    small = np.concatenate([
        _cols(a["c"]), _cols(a["c_ctx"]), _cols(a["c_2"]), _cols(a["ada_b"][0]), _cols(a["ada_b"][1]),
        _cols(a["b_ada_2"]), _cols(a["norm1_g"][0]), _cols(a["norm1_g"][1]), _cols(a["norm2_g"][0]),
        _cols(a["norm2_g"][1]), _cols(a["final_g"]), _cols(a["da_subln_g"]), _cols(a["sc_conv_w"]),
        _cols(a["norm_mix_g_2"]), _cols(a["conv_w_2"]), _cols(a["conv_b_2"]),
        _cols(np.repeat(a["D_skip_2"][0], 64)), _cols(a["ssd_norm_g_2"]), _cols(a["pool_scale_2"]),
        _cols(a["norm_ffn_g_2"]), _cols(a["final_norm_g_2"]), row(a["dt_bias_2"]), row(a["A_log_2"]),
        row(a["router_bias_2"]), row(a["da_lambda"]),
    ], axis=1)
    arrays = {
        "small": np.ascontiguousarray(small), "const": _constants(),
        "xT": np.ascontiguousarray(a["x"][0].T), "ctxT": np.ascontiguousarray(a["ctx"][0].T),
    }
    for name in ("ada_w", "ffn_w_in", "ffn_w_out"):
        arrays[name] = np.ascontiguousarray(a[name])
    for name in ("da_wqkv", "da_wo", "sc_w_in", "sc_w_out", "w_ada_2", "w_in_2", "pool_w_2", "w_br_ssd_2",
                 "w_br_pool_2", "w_out_2", "w_router_2", "we_gate_2", "we_up_2", "we_down_2",
                 "ws_gate_2", "ws_up_2", "ws_down_2"):
        arrays[name] = np.ascontiguousarray(a[name][0])
    plan = None
    for _ in range(2):
        nc = bacc.Bacc("TRN2", target_bir_lowering=False, num_devices=1)
        I = {k: nc.dram_tensor(f"in_{k}", v.shape, F32, kind="ExternalInput").ap() for k, v in arrays.items()}
        out = nc.dram_tensor("out_0", (D, T), F32, kind="ExternalOutput").ap()
        plan = program(nc, I, out, plan)
    r = run_bass_kernel_spmd(nc, [{f"in_{k}": v for k, v in arrays.items()}], core_ids=[0])
    return np.ascontiguousarray(r.results[0]["out_0"].T)[None]
```

```python
import math
from contextlib import ExitStack

import numpy as np
import concourse.bass as bass
import concourse.mybir as mybir

F32 = mybir.dt.float32
F32R = mybir.dt.float32r
ALU = mybir.AluOpType
ACT = mybir.ActivationFunctionType
AX = mybir.AxisListType.X

P = 128
T = 256
D = 1024
KD = D // P
TILE = 1024
FF = 2816
KF = FF // P
NE = 64
EPS = 1e-6
BIG = 1e30

SMALLS = {}
CONSTS = {}


def _layout(table, parts):
    at = 0
    for name, n in parts:
        table[name] = (at, n)
        at += n
    return at


N_SMALL = _layout(SMALLS, [
    ("c", 8), ("c_ctx", 8), ("c_2", 8), ("ada_b0", 48), ("ada_b1", 48), ("b_ada_2", 48),
    ("norm1_g0", 8), ("norm1_g1", 8), ("norm2_g0", 8), ("norm2_g1", 8), ("final_g", 8),
    ("subln", 1), ("sc_conv", 24), ("norm_mix", 8), ("conv_w", 128), ("conv_b", 32),
    ("dskip", 16), ("ssd_g", 16), ("pool_scale", 8), ("norm_ffn", 8), ("final_g2", 8),
    ("dt_bias", 32), ("a_log", 32), ("router_bias", 64), ("lam", 256),
])
N_CONST = _layout(CONSTS, [("ident", P), ("triu", P), ("cos", T), ("sin", T), ("invw", 64)])


class Engine:

    def __init__(self, sem):
        self.sem = sem
        self.count = 0
        self.todo = []
        self.seen = {}

    def wait(self, *tokens):
        for tok in tokens:
            if tok is None:
                continue
            sem, value = tok
            if self.seen.get(sem.name, 0) < value:
                self.seen[sem.name] = value
                self.todo.append(lambda e, s=sem, v=value: e.wait_ge(s, v))

    def op(self, fn, *waits):
        self.wait(*waits)
        self.count += 1
        self.todo.append(lambda e: fn(e).then_inc(self.sem, 1))
        return (self.sem, self.count)

    def quiet(self, fn, *waits):
        self.wait(*waits)
        self.todo.append(fn)

    def run(self, e):
        for fn in self.todo:
            fn(e)


def program(nc, I, out, plan):
    ctx = ExitStack()
    with ctx:
        def sb(name, shape, dt=F32):
            return ctx.enter_context(nc.sbuf_tensor(name, shape, dt))

        def sem(name):
            return ctx.enter_context(nc.semaphore(name))

        banks = [ctx.enter_context(nc.psum_tensor(f"bank{i}", [P, 512], F32)) for i in range(8)]
        pe, act, dve, pool, sp = (Engine(sem(f"s_{n}")) for n in ("pe", "act", "dve", "pool", "sp"))

        NRAW = 4
        NASIS = 2
        FETCH = 6
        NSPLIT = 4
        AHEAD = 2
        raw = [sb(f"raw{i}", [P, TILE]) for i in range(NRAW + NASIS)]
        whi = [sb(f"whi{i}", [P, TILE], F32R) for i in range(NSPLIT)]
        wlo = [sb(f"wlo{i}", [P, TILE], F32R) for i in range(NSPLIT)]
        RR = sb("RR", [P, 15360], F32R)
        small = sb("small", [P, N_SMALL])
        const = sb("const", [P, N_CONST])
        ones_d = sb("ones_d", [P, P])
        ones_h = sb("ones_h", [P, P])
        ones_1 = sb("ones_1", [P, 1])
        ones_g = sb("ones_g", [P, P])
        xT = sb("xT", [P, KD, T])
        nsq = sb("nsq", [P, KD, T])
        nr = sb("nr", [P, T])
        vecs = sb("vecs", [P, 392])
        arena = sb("arena", [P, 12480])
        work = sb("work", [P, 4096])

        def sm(name, a=0, b=None):
            o, n = SMALLS[name]
            return small[:, o + a:o + (n if b is None else b)]

        def cn(name, a=0, b=None):
            o, n = CONSTS[name]
            return const[:, o + a:o + (n if b is None else b)]

        ident, triu = cn("ident"), cn("triu")

        def ar(at, *shape):
            n = int(np.prod(shape))
            v = arena[:, at:at + n]
            if len(shape) == 2:
                v = v.rearrange("p (a b) -> p a b", a=shape[0])
            elif len(shape) == 3:
                v = v.rearrange("p (a b c) -> p a b c", a=shape[0], b=shape[1])
            return v

        class Pair:

            def __init__(self, at, nk, w):
                n = nk * w
                self.hi = RR[:, at:at + n].rearrange("p (k w) -> p k w", k=nk)
                self.lo = RR[:, at + n:at + 2 * n].rearrange("p (k w) -> p k w", k=nk)

            def part(self, a, b):
                q = Pair.__new__(Pair)
                q.hi, q.lo = self.hi[:, :, a:b], self.lo[:, :, a:b]
                return q

            def at(self, k):
                return self.hi[:, k, :], self.lo[:, k, :]

        free = [None] * 8
        turn = [0]
        active = [list(range(8))]

        def bank():
            b = active[0][turn[0] % len(active[0])]
            turn[0] += 1
            pe.wait(free[b])
            free[b] = None
            return b

        raw_sem = [sem(f"s_raw{i}") for i in range(NRAW + NASIS)]
        raw_count = [0] * (NRAW + NASIS)
        raw_free = [()] * (NRAW + NASIS)
        n_raw = {"split": 0, "raw": 0}

        split_free = [None] * NSPLIT
        fetched = {}
        n_split = [0]
        n_taken = [0]
        order = []
        ready = {}

        def source(spec):
            name, lead, k0, k1, c0, c1 = spec[:6]
            w = I[name] if lead is None else I[name][lead]
            if name == "pool_w_2":
                return w.rearrange("g (k p) n -> p (g k) n", p=P)[:, k0:k1, c0:c1]
            return w[k0 * P:k1 * P, c0:c1].rearrange("(k p) n -> p k n", p=P)

        def fetch(n):
            k0, k1, c0, c1 = plan[n][2:6]
            kind = plan[n][6]
            i = n_raw[kind] % NRAW if kind == "split" else NRAW + n_raw[kind] % NASIS
            if raw_free[i] is None:
                return False
            n_raw[kind] += 1
            v = raw[i][:, 0:(k1 - k0) * (c1 - c0)].rearrange("p (k n) -> p k n", k=k1 - k0)
            src = source(plan[n])
            sp.wait(*raw_free[i])
            sp.quiet(lambda e: e.dma_start(v, src).then_inc(raw_sem[i], 16))
            raw_free[i] = None
            raw_count[i] += 16
            fetched[n] = (i, v, (raw_sem[i], raw_count[i]))
            return True

        def prepare(n):
            i, v, tok = fetched[n]
            k, w = v.shape[1], v.shape[2]
            q = n_split[0] % NSPLIT
            n_split[0] += 1
            hi = whi[q][:, 0:k * w].rearrange("p (k n) -> p k n", k=k)
            lo = wlo[q][:, 0:k * w].rearrange("p (k n) -> p k n", k=k)
            t = act.op(lambda e: e.activation(hi, v, ACT.Copy), tok, split_free[q])
            t2 = dve.op(lambda e: e.tensor_tensor(lo, v, hi.bitcast(F32), ALU.subtract), t, tok, split_free[q])
            raw_free[i] = (t, t2)
            ready[n] = (q, hi, lo, t2)

        def tile(name, lead, k0, k1, c0, c1, kind="split"):
            spec = (name, lead, k0, k1, c0, c1, kind)
            n = n_taken[0]
            n_taken[0] += 1
            order.append(spec)
            if plan is None:
                v = raw[0][:, 0:(k1 - k0) * (c1 - c0)].rearrange("p (k n) -> p k n", k=k1 - k0)
                return (0, v, None) if kind == "raw" else (0, v, v, None)
            assert plan[n] == spec
            splits, full = 0, []
            for m in range(n, min(n + FETCH, len(plan))):
                if m not in fetched and (plan[m][6] in full or (plan[m][6] == "raw" and m > n + 2) or not fetch(m)):
                    assert m > n
                    full.append(plan[m][6])
                    continue
                if plan[m][6] == "split" and splits <= AHEAD:
                    splits += 1
                    if m not in ready:
                        prepare(m)
            return fetched[n] if kind == "raw" else ready[n]

        def mm(o, lhsT, rhs, start, stop, **kw):
            pe.quiet(lambda e: e.matmul(o, lhsT, rhs, start=start, stop=stop, **kw))

        def mm_end(o, lhsT, rhs, start, stop, **kw):
            return pe.op(lambda e: e.matmul(o, lhsT, rhs, start=start, stop=stop, **kw))

        def chain(o, pairs, first=True, last=True):
            tok = None
            for i, (l, r, *w) in enumerate(pairs):
                pe.wait(*w)
                tok = (mm_end if i == len(pairs) - 1 else mm)(
                    o, l, r, first and i == 0, last and i == len(pairs) - 1)
            return tok

        def products(w, x, *tok):
            (wh, wl), (xh, xl) = w, x
            return [(wh, xh, *tok), (wh, xl), (wl, xh)]

        def split_into(pair, src, *waits):
            toks = []
            nk = src.shape[1]
            step = max(1, 512 // src.shape[2])
            for k in range(0, nk, step):
                e_ = min(k + step, nk)
                t = act.op(lambda e, k=k, e_=e_: e.activation(pair.hi[:, k:e_, :], src[:, k:e_, :], ACT.Copy), *waits)
                t = dve.op(lambda e, k=k, e_=e_: e.tensor_tensor(pair.lo[:, k:e_, :], src[:, k:e_, :],
                                                                 pair.hi[:, k:e_, :].bitcast(F32), ALU.subtract), t, *waits)
                toks += [t] * (e_ - k)
            return toks

        s_in = sem("s_in")
        s_x = sem("s_x")
        s_cx = sem("s_cx")
        ctxT = ar(6144, KD, T)
        act.quiet(lambda e: e.dma_start(small[:, :], I["small"]).then_inc(s_in, 16))
        act.quiet(lambda e: e.dma_start(const[:, :], I["const"]).then_inc(s_in, 16))
        act.quiet(lambda e: e.dma_start(xT[:, :, :], I["xT"].rearrange("(k p) t -> p k t", p=P)).then_inc(s_x, 16))
        act.quiet(lambda e: e.dma_start(ctxT, I["ctxT"].rearrange("(k p) t -> p k t", p=P)).then_inc(s_cx, 16))
        t_in, t_x, t_cx = (s_in, 32), (s_x, 16), (s_cx, 16)
        t_ones = [pool.op(lambda e, m=m, v=v: e.memset(m[:, :], v))
                  for m, v in ((ones_1, 1.0), (ones_d, 1.0 / D), (ones_g, 1.0 / 256), (ones_h, 1.0 / P))]

        vec_at = [0]

        def vec(n):
            v = vecs[:, vec_at[0]:vec_at[0] + n]
            vec_at[0] += n
            assert vec_at[0] <= 392
            return v

        def silu_into(dst, src, *waits):
            return act.op(lambda e: e.activation(dst, src, ACT.Silu), *waits)

        cs3 = vec(24)
        t_c = silu_into(cs3, small[:, 0:24], t_in)
        c2s = cs3[:, 16:24]

        ada_acc = [ar(11520 + i * 256, 256) for i in range(2)]
        ada_used = [None, None]
        n_ada = [0]

        def ada(name, lead, c0, c1, conds, dst, bias, on_pe):
            nc_ = conds.shape[1]

            def half(i, k0, toks):
                r, v, tok = tile(name, lead, k0, k0 + 4, c0 + i * P, c0 + (i + 2) * P, "raw")
                if k0 == 0:
                    state["q"] = n_ada[0] % 2
                    n_ada[0] += 1
                q = state["q"]
                if on_pe:
                    pe.wait(tok, t_c)
                    if k0 == 0:
                        state["b"] = bank()
                    o = banks[state["b"]][0:nc_, 0:256]
                    t = chain(o, [(conds[:, :, k0 + k], v[:, k, :]) for k in range(4)], k0 == 0, k0 == 4)
                    raw_free[r] = (t,)
                    if k0 == 4:
                        rows = ada_acc[q][0:nc_, :]
                        t = act.op(lambda e: e.activation(rows, o, ACT.Copy), t, ada_used[q])
                        free[state["b"]] = t
                        late.append(lambda: last(i, q, t, rows, ident[0:nc_, 0:nc_], toks))
                else:
                    t = None
                    acc = ada_acc[q]
                    for k in range(4):
                        c = conds[:, 0, k0 + k:k0 + k + 1]
                        if k0 + k == 0:
                            t = dve.op(lambda e, c=c: e.tensor_scalar(acc[:, :], v[:, 0, :], c, None, ALU.mult),
                                       tok, t_c, ada_used[q])
                        else:
                            t = dve.op(lambda e, k=k, c=c: e.scalar_tensor_tensor(
                                out=acc[:, :], in0=v[:, k, :], scalar=c, in1=acc[:, :], op0=ALU.mult, op1=ALU.add),
                                tok, t or state["t"])
                    state["t"] = t
                    raw_free[r] = (t,)
                    if k0 == 4:
                        late.append(lambda: last(i, q, t, acc, ones_1[:, 0:1], toks))

            state = {}

            def last(i, q, t, left, right, toks):
                pe.wait(t, t_ones[3], t_in)
                b = bank()
                for j in range(2):
                    t = mm_end(banks[b][:, j * nc_:(j + 1) * nc_], left[:, j * P:(j + 1) * P], right, True, True)
                ada_used[q] = t
                src = banks[b][:, 0:2 * nc_].rearrange("p (j n) -> p j n", n=nc_)
                bb = bias[:, i:i + 2].rearrange("p (j o) -> p j o", o=1).to_broadcast([P, 2, nc_])
                free[b] = dve.op(lambda e: e.tensor_tensor(dst[:, i:i + 2, :], src, bb, ALU.add), t, t_in)
                toks.append(free[b])

            toks = []
            return [lambda i=i, k0=k0: half(i, k0, toks) for i in range(0, (c1 - c0) // P, 2) for k0 in (0, 4)], toks

        behind = []
        late = []

        def late_parts():
            todo = late[:]
            late.clear()
            for f in todo:
                f()

        def one_behind():
            late_parts()
            if behind:
                behind.pop(0)()

        def all_behind(n=0):
            while len(behind) > n:
                one_behind()
            late_parts()

        def scale_vec(dst, g, sc, *waits):
            return dve.op(lambda e: e.scalar_tensor_tensor(out=dst, in0=sc, scalar=1.0, in1=g,
                                                           op0=ALU.add, op1=ALU.mult), *waits)

        def rsqrt(v, y, u, *waits):
            t = act.op(lambda e: e.activation(y, v, ACT.Ln), *waits)
            t = act.op(lambda e: e.activation(y, y, ACT.Exp, scale=-0.5), t)
            t = dve.op(lambda e: e.scalar_tensor_tensor(out=u, in0=v, scalar=-0.5, in1=y, op0=ALU.mult, op1=ALU.mult), t)
            t = dve.op(lambda e: e.tensor_tensor(u, u, y, ALU.mult), t)
            return dve.op(lambda e: e.scalar_tensor_tensor(out=y, in0=u, scalar=1.5, in1=y, op0=ALU.add, op1=ALU.mult), t)

        def mean_sq(o, ones, nk, sq, *waits):
            pe.wait(t_ones[3], *waits)
            b = bank()
            t = chain(banks[b][:, 0:T], [(ones[:, :], sq[:, k, :]) for k in range(nk)])
            free[b] = dve.op(lambda e: e.tensor_scalar(o, banks[b][:, 0:T], EPS, None, ALU.add), t)
            return free[b]

        def norm_mod(src, a, sh, dst, *waits):
            return norm_apply(src, a, sh, dst, nr[:, :], norm_stats(src, nr[:, :], *waits))

        def norm_stats(src, nr, *waits):
            t = act.op(lambda e: e.activation(nsq[:, :, :], src, ACT.Square), *waits)
            t = mean_sq(nsq[:, 0, :], ones_d, KD, nsq, t)
            return rsqrt(nsq[:, 0, :], nr, nsq[:, 1, :], t)

        def norm_apply(src, a, sh, dst, nr, t, *waits):
            dve.wait(*waits)
            o = nsq if dst is None or isinstance(dst, Pair) else dst
            toks = []
            rb = nr.rearrange("p (o t) -> p o t", o=1).to_broadcast([P, 2, T])
            for k in range(0, KD, 2):
                t1 = dve.op(lambda e, k=k: e.tensor_tensor(nsq[:, k:k + 2, :], src[:, k:k + 2, :], rb, ALU.mult), t)
                for j in (k, k + 1):
                    if sh is None:
                        t2 = dve.op(lambda e, j=j: e.tensor_scalar(o[:, j, :], nsq[:, j, :], a[:, j:j + 1], None,
                                                                   ALU.mult), t1)
                    else:
                        t2 = dve.op(lambda e, j=j: e.tensor_scalar(o[:, j, :], nsq[:, j, :], a[:, j:j + 1],
                                                                   sh[:, j:j + 1], ALU.mult, ALU.add), t1)
                if isinstance(dst, Pair):
                    q = Pair.__new__(Pair)
                    q.hi, q.lo = dst.hi[:, k:k + 2, :], dst.lo[:, k:k + 2, :]
                    toks += split_into(q, nsq[:, k:k + 2, :], t2)
                else:
                    toks += [t2, t2]
            return toks

        def project(name, lead, x, nk, consume, waits, c0=0, n=D):
            for cc in range(0, n, 256):
                bs = [bank(), bank()]
                for k0 in range(0, nk, 4):
                    k1 = min(k0 + 4, nk)
                    q, hi, lo, tw = tile(name, lead, k0, k1, c0 + cc, c0 + cc + 256)
                    for j in range(2):
                        pairs = []
                        for k in range(k0, k1):
                            cs = slice(j * P, (j + 1) * P)
                            pairs += products((hi[:, k - k0, cs], lo[:, k - k0, cs]), x.at(k), tw, waits[k])
                        t = chain(banks[bs[j]][:, 0:T], pairs, first=k0 == 0, last=k1 == nk)
                        if j == 1:
                            split_free[q] = t
                        if k1 == nk:
                            consume(cc // P + j, bs[j], t)
                    if k0 % 8 == 4:
                        one_behind()

        def add_gated(g):
            toks = []

            def consume(n, b, t):
                t = dve.op(lambda e: e.scalar_tensor_tensor(out=xT[:, n, :], in0=banks[b][:, 0:T],
                                                            scalar=g[:, n:n + 1], in1=xT[:, n, :],
                                                            op0=ALU.mult, op1=ALU.add), t)
                free[b] = t
                toks.append(t)
            return consume, toks

        gate_tmp = [work[:, i * 512:(i + 1) * 512] for i in range(4)]
        gate_used = [None] * 4
        n_gate = [0]

        def gated(pair, k, a, b, t_a, t_b, extra=None):
            i = n_gate[0] % 4
            n_gate[0] += 1
            n = a.shape[1]
            tmp = gate_tmp[i][:, 0:n * T].rearrange("p (x y) -> p x y", x=n)
            ta = act.op(lambda e: e.activation(tmp, a, ACT.Silu), t_a, gate_used[i])

            def finish(b, t_b):
                tb = dve.op(lambda e: e.tensor_tensor(tmp, b, tmp, ALU.mult), ta, t_b)
                t = tb
                if extra is not None:
                    t = dve.op(lambda e: e.tensor_tensor(tmp, tmp, extra[0], ALU.mult), tb, extra[1])
                q = Pair.__new__(Pair)
                q.hi, q.lo = pair.hi[:, k:k + n, :], pair.lo[:, k:k + n, :]
                toks = split_into(q, tmp, t)
                gate_used[i] = toks[-1]
                return tb, toks
            return ta, finish

        def ffn(layer, h, t_h, consume):
            hid = Pair(4096, KF, T)
            toks = []
            for c in range(FF // 256):
                fin = []
                for half in range(2):
                    def take(n, b, t):
                        ps = banks[b][:, 0:T].rearrange("p (o t) -> p o t", o=1)
                        if half == 0:
                            free[b], f = gated(hid, 2 * c + n, ps, None, t, None)
                            fin.append(f)
                        else:
                            free[b], tk = fin[n](ps, t)
                            toks.extend(tk)

                    project("ffn_w_in", layer, h, KD, take, t_h, half * FF + c * 256, 256)
            project("ffn_w_out", layer, hid, KF, consume, toks)

        mod0 = vec(32).rearrange("p (b n) -> p b n", n=2)
        steps, toks = ada("ada_w", 0, 0, 2048, cs3[:, 0:16].rearrange("p (n k) -> p n k", n=2), mod0,
                          sm("ada_b0", 0, 16), True)
        nr_c = work[:, 3072:3328]
        t_sx = norm_stats(xT[:, :, :], nr[:, :], t_x)
        t_sc = norm_stats(ctxT, nr_c, t_cx, t_sx)
        behind += steps
        all_behind()
        c1 = cs3[:, 0:8].rearrange("p (n k) -> p n k", n=1)
        modr0 = vec(32)
        steps, toks0 = ada("ada_w", 0, 2048, 6144, c1, modr0.rearrange("p (b n) -> p b n", n=1), sm("ada_b0", 16, 48), False)
        behind += steps
        modr1 = vec(48)
        steps, toks1 = ada("ada_w", 1, 0, 6144, c1, modr1.rearrange("p (b n) -> p b n", n=1), sm("ada_b1"), False)
        behind += steps
        modr2 = vec(48)
        steps, toks2 = ada("w_ada_2", None, 0, 6144, c2s.rearrange("p (n k) -> p n k", n=1),
                           modr2.rearrange("p (b n) -> p b n", n=1), sm("b_ada_2"), False)
        behind += steps
        t_mod = toks[-1]
        sh_x, sh_c = vec(8), vec(8)
        a_x, a_c = vec(8), vec(8)
        t1 = dve.op(lambda e: e.tensor_copy(sh_x, mod0[:, 0:8, 0]), t_mod)
        t2 = dve.op(lambda e: e.tensor_copy(sh_c, mod0[:, 0:8, 1]), t_mod)
        t3 = scale_vec(a_x, sm("norm1_g0"), mod0[:, 8:16, 0], t_mod)
        t4 = scale_vec(a_c, sm("norm1_g0"), mod0[:, 8:16, 1], t_mod)
        dve.wait(t4)
        hcat = Pair(0, KD, 512)
        t_hx = norm_apply(xT[:, :, :], a_x, sh_x, hcat.part(256, 512), nr[:, :], t_sx, t_sc)
        t_hc = norm_apply(ctxT, a_c, sh_c, hcat.part(0, 256), nr_c, t_sc, t_hx[-1])

        qT = ar(0, KD, T)
        kT = ar(2048, KD, 512)
        vv = ar(6144, 4, 1024)
        pT = [work[:, i * 1024:(i + 1) * 1024].rearrange("p (k q) -> p k q", k=4) for i in range(2)]
        oT = nsq[:, :, :]
        pexp = [[work[:, 2048 + i * 1024 + m * 512:2560 + i * 1024 + m * 512] for m in range(2)] for i in range(2)]
        pcomb = [ar(10240 + i * 512, 512) for i in range(2)]
        SWAP = [i ^ 16 for i in range(32)]
        rt = [work[:, i * 512:i * 512 + 256] for i in range(4)]
        ru = [work[:, i * 512 + 256:i * 512 + 512] for i in range(4)]
        rt_used = [None] * 4
        n_rope = [0]

        def rope(dst, src, t):
            i = n_rope[0] % 4
            n_rope[0] += 1
            a, b = rt[i], ru[i]
            t0 = act.op(lambda e: e.activation(a, src, ACT.Copy), t, rt_used[i])
            t1 = dve.op(lambda e: e.stream_shuffle(b, a, SWAP), t0)
            t1 = dve.op(lambda e: e.tensor_tensor(b, b, cn("sin"), ALU.mult), t1)
            t2 = dve.op(lambda e: e.tensor_tensor(a, a, cn("cos"), ALU.mult), t1)
            t3 = dve.op(lambda e: e.tensor_tensor(dst, a, b, ALU.add), t2)
            rt_used[i] = t3
            return t0, t3

        t_q = {}

        def take_q(n, b, t):
            free[b], t_q[n] = rope(qT[:, n, :], banks[b][:, 0:T], t)

        project("da_wqkv", None, hcat.part(256, 512), KD, take_q, t_hx)
        t_k = {}
        for cc in range(0, D, 256):
            bs = [bank(), bank()]
            for k0 in (0, 4):
                q, hi, lo, tw = tile("da_wqkv", None, k0, k0 + 4, D + cc, D + cc + 256)
                one_behind()
                t_n = []
                for j in range(2):
                    pairs = []
                    for k in range(4):
                        cs = slice(j * P, (j + 1) * P)
                        pairs += products((hi[:, k, cs], lo[:, k, cs]), hcat.at(k0 + k), tw, t_hc[k0 + k])
                    t_n.append(chain(banks[bs[j]][:, :], pairs, k0 == 0, k0 == 4))
                split_free[q] = t_n[1]
            for j in range(2):
                n, b, t = cc // P + j, bs[j], t_n[j]
                tc = act.op(lambda e, b=b, n=n: e.activation(kT[:, n, 0:256], banks[b][:, 0:256], ACT.Copy), t)
                free[b], t_k[n] = rope(kT[:, n, 256:512], banks[b][:, 256:512], t)
        t_v = None
        for cc in range(0, D, 256):
            bs = [bank() for _ in range(4)]
            for k0 in (0, 4):
                q, hi, lo, tw = tile("da_wqkv", None, k0, k0 + 4, 2 * D + cc, 2 * D + cc + 256)
                one_behind()
                t_n = []
                for m in range(4):
                    pairs = []
                    for k in range(4):
                        xh, xl = (v[:, k0 + k, m * P:(m + 1) * P] for v in (hcat.hi, hcat.lo))
                        pairs += products((xh, xl), (hi[:, k, :], lo[:, k, :]), tw, t_hc[k0 + k])
                    t_n.append(chain(banks[bs[m]][:, 0:256], pairs, k0 == 0, k0 == 4))
                split_free[q] = t_n[3]
            for m in range(4):
                b, t = bs[m], t_n[m]
                t_v = act.op(lambda e, b=b, m=m, cc=cc: e.activation(vv[:, m, cc:cc + 256], banks[b][:, 0:256], ACT.Copy), t)
                free[b] = t_v

        lam2 = vec(2)
        lamx = vec(2)
        lamn = vec(1)
        lp = ar(11264, 128).rearrange("p (a d) -> p a d", a=2)
        l4 = sm("lam").rearrange("p (a b d) -> p a b d", a=2, b=2)
        t = dve.op(lambda e: e.tensor_tensor(lp, l4[:, :, 0, :], l4[:, :, 1, :], ALU.mult), t_in)
        t = dve.op(lambda e: e.tensor_reduce(lam2, lp, AX, ALU.add), t)
        t = act.op(lambda e: e.activation(lamx, lam2, ACT.Exp), t)
        LAM_INIT = 0.8 - 0.6 * math.exp(-0.3 * 0)
        t = dve.op(lambda e: e.tensor_tensor(lamn, lamx[:, 1:2], lamx[:, 0:1], ALU.subtract), t)
        t_lam = dve.op(lambda e: e.tensor_scalar(lamn, lamn, -LAM_INIT, None, ALU.add), t)
        sub_g = vec(1)
        t_subg = dve.op(lambda e: e.tensor_scalar(sub_g, sm("subln"), 1.0 - LAM_INIT, None, ALU.mult), t_in)

        SCALE = 64 ** -0.5
        stat = vec(64)
        pe.wait(t_v)
        act.wait(t_k[7])
        t_o = {}
        units = [(h, qb) for h in range(8) for qb in range(2)]
        comb_tok = {}
        comb_free = [None, None]
        pT_free = [None, None]
        evac_tok = {}

        def scores(u):
            h, qb = units[u]
            pe.wait(t_q[h], t_k[h])
            st = stat[:, (u % 4) * 8:(u % 4) * 8 + 8]
            ends = []
            for m in range(2):
                b = bank()
                t = mm_end(banks[b][:, :], qT[m * 64:m * 64 + 64, h, qb * P:qb * P + P],
                           kT[m * 64:m * 64 + 64, h, :], True, True)
                t = dve.op(lambda e, b=b, m=m: e.tensor_reduce(st[:, m:m + 1], banks[b][:, :], AX, ALU.max), t)
                t = dve.op(lambda e, m=m: e.tensor_scalar(st[:, 2 + m:3 + m], st[:, m:m + 1], -SCALE, None, ALU.mult), t)
                t = act.op(lambda e, b=b, m=m: e.activation(pexp[u % 2][m], banks[b][:, :], ACT.Exp,
                                                            bias=st[:, 2 + m:3 + m], scale=SCALE,
                                                            accum_out=st[:, 4 + m:5 + m]), t, comb_free[u % 2])
                free[b] = t
                ends.append(t)
            return ends

        def combine(u, ends):
            st = stat[:, (u % 4) * 8:(u % 4) * 8 + 8]
            t = dve.op(lambda e: e.reciprocal(st[:, 6:8], st[:, 4:6]), *ends)
            t1 = dve.op(lambda e: e.tensor_tensor(st[:, 7:8], st[:, 7:8], lamn, ALU.mult), t, t_lam)
            t2 = dve.op(lambda e: e.tensor_scalar(pexp[u % 2][0], pexp[u % 2][0], st[:, 6:7], None, ALU.mult), t)
            comb_tok[u] = dve.op(lambda e: e.scalar_tensor_tensor(
                out=pcomb[u % 2], in0=pexp[u % 2][1], scalar=st[:, 7:8], in1=pexp[u % 2][0],
                op0=ALU.mult, op1=ALU.add), t1, t2, evac_tok.get(("tr", u - 2)))
            comb_free[u % 2] = comb_tok[u]

        def turn_p(u):
            h, qb = units[u]
            pe.wait(comb_tok[u], t_in)
            b = bank()
            for kt in range(4):
                o = banks[b][:, kt * P:(kt + 1) * P]
                i = pcomb[u % 2][:, kt * P:(kt + 1) * P]
                if kt < 3:
                    pe.quiet(lambda e, o=o, i=i: e.transpose(o, i, ident))
                else:
                    t = pe.op(lambda e, o=o, i=i: e.transpose(o, i, ident))
            evac_tok[("tr", u)] = t
            t = act.op(lambda e: e.activation(pT[h % 2][:, :, qb * P:qb * P + P],
                                              banks[b][:, :].rearrange("p (k q) -> p k q", k=4), ACT.Copy),
                       t, pT_free[h % 2])
            free[b] = t
            evac_tok[u] = t

        def pv(h):
            pe.wait(evac_tok[2 * h], evac_tok[2 * h + 1])
            b = bank()
            t = chain(banks[b][:, 0:T], [(vv[:, kt, h * P:(h + 1) * P], pT[h % 2][:, kt, :]) for kt in range(4)])
            pT_free[h % 2] = t
            t_o[h] = act.op(lambda e: e.activation(oT[:, h, :], banks[b][:, 0:T], ACT.Copy), t)
            free[b] = t_o[h]

        for u in range(len(units) + 2):
            if u < len(units):
                ends = scores(u)
                combine(u, ends)
            if u >= 1 and u - 1 < len(units):
                turn_p(u - 1)
            if u >= 2 and u % 2 == 1 and (u - 3) // 2 >= 0:
                pv((u - 3) // 2)
            one_behind()

        all_behind(96)
        t_modr = toks0[15]
        g1, sh2, sc2, g2 = (modr0[:, i * 8:i * 8 + 8] for i in range(4))
        a2 = vec(8)
        t_a2 = scale_vec(a2, sm("norm2_g0"), sc2, t_modr)

        osq = ar(0, KD, T)
        ors = ar(2048, KD, T)
        oru = ar(4096, KD, T)
        on = Pair(8192, KD, T)
        t = act.op(lambda e: e.activation(osq, oT, ACT.Square), t_o[7])
        for h in range(8):
            tm = mean_sq(osq[:, h, :], ones_h, 1, osq[:, h:h + 1, :], t)
        t = rsqrt(osq, ors, oru, tm)
        t_on = []
        for h in range(0, 8, 2):
            t1 = dve.op(lambda e, h=h: e.scalar_tensor_tensor(out=ors[:, h:h + 2, :], in0=oT[:, h:h + 2, :], scalar=sub_g,
                                                              in1=ors[:, h:h + 2, :], op0=ALU.mult, op1=ALU.mult),
                        t, t_subg)
            q = Pair.__new__(Pair)
            q.hi, q.lo = on.hi[:, h:h + 2, :], on.lo[:, h:h + 2, :]
            t_on += split_into(q, ors[:, h:h + 2, :], t1)
        consume, t_res = add_gated(g1)
        dve.wait(t_modr)
        project("da_wo", None, on, KD, consume, t_on)

        h = Pair(0, KD, T)
        t_h = norm_mod(xT[:, :, :], a2, sh2, h, t_res[-1], t_a2)
        consume, t_res = add_gated(g2)
        ffn(0, h, t_h, consume)

        all_behind(48)
        t_mod = toks1[23]
        sh1, sc1, g1b, sh2b, sc2b, g2b = (modr1[:, i * 8:i * 8 + 8] for i in range(6))
        a1b, a2b = vec(8), vec(8)
        t_a = scale_vec(a1b, sm("norm1_g1"), sc1, t_mod)
        t_a2 = scale_vec(a2b, sm("norm2_g1"), sc2b, t_mod)
        t_h = norm_mod(xT[:, :, :], a1b, sh1, h, t_res[-1], t_a)
        zp = ar(0, KD, 258)
        cv = ar(2064, KD, T)
        bzf = ar(4112, KD, T)
        bz = Pair(4096, KD, T)
        t_z0 = dve.op(lambda e: e.memset(zp[:, :, 0:1], 0.0), t_res[-1])
        t_z0 = dve.op(lambda e: e.memset(zp[:, :, 257:258], 0.0), t_res[-1])
        t_cv = {}
        scw = sm("sc_conv")
        t_cg = {}

        def take_cgate(n, b, t):
            free[b] = t_cg[n] = act.op(lambda e: e.activation(bzf[:, n, :], banks[b][:, 0:T], ACT.Copy), t, t_res[-1])

        def take_u(n, b, t):
            t = dve.op(lambda e: e.tensor_tensor(zp[:, n, 1:257], banks[b][:, 0:T], bzf[:, n, :], ALU.mult), t, t_cg[n])
            free[b] = t
            t = dve.op(lambda e: e.tensor_scalar(cv[:, n, :], zp[:, n, 0:256], scw[:, n:n + 1], None,
                                                 ALU.mult), t, t_z0)
            for q in range(1, 3):
                t = dve.op(lambda e, q=q: e.scalar_tensor_tensor(
                    out=cv[:, n, :], in0=zp[:, n, q:q + 256], scalar=scw[:, q * 8 + n:q * 8 + n + 1],
                    in1=cv[:, n, :], op0=ALU.mult, op1=ALU.add), t)
            t_cv[n] = t

        t_bz = []

        def take_b(n, b, t):
            t = dve.op(lambda e: e.tensor_tensor(bzf[:, n, :], banks[b][:, 0:T], cv[:, n, :], ALU.mult), t, t_cv[n])
            free[b] = t
            q = Pair.__new__(Pair)
            q.hi, q.lo = bz.hi[:, n:n + 1, :], bz.lo[:, n:n + 1, :]
            t_bz.extend(split_into(q, bzf[:, n:n + 1, :], t))

        project("sc_w_in", None, h, KD, take_cgate, t_h, D)
        project("sc_w_in", None, h, KD, take_u, t_h, 2 * D)
        project("sc_w_in", None, h, KD, take_b, t_h, 0)
        consume, t_res = add_gated(g1b)
        project("sc_w_out", None, bz, KD, consume, t_bz)
        t_h = norm_mod(xT[:, :, :], a2b, sh2b, h, t_res[-1], t_a2)
        consume, t_res = add_gated(g2b)
        ffn(1, h, t_h, consume)

        all_behind()
        t_mod = toks2[23]
        sh1, sc1, g1c, sh2c, sc2c, g2c = (modr2[:, i * 8:i * 8 + 8] for i in range(6))
        a1c, a2c = vec(8), vec(8)
        t_a = scale_vec(a1c, sm("norm_mix"), sc1, t_mod)
        t_a2 = scale_vec(a2c, sm("norm_ffn"), sc2c, t_mod)
        t = norm_mod(xT[:, :, :], sm("final_g"), None, xT[:, :, :], t_res[-1])
        t_h = norm_mod(xT[:, :, :], a1c, sh1, h, t[-1], t_a)

        DTC, XPC, GTC = 6144, 6176, 7200
        xbc = ar(0, 32, T)
        xdt = ar(8192, 2, 2048)
        lt = ar(12288, 192)

        r, vdt, tok = tile("w_in_2", None, 0, KD, DTC, DTC + 32, "raw")
        pe.wait(tok, t_h[-1])
        b = bank()
        for m in range(2):
            t = chain(banks[b][:, m * 32:m * 32 + 32], [(nsq[:, k, m * P:(m + 1) * P], vdt[:, k, :]) for k in range(KD)])
        raw_free[r] = (t,)
        u_, dt_, a_ = (lt[:, i * 64:i * 64 + 64] for i in range(3))
        e_, w_, q_ = (nr[:, i * 64:i * 64 + 64] for i in range(3))
        b3 = lambda v: v.rearrange("p (c h) -> p c h", c=2)
        bc = lambda v: v.rearrange("p (o h) -> p o h", o=1).to_broadcast([P, 2, 32])
        pb = banks[b][:, 0:64].rearrange("p (c h) -> p c h", c=2)
        t = dve.op(lambda e: e.tensor_tensor(b3(u_), pb, bc(sm("dt_bias")), ALU.add), t)
        free[b] = t
        t = dve.op(lambda e: e.scalar_tensor_tensor(out=e_, in0=u_, scalar=-1.0, in1=u_, op0=ALU.mult, op1=ALU.max), t)
        t = act.op(lambda e: e.activation(e_, e_, ACT.Exp, scale=-1.0), t)
        t = dve.op(lambda e: e.tensor_scalar(w_, e_, 1.0, None, ALU.add), t)
        t = act.op(lambda e: e.activation(q_, w_, ACT.Ln), t)
        t = dve.op(lambda e: e.tensor_scalar(dt_, w_, 1.0, None, ALU.is_equal), t)
        t = dve.op(lambda e: e.tensor_tensor(q_, q_, dt_, ALU.add), t)
        t = dve.op(lambda e: e.scalar_tensor_tensor(out=w_, in0=w_, scalar=-1.0, in1=dt_, op0=ALU.add, op1=ALU.add), t)
        t = dve.op(lambda e: e.reciprocal(w_, w_), t)
        t = dve.op(lambda e: e.tensor_tensor(q_, q_, w_, ALU.mult), t)
        t = dve.op(lambda e: e.tensor_tensor(q_, q_, e_, ALU.mult), t)
        t_dt = dve.op(lambda e: e.scalar_tensor_tensor(out=dt_, in0=u_, scalar=0.0, in1=q_, op0=ALU.max, op1=ALU.add), t)
        A_ = vec(32)
        t = act.op(lambda e: e.activation(A_, sm("a_log"), ACT.Exp))
        t = dve.op(lambda e: e.tensor_scalar(A_, A_, -1.0, None, ALU.mult), t)
        t_av = dve.op(lambda e: e.tensor_tensor(b3(a_), b3(dt_), bc(A_), ALU.mult), t, t_dt)

        praw = [work[:, i * 1024:i * 1024 + 259] for i in range(4)]
        pacc = [work[:, i * 1024 + 260:i * 1024 + 516] for i in range(4)]
        ptmp = [work[:, i * 1024 + 516:i * 1024 + 772] for i in range(4)]
        t_pad = [dve.op(lambda e, i=i: e.memset(praw[i][:, 0:3], 0.0), t_h[-1]) for i in range(4)]
        p_used = [t_pad[3]] * 4
        cw, cb = sm("conv_w"), sm("conv_b")
        t_xbc = {}

        def take_xbc(n, b, t):
            i = n % 4
            raw, acc = praw[i], pacc[i]
            t = act.op(lambda e: e.activation(raw[:, 3:259], banks[b][:, 0:T], ACT.Copy), t, p_used[i])
            free[b] = t
            t = dve.op(lambda e: e.tensor_scalar(acc, raw[:, 0:256], cw[:, n:n + 1], cb[:, n:n + 1],
                                                 ALU.mult, ALU.add), t)
            for q in range(1, 4):
                t = dve.op(lambda e, q=q: e.scalar_tensor_tensor(
                    out=acc, in0=raw[:, q:q + 256], scalar=cw[:, q * 32 + n:q * 32 + n + 1], in1=acc,
                    op0=ALU.mult, op1=ALU.add), t)
            p_used[i] = t_xbc[n] = silu_into(xbc[:, n, :], acc, t)

        project("w_in_2", None, h, KD, take_xbc, t_h, 2048, 4096)

        cs_ = u_
        b = bank()
        pe.wait(t_av)
        for c in range(2):
            t = mm_end(banks[b][:, c * 32:c * 32 + 32], triu, a_[:, c * 32:c * 32 + 32], True, True)
        t_cs = act.op(lambda e, b=b: e.activation(cs_, banks[b][:, 0:64], ACT.Copy), t)
        free[b] = t_cs

        nsf = nsq[:, :, :].rearrange("p k t -> p (k t)")
        Bt = nsf[:, 0:1024].rearrange("p (g n) -> p g n", g=8)
        t_xdt = {}
        for c in range(2):
            for q in range(4):
                b = bank()
                for j in range(4):
                    n = 4 * q + j
                    pe.wait(t_xbc[n])
                    o, i = banks[b][:, j * P:(j + 1) * P], xbc[:, n, c * P:(c + 1) * P]
                    t = pe.op(lambda e, o=o, i=i: e.transpose(o, i, ident))
                src = banks[b][:, :].rearrange("p (h d) -> p h d", d=64)
                dst = xdt[:, c, q * 512:(q + 1) * 512].rearrange("p (h d) -> p h d", d=64)
                dtb = dt_[:, c * 32 + q * 8:c * 32 + q * 8 + 8].rearrange("p (h o) -> p h o", o=1).to_broadcast([P, 8, 64])
                t_xdt[c, q] = dve.op(lambda e, src=src, dst=dst, dtb=dtb: e.tensor_tensor(dst, src, dtb, ALU.mult),
                                     t, t_dt)
                free[b] = t_xdt[c, q]
        for q in range(2):
            b = bank()
            for j in range(4):
                g = 4 * q + j
                pe.wait(t_xbc[16 + g])
                o, i = banks[b][:, j * P:(j + 1) * P], xbc[:, 16 + g, 0:P]
                t = pe.op(lambda e, o=o, i=i: e.transpose(o, i, ident))
            t_Bt = act.op(lambda e, b=b, q=q: e.activation(
                Bt[:, 4 * q:4 * q + 4, :], banks[b][:, :].rearrange("p (g n) -> p g n", g=4), ACT.Copy), t)
            free[b] = t_Bt

        Rs = [work[:, i * 2048:i * 2048 + 512].rearrange("p (r l) -> p r l", r=4) for i in range(2)]
        Ex = [work[:, i * 2048 + 512:i * 2048 + 1024].rearrange("p (r l) -> p r l", r=4) for i in range(2)]
        Ce = [work[:, i * 2048 + 1024:i * 2048 + 1536].rearrange("p (r l) -> p r l", r=4) for i in range(2)]
        CBm = [work[:, i * 2048 + 1536:i * 2048 + 1664] for i in range(2)]
        xdec = [work[:, i * 2048 + 1664:i * 2048 + 1920] for i in range(2)]
        dec = vec(8)
        Sg = [nsf[:, 1024 + i * 256:1280 + i * 256] for i in range(2)]
        buf_free = [list(p_used), list(p_used)]
        sg_free = [None, None]
        y_tok = {}
        dsk = sm("dskip")

        def decays(u):
            g, c = divmod(u, 2)
            i = u % 2
            b = bank()
            for r in range(4):
                h = c * 32 + 4 * g + r
                t = mm_end(banks[b][:, r * P:(r + 1) * P], a_[:, h:h + 1].to_broadcast([P, P]), triu, True, True)
            tR = act.op(lambda e: e.activation(Rs[i], banks[b][:, :].rearrange("p (r l) -> p r l", r=4), ACT.Copy),
                        t, *buf_free[i])
            free[b] = tR
            pe.wait(t_xbc[16 + g], t_xbc[24 + g])
            b2 = bank()
            t = mm_end(banks[b2][:, 0:P], xbc[:, 16 + g, c * P:(c + 1) * P], xbc[:, 24 + g, c * P:(c + 1) * P], True, True)
            tCB = dve.op(lambda e: e.tensor_tensor(CBm[i], banks[b2][:, 0:P], triu, ALU.mult), t, *buf_free[i])
            free[b2] = tCB
            if c == 0:
                h0 = 4 * g
                d4 = dec[:, 4 * (g % 2):4 * (g % 2) + 4]
                t = dve.op(lambda e: e.tensor_tensor(d4, Rs[i][:, :, 127], cs_[:, h0:h0 + 4], ALU.subtract), tR, t_cs)
                t = act.op(lambda e: e.activation(d4, d4, ACT.Exp), t)
                xv = xdt[:, 0, h0 * 64:h0 * 64 + 256].rearrange("p (r d) -> p r d", r=4)
                db = d4.rearrange("p (r o) -> p r o", o=1).to_broadcast([P, 4, 64])
                xd = xdec[i].rearrange("p (r d) -> p r d", r=4)
                tX = dve.op(lambda e: e.tensor_tensor(xd, xv, db, ALU.mult), t, t_xdt[0, g // 2])
                tC = None
            else:
                t = act.op(lambda e: e.activation(Ce[i], Rs[i], ACT.Exp), tR)
                cb_ = xbc[:, 24 + g, P:2 * P].rearrange("p (o l) -> p o l", o=1).to_broadcast([P, 4, P])
                tC = dve.op(lambda e: e.tensor_tensor(Ce[i], Ce[i], cb_, ALU.mult), t)
                tX = None
            for r in range(4):
                h = c * 32 + 4 * g + r
                t = dve.op(lambda e, r=r, h=h: e.tensor_scalar(Ex[i][:, r, :], Rs[i][:, r, :], cs_[:, h:h + 1], 0.0,
                                                               ALU.subtract, ALU.min), tR, t_cs)
            t = act.op(lambda e: e.activation(Ex[i], Ex[i], ACT.Exp), t)
            mb = CBm[i].rearrange("p (o l) -> p o l", o=1).to_broadcast([P, 4, P])
            tE = dve.op(lambda e: e.tensor_tensor(Ex[i], Ex[i], mb, ALU.mult), t, tCB)
            return tE, tX, tC

        y_bank = {}

        def outputs(u, toks):
            g, c = divmod(u, 2)
            i = u % 2
            tE, tX, tC = toks
            if c == 0:
                y_bank[g] = (bank(), bank())
                bs = bank()
                pe.wait(tX, t_Bt)
                t = mm_end(banks[bs][:, 0:256], Bt[:, g, :], xdec[i], True, True)
                t_S = act.op(lambda e: e.activation(Sg[g % 2], banks[bs][:, 0:256], ACT.Copy), t, sg_free[g % 2])
                free[bs] = t_S
                y_tok["S", g] = t_S
            pe.wait(tE, t_xdt[c, g // 2], tC, y_tok["S", g] if c else None)
            for r in range(4):
                bk = banks[y_bank[g][r // 2]]
                o = bk[64 * (r % 2):64 * (r % 2) + 64, c * P:(c + 1) * P]
                h = 4 * g + r
                t = mm_end(o, xdt[:, c, h * 64:h * 64 + 64], Ex[i][:, r, :], True, c == 0)
                if c:
                    t = mm_end(o, Sg[g % 2][:, r * 64:r * 64 + 64], Ce[i][:, r, :], False, True)
            buf_free[i] = [t]
            if c:
                sg_free[g % 2] = t
                for j in range(2):
                    n = 2 * g + j
                    bb = y_bank[g][j]
                    free[bb] = y_tok[n] = dve.op(lambda e, n=n, bb=bb: e.scalar_tensor_tensor(
                        out=xbc[:, n, :], in0=xbc[:, n, :], scalar=dsk[:, n:n + 1], in1=banks[bb][:, 0:T],
                        op0=ALU.mult, op1=ALU.add), t)

        prev = None
        for u in range(17):
            cur = decays(u) if u < 16 else None
            if prev is not None:
                outputs(u - 1, prev)
            prev = cur

        t_scan = y_tok[15]
        yf = xbc[:, 0:16, :]
        zt = [work[:, i * 256:i * 256 + 256] for i in range(2)]
        zt_used = [t_scan, t_scan]

        def take_z(n, b, t):
            i = n % 2
            free[b] = t = act.op(lambda e: e.activation(zt[i], banks[b][:, 0:T], ACT.Silu), t, zt_used[i])
            zt_used[i] = y_tok[n] = dve.op(lambda e: e.tensor_tensor(yf[:, n, :], yf[:, n, :], zt[i], ALU.mult), t)

        project("w_in_2", None, h, KD, take_z, t_h, 0, 2048)
        ysq = ar(4096, 16, T)
        gv_ = nsq[:, :, :]
        gy_ = ar(8192, 8, T)
        gu_ = ar(10240, 8, T)
        gg = sm("ssd_g")
        yT = Pair(4096, 16, T)

        def group_norm():
            for g in range(8):
                t = act.op(lambda e, g=g: e.activation(ysq[:, 2 * g:2 * g + 2, :], yf[:, 2 * g:2 * g + 2, :], ACT.Square),
                           y_tok[2 * g + 1])
                tm = mean_sq(gv_[:, g, :], ones_g, 2, ysq[:, 2 * g:2 * g + 2, :], t)
            t = rsqrt(gv_, gy_, gu_, tm)
            toks = []
            for n in range(0, 16, 2):
                for j in (n, n + 1):
                    t2 = dve.op(lambda e, j=j: e.scalar_tensor_tensor(out=yf[:, j, :], in0=yf[:, j, :],
                                                                      scalar=gg[:, j:j + 1], in1=gy_[:, j // 2, :],
                                                                      op0=ALU.mult, op1=ALU.mult), t)
                q = Pair.__new__(Pair)
                q.hi, q.lo = yT.hi[:, n:n + 2, :], yT.lo[:, n:n + 2, :]
                toks += split_into(q, yf[:, n:n + 2, :], t2)
            return toks

        t_y = group_norm()

        pp = [work[:, 512 + i * 1024:512 + i * 1024 + 272] for i in range(2)]
        pq = [[work[:, 512 + i * 1024 + 272:512 + i * 1024 + 544], work[:, 512 + i * 1024 + 544:512 + i * 1024 + 816]]
              for i in range(2)]
        pooled = ar(4096, KD, T)
        mixf = ar(6144, KD, T)
        mixp = Pair(0, KD, T)
        pz = [pool.op(lambda e, i=i: e.memset(pp[i][:, 0:16], 0.0), t_scan) for i in range(2)]
        pp_used = [pz[1], pz[1]]
        t_pool = {}

        def take_xp(n, b, t):
            i = n % 2
            t = act.op(lambda e: e.activation(pp[i][:, 16:272], banks[b][:, 0:T], ACT.Copy), t, pp_used[i])
            free[b] = t
            src, w, q = pp[i], 1, 0
            for step in range(n // 2 + 1):
                dst = pq[i][q]
                t = pool.op(lambda e, src=src, dst=dst, w=w: e.tensor_tensor(
                    dst[:, 2 * w:272], src[:, 2 * w:272], src[:, w:272 - w], ALU.add), t)
                src, w, q = dst, 2 * w, 1 - q
            g = n // 2
            iw = cn("invw", g * 16, g * 16 + 16)
            dst = pq[i][q]
            t0 = pool.op(lambda e: e.tensor_tensor(dst[:, 16:32], src[:, 16:32], iw, ALU.mult), t)
            t = pool.op(lambda e: e.tensor_scalar(dst[:, 32:272], src[:, 32:272], 0.5 ** (g + 1), None, ALU.mult), t)
            t = pool.op(lambda e: e.tensor_tensor(pooled[:, n, :], dst[:, 16:272], pp[i][:, 16:272], ALU.subtract),
                        t0, t, t_y[-1])
            pp_used[i] = t_pool[n] = t

        project("w_in_2", None, h, KD, take_xp, t_h, XPC, 1024)

        gts = ar(8192, 16, T)
        t_gt = {}

        def take_gt(n, b, t):
            v = gts[:, n, :]
            free[b] = t_gt[n] = act.op(lambda e: e.activation(v, banks[b][:, 0:T], ACT.Sigmoid), t, t_y[-1])

        project("w_in_2", None, h, KD, take_gt, t_h, GTC, 2048)

 
        psc = sm("pool_scale")
        t_mx = []
        for n in range(8):
            g, j = divmod(n, 2)
            if n % 4 == 0:
                r, vp, tok = tile("pool_w_2", None, n, n + 4, 0, 256, "raw")
                pe.wait(tok)
            pe.wait(t_pool[2 * g], t_pool[2 * g + 1])
            b = bank()
            t = chain(banks[b][:, 0:T], [(vp[:, 2 * g + k - n // 4 * 4, j * P:(j + 1) * P], pooled[:, 2 * g + k, :]) for k in range(2)])
            t1 = dve.op(lambda e, n=n, b=b: e.tensor_scalar(mixf[:, n, :], banks[b][:, 0:T], psc[:, n:n + 1], None,
                                                            ALU.mult), t)
            free[b] = t1
            q = Pair.__new__(Pair)
            q.hi, q.lo = mixp.hi[:, n:n + 1, :], mixp.lo[:, n:n + 1, :]
            t_mx += split_into(q, mixf[:, n:n + 1, :], t1)
            raw_free[r] = (t,)

        t_m1 = {}

        def take_ssd(n, b, t):
            free[b] = t_m1[n] = dve.op(lambda e: e.tensor_tensor(gts[:, n, :], banks[b][:, 0:T], gts[:, n, :], ALU.mult),
                                       t, t_gt[n])

        project("w_br_ssd_2", None, yT, 16, take_ssd, t_y)
        t_m2 = []
        mix = Pair(4096, KD, T)

        def take_pool(n, b, t):
            t = dve.op(lambda e: e.tensor_tensor(gts[:, 8 + n, :], banks[b][:, 0:T], gts[:, 8 + n, :], ALU.mult),
                       t, t_gt[8 + n])
            free[b] = t
            t = dve.op(lambda e: e.tensor_tensor(gts[:, n, :], gts[:, n, :], gts[:, 8 + n, :], ALU.add), t, t_m1[n])
            q = Pair.__new__(Pair)
            q.hi, q.lo = mix.hi[:, n:n + 1, :], mix.lo[:, n:n + 1, :]
            t_m2.extend(split_into(q, gts[:, n:n + 1, :], t))

        project("w_br_pool_2", None, mixp, KD, take_pool, t_mx)
        consume, t_res = add_gated(g1c)
        project("w_out_2", None, mix, KD, consume, t_m2)

        t_u = norm_mod(xT[:, :, :], a2c, sh2c, h, t_res[-1], t_a2)
        r, vr, tok = tile("w_router_2", None, 0, KD, 0, 64, "raw")
        pe.wait(tok, t_u[-1])
        wT = ar(1024, T)[0:64, :]
        b = bank()
        for m in range(2):
            t = chain(banks[b][:, m * 64:m * 64 + 64], [(nsq[:, k, m * P:(m + 1) * P], vr[:, k, :]) for k in range(KD)])
        raw_free[r] = (t,)
        lg = banks[b][:, 0:128]
        scs = ar(0, 128)
        cho = ar(128, 128)
        msk = ar(256, 128)
        m8 = ar(384, 2, 64)
        gsc = ar(512, 16)
        gv = ar(528, 16)
        rpl = ar(544, 128)
        gmk = ar(672, 16)
        top = ar(688, 16)
        den = ar(704, 2)
        wts = ar(706, 128)
        three = lambda v, a: v.rearrange("p (a b) -> p a b", a=a)
        t = act.op(lambda e: e.activation(scs, lg, ACT.Exp, scale=-1.0), t)
        free[b] = t
        t = dve.op(lambda e: e.tensor_scalar(scs, scs, 1.0, None, ALU.add), t)
        t = dve.op(lambda e: e.reciprocal(scs, scs), t)
        rb = sm("router_bias").rearrange("p (o n) -> p o n", o=1).to_broadcast([P, 2, 64])
        t = dve.op(lambda e: e.tensor_tensor(three(cho, 2), three(scs, 2), rb, ALU.add), t)
        bw = bank()

        def route(m, t):
            cm = cho[:, m * 64:m * 64 + 64]
            sm_ = scs[:, m * 64:m * 64 + 64]
            mk = msk[:, m * 64:m * 64 + 64]
            wm = wts[:, m * 64:m * 64 + 64]
            for g in range(8):
                tg = dve.op(lambda e, g=g: e.max(m8[:, m, g * 8:g * 8 + 8], cm[:, g * 8:g * 8 + 8]), t)
            m3 = three(m8[:, m, :], 8)
            gs, gvm, gmm, tp = (v[:, m * 8:m * 8 + 8] for v in (gsc, gv, gmk, top))
            t2 = dve.op(lambda e: e.tensor_tensor(gs, m3[:, :, 0], m3[:, :, 1], ALU.add), tg)
            t2 = dve.op(lambda e: e.max(gvm, gs), t2)
            t2 = dve.op(lambda e: e.memset(gvm[:, 4:8], BIG), t2)
            t2 = dve.op(lambda e: e.match_replace(gmm, gvm, gs, -BIG), t2)
            t2 = dve.op(lambda e: e.tensor_tensor(gmm, gmm, gs, ALU.not_equal), t2)
            gb = gmm.rearrange("p (g o) -> p g o", o=1).to_broadcast([P, 8, 8])
            t3 = dve.op(lambda e: e.tensor_scalar(gs, gmm, 1.0, BIG, ALU.subtract, ALU.mult), t2)
            t2 = dve.op(lambda e: e.tensor_tensor(three(mk, 8), three(cm, 8), gb, ALU.mult), t2)
            gsb = gs.rearrange("p (g o) -> p g o", o=1).to_broadcast([P, 8, 8])
            t2 = dve.op(lambda e: e.tensor_tensor(three(mk, 8), three(mk, 8), gsb, ALU.add), t2, t3)
            t2 = dve.op(lambda e: e.max(tp, mk), t2)
            rp = rpl[:, m * 64:m * 64 + 64]
            t2 = dve.op(lambda e: e.match_replace(rp, tp, mk, -3e30), t2)
            t2 = dve.op(lambda e: e.tensor_tensor(rp, rp, mk, ALU.not_equal), t2)
            t2 = dve.op(lambda e: e.tensor_tensor(wm, rp, sm_, ALU.mult), t2)
            dm = den[:, m:m + 1]
            t2 = dve.op(lambda e: e.tensor_reduce(dm, wm, AX, ALU.add), t2)
            t2 = dve.op(lambda e: e.reciprocal(dm, dm), t2)
            t2 = dve.op(lambda e: e.tensor_scalar(wm, wm, dm, 2.5, ALU.mult, ALU.mult), t2)
            pe.wait(t2)
            return pe.op(lambda e: e.transpose(banks[bw][0:64, m * P:(m + 1) * P], wm, ident))

        t_wt = [route(m, t) for m in range(2)]
        t_wT = act.op(lambda e: e.activation(wT, banks[bw][0:64, 0:T], ACT.Copy), t_wt[1])
        free[bw] = t_wT

        for b in range(4, 8):
            pe.wait(free[b])
        active[0] = [0, 1, 2, 3]
        hidE = [Pair(4096 + i * 1024, 2, T) for i in range(2)]
        wrow = [ar(1280 + i * 256, T) for i in range(2)]
        hid_used = [t_res[-1], t_res[-1]]
        wrow_used = [None, None]
        acc = [banks[4 + n // 2][:, (n % 2) * T:(n % 2) * T + T] for n in range(8)]

        def shared_bank(todo):
            for n, (o, l, x, st, en, w) in enumerate(todo):
                pe.wait(*w)
                (pe.op if n == len(todo) - 1 else pe.quiet)(
                    lambda e, o=o, l=l, x=x, st=st, en=en: e.matmul(o, l, x, start=st, stop=en, skip_group_check=True))
            return (pe.sem, pe.count)

        def expert_in(i):
            q = i % 2
            extra = None
            names = ("ws_gate_2", "ws_up_2") if i == 0 else ("we_gate_2", "we_up_2")
            lead = None if i == 0 else i - 1
            if i:
                bw = bank()
                pe.wait(t_wT)
                t = mm_end(banks[bw][:, 0:T], ident[0:64, lead:lead + 1].to_broadcast([64, P]), wT, True, True)
                t = act.op(lambda e: e.activation(wrow[q], banks[bw][:, 0:T], ACT.Copy), t, wrow_used[q])
                free[bw] = t
                extra = (wrow[q].rearrange("p (o t) -> p o t", o=1).to_broadcast([P, 2, T]), t)
            fin = None
            for name in names:
                b = bank()
                for k0 in (0, 4):
                    sq, hi, lo, tw = tile(name, lead, k0, k0 + 4, 0, 256)
                    todo = []
                    for j in range(2):
                        for k in range(4):
                            cs = slice(j * P, (j + 1) * P)
                            for m, (l, x, *w) in enumerate(products((hi[:, k, cs], lo[:, k, cs]), h.at(k0 + k),
                                                                    tw, t_u[k0 + k])):
                                todo.append((banks[b][:, j * T:(j + 1) * T], l, x, k0 + k + j + m == 0,
                                             k0 + k == 7 and m == 2, w))
                    t = split_free[sq] = shared_bank(todo)
                ps = three(banks[b][:, :], 2)
                if fin is None:
                    act.wait(hid_used[q])
                    dve.wait(hid_used[q])
                    free[b], fin = gated(hidE[q], 0, ps, None, t, None, extra)
                else:
                    free[b], toks = fin(ps, t)
            wrow_used[q] = toks[-1]
            return toks

        def expert_out(i, t_hid, first, last):
            q = i % 2
            for n0 in (0, 4):
                sq, hi, lo, tw = tile("ws_down_2" if i == 0 else "we_down_2", None if i == 0 else i - 1, 0, 2,
                                      n0 * P, n0 * P + 512)
                todo = []
                for n in range(n0, n0 + 4):
                    for k in range(2):
                        cs = slice((n - n0) * P, (n - n0 + 1) * P)
                        for m, (l, x, *w) in enumerate(products((hi[:, k, cs], lo[:, k, cs]), hidE[q].at(k), tw, t_hid[k])):
                            todo.append((acc[n], l, x, first and k == 0 and m == 0 and n % 2 == 0,
                                         last and k == 1 and m == 2, w))
                t = split_free[sq] = shared_bank(todo)
            hid_used[q] = t
            return t

        prev = None
        for i in range(NE + 2):
            cur = expert_in(i) if i <= NE else None
            if prev is not None:
                t_acc = expert_out(i - 1, prev, i == 1, i == NE + 1)
            prev = cur

        for n in range(8):
            t = dve.op(lambda e, n=n: e.scalar_tensor_tensor(out=xT[:, n, :], in0=acc[n], scalar=g2c[:, n:n + 1],
                                                             in1=xT[:, n, :], op0=ALU.mult, op1=ALU.add), t_acc)
        t = norm_mod(xT[:, :, :], sm("final_g2"), None, None, t)[-1]
        s_out = sem("s_out")
        sp.quiet(lambda e: e.dma_start(out.rearrange("(k p) t -> p k t", p=P), nsq[:, :, :]).then_inc(s_out, 16), t)
        sp.wait((s_out, 16))
        if plan is None:
            return order

        block = ctx.enter_context(nc.Block())
        block.sync(sp.run)
        block.scalar(act.run)
        block.vector(dve.run)
        block.gpsimd(pool.run)
        block.tensor(pe.run)


def _cols(v):
    return np.ascontiguousarray(v.reshape(-1, P).T)


def _constants():
    f = np.float32
    tok = np.arange(T)
    inv = (1.0 / (f(10000.0) ** (np.arange(0, 32, 2, dtype=f) / f(32)))).astype(f)
    ang = np.concatenate([(tok // 64).astype(f)[:, None] * inv, (tok % 64).astype(f)[:, None] * inv], axis=-1)
    d = np.arange(P) % 64
    idx = (d // 32) * 16 + d % 16
    sign = np.where(d % 32 < 16, -1.0, 1.0).astype(f)
    cos = np.cos(ang).astype(f)[:, idx].T
    sin = np.sin(ang).astype(f)[:, idx].T * sign[:, None]
    invw = np.stack([1.0 / np.minimum(tok + 1, w) for w in (2, 4, 8, 16)]).astype(f)[:, 0:16].reshape(1, -1)
    return np.concatenate([np.eye(P, dtype=f), np.triu(np.ones((P, P), f)), cos, sin,
                           np.broadcast_to(invw, (P, 64))], axis=1).astype(f)


def kernel(**inputs):
    import concourse.bacc as bacc
    from concourse.bass_utils import run_bass_kernel_spmd

    a = {k: np.asarray(v) for k, v in inputs.items()}
    row = lambda v: np.broadcast_to(v.reshape(1, -1), (P, v.size))
    small = np.concatenate([
        _cols(a["c"]), _cols(a["c_ctx"]), _cols(a["c_2"]), _cols(a["ada_b"][0]), _cols(a["ada_b"][1]),
        _cols(a["b_ada_2"]), _cols(a["norm1_g"][0]), _cols(a["norm1_g"][1]), _cols(a["norm2_g"][0]),
        _cols(a["norm2_g"][1]), _cols(a["final_g"]), _cols(a["da_subln_g"]), _cols(a["sc_conv_w"]),
        _cols(a["norm_mix_g_2"]), _cols(a["conv_w_2"]), _cols(a["conv_b_2"]),
        _cols(np.repeat(a["D_skip_2"][0], 64)), _cols(a["ssd_norm_g_2"]), _cols(a["pool_scale_2"]),
        _cols(a["norm_ffn_g_2"]), _cols(a["final_norm_g_2"]), row(a["dt_bias_2"]), row(a["A_log_2"]),
        row(a["router_bias_2"]), row(a["da_lambda"]),
    ], axis=1)
    arrays = {
        "small": np.ascontiguousarray(small), "const": _constants(),
        "xT": np.ascontiguousarray(a["x"][0].T), "ctxT": np.ascontiguousarray(a["ctx"][0].T),
    }
    for name in ("ada_w", "ffn_w_in", "ffn_w_out"):
        arrays[name] = np.ascontiguousarray(a[name])
    for name in ("da_wqkv", "da_wo", "sc_w_in", "sc_w_out", "w_ada_2", "w_in_2", "pool_w_2", "w_br_ssd_2",
                 "w_br_pool_2", "w_out_2", "w_router_2", "we_gate_2", "we_up_2", "we_down_2",
                 "ws_gate_2", "ws_up_2", "ws_down_2"):
        arrays[name] = np.ascontiguousarray(a[name][0])
    plan = None
    for _ in range(2):
        nc = bacc.Bacc("TRN2", target_bir_lowering=False, num_devices=1)
        I = {k: nc.dram_tensor(f"in_{k}", v.shape, F32, kind="ExternalInput").ap() for k, v in arrays.items()}
        out = nc.dram_tensor("out_0", (D, T), F32, kind="ExternalOutput").ap()
        plan = program(nc, I, out, plan)
    r = run_bass_kernel_spmd(nc, [{f"in_{k}": v for k, v in arrays.items()}], core_ids=[0])
    return np.ascontiguousarray(r.results[0]["out_0"].T)[None]
```

```python
import math
from contextlib import ExitStack

import numpy as np
import concourse.bass as bass
import concourse.mybir as mybir

F32 = mybir.dt.float32
F32R = mybir.dt.float32r
ALU = mybir.AluOpType
ACT = mybir.ActivationFunctionType
AX = mybir.AxisListType.X

P = 128
T = 256
D = 1024
KD = D // P
TILE = 1024
FF = 2816
KF = FF // P
NE = 64
EPS = 1e-6
BIG = 1e30

SMALLS = {}
CONSTS = {}


def _layout(table, parts):
    at = 0
    for name, n in parts:
        table[name] = (at, n)
        at += n
    return at


N_SMALL = _layout(SMALLS, [
    ("c", 8), ("c_ctx", 8), ("c_2", 8), ("ada_b0", 48), ("ada_b1", 48), ("b_ada_2", 48),
    ("norm1_g0", 8), ("norm1_g1", 8), ("norm2_g0", 8), ("norm2_g1", 8), ("final_g", 8),
    ("subln", 1), ("sc_conv", 24), ("norm_mix", 8), ("conv_w", 128), ("conv_b", 32),
    ("dskip", 16), ("ssd_g", 16), ("pool_scale", 8), ("norm_ffn", 8), ("final_g2", 8),
    ("dt_bias", 32), ("a_log", 32), ("router_bias", 64), ("lam", 256),
])
N_CONST = _layout(CONSTS, [("ident", P), ("triu", P), ("cos", T), ("sin", T), ("invw", 64)])


class Engine:

    def __init__(self, sem):
        self.sem = sem
        self.count = 0
        self.todo = []
        self.seen = {}

    def wait(self, *tokens):
        for tok in tokens:
            if tok is None:
                continue
            sem, value = tok
            if self.seen.get(sem.name, 0) < value:
                self.seen[sem.name] = value
                self.todo.append(lambda e, s=sem, v=value: e.wait_ge(s, v))

    def op(self, fn, *waits):
        self.wait(*waits)
        self.count += 1
        self.todo.append(lambda e: fn(e).then_inc(self.sem, 1))
        return (self.sem, self.count)

    def quiet(self, fn, *waits):
        self.wait(*waits)
        self.todo.append(fn)

    def run(self, e):
        for fn in self.todo:
            fn(e)


def program(nc, I, out, plan):
    ctx = ExitStack()
    with ctx:
        def sb(name, shape, dt=F32):
            return ctx.enter_context(nc.sbuf_tensor(name, shape, dt))

        def sem(name):
            return ctx.enter_context(nc.semaphore(name))

        banks = [ctx.enter_context(nc.psum_tensor(f"bank{i}", [P, 512], F32)) for i in range(8)]
        pe, act, dve, pool, sp = (Engine(sem(f"s_{n}")) for n in ("pe", "act", "dve", "pool", "sp"))

        NRAW = 4
        NASIS = 2
        NSPLIT = 4
        AHEAD = 2
        raw = [sb(f"raw{i}", [P, TILE]) for i in range(NRAW + NASIS)]
        whi = [sb(f"whi{i}", [P, TILE], F32R) for i in range(NSPLIT)]
        wlo = [sb(f"wlo{i}", [P, TILE], F32R) for i in range(NSPLIT)]
        low = sb("low", [P, 4096], F32R)
        small = sb("small", [P, N_SMALL])
        const = sb("const", [P, N_CONST])
        ones_d = sb("ones_d", [P, P])
        ones_h = sb("ones_h", [P, P])
        ones_1 = sb("ones_1", [P, 1])
        ones_g = sb("ones_g", [P, P])
        xT = sb("xT", [P, KD, T])
        nsq = sb("nsq", [P, KD, T])
        nr = sb("nr", [P, T])
        vecs = sb("vecs", [P, 392])
        arena = sb("arena", [P, 12480])
        work = sb("work", [P, 4096])
        top_scope = ctx.enter_context(ExitStack())
        upper = []

        def new_top(name, dt):
            top_scope.close()
            upper[:] = [top_scope.enter_context(nc.sbuf_tensor(name, [P, 11264], dt))]
            return upper[0]

        new_top("top_1", F32R)

        def rr(at, n):
            return low[:, at:at + n] if at + n <= 4096 else upper[0][:, at - 4096:at - 4096 + n]

        def sm(name, a=0, b=None):
            o, n = SMALLS[name]
            return small[:, o + a:o + (n if b is None else b)]

        def cn(name, a=0, b=None):
            o, n = CONSTS[name]
            return const[:, o + a:o + (n if b is None else b)]

        ident, triu = cn("ident"), cn("triu")

        def ar(at, *shape):
            n = int(np.prod(shape))
            v = arena[:, at:at + n]
            if len(shape) == 2:
                v = v.rearrange("p (a b) -> p a b", a=shape[0])
            elif len(shape) == 3:
                v = v.rearrange("p (a b c) -> p a b c", a=shape[0], b=shape[1])
            return v

        class Pair:

            def __init__(self, at, nk, w):
                n = nk * w
                self.hi = rr(at, n).rearrange("p (k w) -> p k w", k=nk)
                self.lo = rr(at + n, n).rearrange("p (k w) -> p k w", k=nk)

            def part(self, a, b):
                q = Pair.__new__(Pair)
                q.hi, q.lo = self.hi[:, :, a:b], self.lo[:, :, a:b]
                return q

            def at(self, k):
                return self.hi[:, k, :], self.lo[:, k, :]

        free = [None] * 8
        turn = [0]
        active = [list(range(8))]
        TAKEN = ()

        def bank():
            for _ in active[0]:
                b = active[0][turn[0] % len(active[0])]
                turn[0] += 1
                if free[b] != TAKEN:
                    pe.wait(free[b])
                    free[b] = TAKEN
                    return b
            raise RuntimeError("no bank is free")

        raw_sem = [sem(f"s_raw{i}") for i in range(NRAW + NASIS)]
        raw_count = [0] * (NRAW + NASIS)
        raw_free = [()] * (NRAW + NASIS)
        n_raw = [0, 0]

        split_free = [None] * NSPLIT
        fetched = {}
        n_split = [0]
        n_taken = [0]
        order = []
        ready = {}

        def source(spec):
            name, lead, k0, k1, c0, c1 = spec[:6]
            w = I[name] if lead is None else I[name][lead]
            if name == "pool_w_2":
                return w.rearrange("g (k p) n -> p (g k) n", p=P)[:, k0:k1, c0:c1]
            return w[k0 * P:k1 * P, c0:c1].rearrange("(k p) n -> p k n", p=P)

        def fetch(n):
            k0, k1, c0, c1 = plan[n][2:6]
            kind = plan[n][6]
            ring = kind == "raw"
            i = NRAW + n_raw[ring] % NASIS if ring else n_raw[ring] % NRAW
            if raw_free[i] is None:
                return False
            n_raw[ring] += 1
            v = raw[i][:, 0:(k1 - k0) * (c1 - c0)].rearrange("p (k n) -> p k n", k=k1 - k0)
            src = source(plan[n])
            sp.wait(*raw_free[i])
            sp.quiet(lambda e: e.dma_start(v, src).then_inc(raw_sem[i], 16))
            raw_free[i] = None
            raw_count[i] += 16
            fetched[n] = (i, v, (raw_sem[i], raw_count[i]))
            return True

        def prepare(n):
            i, v, tok = fetched[n]
            k, w = v.shape[1], v.shape[2]
            q = n_split[0] % NSPLIT
            n_split[0] += 1
            hi = whi[q][:, 0:k * w].rearrange("p (k n) -> p k n", k=k)
            lo = wlo[q][:, 0:k * w].rearrange("p (k n) -> p k n", k=k)
            t = act.op(lambda e: e.activation(hi, v, ACT.Copy), tok, split_free[q])
            t2 = dve.op(lambda e: e.tensor_tensor(lo, v, hi.bitcast(F32), ALU.subtract), t, tok, split_free[q])
            raw_free[i] = (t, t2)
            ready[n] = (q, hi, lo, t2)

        pend = []

        def run_pend():
            todo = pend[:]
            pend.clear()
            for f in todo:
                f()

        def tile(name, lead, k0, k1, c0, c1, kind="split"):
            spec = (name, lead, k0, k1, c0, c1, kind)
            n = n_taken[0]
            n_taken[0] += 1
            order.append(spec)
            if plan is None:
                run_pend()
                v = raw[0][:, 0:(k1 - k0) * (c1 - c0)].rearrange("p (k n) -> p k n", k=k1 - k0)
                return (0, v, v, None) if kind == "split" else (0, v, None)
            assert plan[n] == spec
            for ring in (0, 1):
                seen = 0
                for m in range(n, min(n + (3 if ring else 12), len(plan))):
                    if ring != (plan[m][6] == "raw"):
                        continue
                    seen += 1
                    if m not in fetched and (seen > AHEAD + 3 or not fetch(m)):
                        assert m > n
                        break
                    if plan[m][6] == "split" and seen <= AHEAD + 1 and m not in ready:
                        prepare(m)
            run_pend()
            return ready[n] if kind == "split" else fetched[n]

        def mm(o, lhsT, rhs, start, stop, **kw):
            pe.quiet(lambda e: e.matmul(o, lhsT, rhs, start=start, stop=stop, **kw))

        def mm_end(o, lhsT, rhs, start, stop, **kw):
            return pe.op(lambda e: e.matmul(o, lhsT, rhs, start=start, stop=stop, **kw))

        def chain(o, pairs, first=True, last=True):
            tok = None
            for i, (l, r, *w) in enumerate(pairs):
                pe.wait(*w)
                tok = (mm_end if i == len(pairs) - 1 else mm)(
                    o, l, r, first and i == 0, last and i == len(pairs) - 1)
            return tok

        def products(w, x, *tok):
            (wh, wl), (xh, xl) = w, x
            return [(wh, xh, *tok), (wh, xl), (wl, xh)]

        def split_into(pair, src, *waits):
            toks = []
            nk = src.shape[1]
            step = max(1, 512 // src.shape[2])
            for k in range(0, nk, step):
                e_ = min(k + step, nk)
                t = act.op(lambda e, k=k, e_=e_: e.activation(pair.hi[:, k:e_, :], src[:, k:e_, :], ACT.Copy), *waits)
                t = dve.op(lambda e, k=k, e_=e_: e.tensor_tensor(pair.lo[:, k:e_, :], src[:, k:e_, :],
                                                                 pair.hi[:, k:e_, :].bitcast(F32), ALU.subtract), t, *waits)
                toks += [t] * (e_ - k)
            return toks

        s_in = sem("s_in")
        s_small = sem("s_small")
        s_x = sem("s_x")
        s_cx = sem("s_cx")
        ctxT = ar(6144, KD, T)
        act.quiet(lambda e: e.dma_start(small[:, :], I["small"]).then_inc(s_small, 16))
        act.quiet(lambda e: e.dma_start(const[:, :], I["const"]).then_inc(s_in, 16))
        act.quiet(lambda e: e.dma_start(xT[:, :, :], I["xT"].rearrange("(k p) t -> p k t", p=P)).then_inc(s_x, 16))
        act.quiet(lambda e: e.dma_start(ctxT, I["ctxT"].rearrange("(k p) t -> p k t", p=P)).then_inc(s_cx, 16))
        t_in, t_cn, t_x, t_cx = (s_small, 16), (s_in, 16), (s_x, 16), (s_cx, 16)
        t_ones = [pool.op(lambda e, m=m, v=v: e.memset(m[:, :], v))
                  for m, v in ((ones_1, 1.0), (ones_d, 1.0 / D), (ones_g, 1.0 / 256), (ones_h, 1.0 / P))]

        vec_at = [0]

        def vec(n):
            v = vecs[:, vec_at[0]:vec_at[0] + n]
            vec_at[0] += n
            assert vec_at[0] <= 392
            return v

        def silu_into(dst, src, *waits):
            return act.op(lambda e: e.activation(dst, src, ACT.Silu), *waits)

        cs3 = vec(24)
        t_c = silu_into(cs3, small[:, 0:24], t_in)
        c2s = cs3[:, 16:24]

        ada_acc = [[ar(11392 + i * 512 + j * 256, 256) for j in range(2)] for i in range(2)]
        ada_used = [None, None]
        n_ada = [0]

        def ada(name, lead, c0, c1, conds, dst, bias, pe_steps, kind="raw"):
            nc_ = conds.shape[1]

            def half(i, k0, toks):
                r, v, tok = tile(name, lead, k0, k0 + 4, c0 + i * P, c0 + (i + 2) * P, kind)
                if k0 == 0:
                    state["q"] = n_ada[0] % 2
                    n_ada[0] += 1
                q = state["q"]
                if i // 2 in pe_steps:
                    pe.wait(tok, t_c)
                    if k0 == 0:
                        state["b"] = bank()
                    o = banks[state["b"]][0:nc_, 0:256]
                    t = chain(o, [(conds[:, :, k0 + k], v[:, k, :]) for k in range(4)], k0 == 0, k0 == 4)
                    raw_free[r] = (t,)
                    if k0 == 4:
                        rows = ada_acc[q][0][0:nc_, :]
                        t = act.op(lambda e: e.activation(rows, o, ACT.Copy), t, ada_used[q])
                        free[state["b"]] = t
                        late.append(lambda: last(i, q, (t,), [rows], ident[0:nc_, 0:nc_], toks))
                else:
                    sums = ada_acc[q]
                    ts = [None, None] if k0 == 0 else state["t"]
                    for k in range(4):
                        c = conds[:, 0, k0 + k:k0 + k + 1]
                        acc = sums[k % 2]
                        if k0 + k < 2:
                            ts[k] = dve.op(lambda e, k=k, c=c, acc=acc: e.tensor_scalar(acc, v[:, k, :], c, None, ALU.mult),
                                           tok, t_c, ada_used[q])
                        else:
                            ts[k % 2] = dve.op(lambda e, k=k, c=c, acc=acc: e.scalar_tensor_tensor(
                                out=acc, in0=v[:, k, :], scalar=c, in1=acc, op0=ALU.mult, op1=ALU.add),
                                tok, ts[k % 2])
                    state["t"] = ts
                    raw_free[r] = tuple(ts)
                    if k0 == 4:
                        t = dve.op(lambda e: e.tensor_tensor(sums[0], sums[0], sums[1], ALU.add), *ts)
                        late.append(lambda: last(i, q, (t,), sums[:1], ones_1[:, 0:1], toks))

            state = {}

            def last(i, q, ts, left, right, toks):
                pe.wait(*ts, t_ones[3], t_cn)
                b = bank()
                for j in range(2):
                    t = chain(banks[b][:, j * nc_:(j + 1) * nc_], [(l[:, j * P:(j + 1) * P], right) for l in left])
                ada_used[q] = t
                src = banks[b][:, 0:2 * nc_].rearrange("p (j n) -> p j n", n=nc_)
                bb = bias[:, i:i + 2].rearrange("p (j o) -> p j o", o=1).to_broadcast([P, 2, nc_])
                free[b] = dve.op(lambda e: e.tensor_tensor(dst[:, i:i + 2, :], src, bb, ALU.add), t, t_in)
                toks.append(free[b])

            toks = []
            return [lambda i=i, k0=k0: half(i, k0, toks) for i in range(0, (c1 - c0) // P, 2) for k0 in (0, 4)], toks

        behind = []
        late = []

        def late_parts():
            todo = late[:]
            late.clear()
            for f in todo:
                f()

        def one_behind():
            late_parts()
            if behind:
                behind.pop(0)()

        def all_behind(n=0):
            while len(behind) > n:
                one_behind()
            late_parts()

        def scale_vec(dst, g, sc, *waits):
            return dve.op(lambda e: e.scalar_tensor_tensor(out=dst, in0=sc, scalar=1.0, in1=g,
                                                           op0=ALU.add, op1=ALU.mult), *waits)

        def rsqrt(v, y, u, *waits):
            t = act.op(lambda e: e.activation(y, v, ACT.Ln), *waits)
            t = act.op(lambda e: e.activation(y, y, ACT.Exp, scale=-0.5), t)
            return newton(v, y, u, t)

        def newton(v, y, u, t):
            t = dve.op(lambda e: e.scalar_tensor_tensor(out=u, in0=v, scalar=-0.5, in1=y, op0=ALU.mult, op1=ALU.mult), t)
            t = dve.op(lambda e: e.tensor_tensor(u, u, y, ALU.mult), t)
            return dve.op(lambda e: e.scalar_tensor_tensor(out=y, in0=u, scalar=1.5, in1=y, op0=ALU.add, op1=ALU.mult), t)

        def mean_sq(o, ones, nk, sq, *waits):
            pe.wait(t_ones[3], *waits)
            b = bank()
            t = chain(banks[b][:, 0:T], [(ones[:, :], sq[:, k, :]) for k in range(nk)])
            free[b] = dve.op(lambda e: e.tensor_scalar(o, banks[b][:, 0:T], EPS, None, ALU.add), t)
            return free[b]

        def norm_stats(src, nr, *waits):
            t = act.op(lambda e: e.activation(nsq[:, :, :], src, ACT.Square), *waits)
            t = mean_sq(nsq[:, 0, :], ones_d, KD, nsq, t)
            return rsqrt(nsq[:, 0, :], nr, nsq[:, 1, :], t)

        class MeanSq:

            def __init__(self):
                self.bank = None
                self.todo = []

            def add(self, k, src, *waits):
                if self.bank is None:
                    pe.wait(t_ones[3])
                    self.bank = bank()
                t = act.op(lambda e: e.activation(nsq[:, k, :], src, ACT.Square), *waits)
                self.todo.append((k, t))
                self.some(2)

            def some(self, keep):
                while len(self.todo) > keep:
                    k, t = self.todo.pop(0)
                    pe.wait(t)
                    self.tok = mm_end(banks[self.bank][:, 0:T], ones_d[:, :], nsq[:, k, :], k == 0, k == KD - 1)

            def rsqrt(self, nr):
                self.some(0)
                o = nsq[:, 0, :]
                b = self.bank
                t = free[b] = dve.op(lambda e: e.tensor_scalar(o, banks[b][:, 0:T], EPS, None, ALU.add), self.tok)
                return rsqrt(o, nr, nsq[:, 1, :], t)

        def norm_apply(src, a, sh, dst, nr, t, *waits, ks=range(0, KD, 2)):
            dve.wait(*waits)
            o = nsq if dst is None or isinstance(dst, Pair) else dst
            toks = []
            rb = nr.rearrange("p (o t) -> p o t", o=1).to_broadcast([P, 2, T])
            for k in ks:
                t1 = dve.op(lambda e, k=k: e.tensor_tensor(nsq[:, k:k + 2, :], src[:, k:k + 2, :], rb, ALU.mult), t)
                for j in (k, k + 1):
                    if sh is None:
                        t2 = dve.op(lambda e, j=j: e.tensor_scalar(o[:, j, :], nsq[:, j, :], a[:, j:j + 1], None,
                                                                   ALU.mult), t1)
                    else:
                        t2 = dve.op(lambda e, j=j: e.tensor_scalar(o[:, j, :], nsq[:, j, :], a[:, j:j + 1],
                                                                   sh[:, j:j + 1], ALU.mult, ALU.add), t1)
                if isinstance(dst, Pair):
                    q = Pair.__new__(Pair)
                    q.hi, q.lo = dst.hi[:, k:k + 2, :], dst.lo[:, k:k + 2, :]
                    toks += split_into(q, nsq[:, k:k + 2, :], t2)
                else:
                    toks += [t2, t2]
            return toks

        def project(name, lead, x, nk, consume, waits, c0=0, n=D, n_behind=1, flush=True):
            for cc in range(0, n, 256):
                bs = [bank(), bank()]
                for k0 in range(0, nk, 4):
                    k1 = min(k0 + 4, nk)
                    q, hi, lo, tw = tile(name, lead, k0, k1, c0 + cc, c0 + cc + 256)
                    for j in range(2):
                        pairs = []
                        for k in range(k0, k1):
                            cs = slice(j * P, (j + 1) * P)
                            pairs += products((hi[:, k - k0, cs], lo[:, k - k0, cs]), x.at(k), tw, waits[k])
                        t = chain(banks[bs[j]][:, 0:T], pairs, first=k0 == 0, last=k1 == nk)
                        if j == 1:
                            split_free[q] = t
                        if k1 == nk:
                            pend.append(lambda n=cc // P + j, b=bs[j], t=t: consume(n, b, t))
                    for _ in range(n_behind if k0 % 8 == 4 else 0):
                        one_behind()
            if flush:
                run_pend()

        def add_gated(g):
            ms = MeanSq()

            def consume(n, b, t):
                t = dve.op(lambda e: e.scalar_tensor_tensor(out=xT[:, n, :], in0=banks[b][:, 0:T],
                                                            scalar=g[:, n:n + 1], in1=xT[:, n, :],
                                                            op0=ALU.mult, op1=ALU.add), t)
                free[b] = t
                ms.add(n, xT[:, n, :], t)
            return consume, ms

        gate_tmp = [work[:, i * 512:(i + 1) * 512] for i in range(4)]
        gate_used = [None] * 4
        n_gate = [0]

        def gated(pair, k, a, b, t_a, t_b):
            i = n_gate[0] % 4
            n_gate[0] += 1
            n = a.shape[1]
            tmp = gate_tmp[i][:, 0:n * T].rearrange("p (x y) -> p x y", x=n)
            ta = act.op(lambda e: e.activation(tmp, a, ACT.Silu), t_a, gate_used[i])

            def finish(b, t_b, extra=None):
                tb = dve.op(lambda e: e.tensor_tensor(tmp, b, tmp, ALU.mult), ta, t_b)
                t = tb
                if extra is not None:
                    t = dve.op(lambda e: e.tensor_tensor(tmp, tmp, extra[0], ALU.mult), tb, extra[1])
                q = Pair.__new__(Pair)
                q.hi, q.lo = pair.hi[:, k:k + n, :], pair.lo[:, k:k + n, :]
                toks = split_into(q, tmp, t)
                gate_used[i] = toks[-1]
                return tb, toks
            return ta, finish

        def ffn(layer, h, t_h, consume):
            hid = Pair(4096, KF, T)
            toks = []
            for c in range(FF // 256):
                fin = []
                for half in range(2):
                    def take(n, b, t, half=half, c=c, fin=fin):
                        ps = banks[b][:, 0:T].rearrange("p (o t) -> p o t", o=1)
                        if half == 0:
                            free[b], f = gated(hid, 2 * c + n, ps, None, t, None)
                            fin.append(f)
                        else:
                            free[b], tk = fin[n](ps, t)
                            toks.extend(tk)

                    project("ffn_w_in", layer, h, KD, take, t_h, half * FF + c * 256, 256, flush=False)
            project("ffn_w_out", layer, hid, KF, consume, toks)

        mod0 = vec(32).rearrange("p (b n) -> p b n", n=2)
        steps, toks = ada("ada_w", 0, 0, 2048, cs3[:, 0:16].rearrange("p (n k) -> p n k", n=2), mod0,
                          sm("ada_b0", 0, 16), range(8), "early")
        nr_c = work[:, 3072:3328]
        behind += steps
        all_behind(10)
        t_sx = norm_stats(xT[:, :, :], nr[:, :], t_x)
        all_behind(4)
        t_sc = norm_stats(ctxT, nr_c, t_cx, t_sx)
        all_behind()
        c1 = cs3[:, 0:8].rearrange("p (n k) -> p n k", n=1)
        modr0 = vec(32)
        steps, toks0 = ada("ada_w", 0, 2048, 6144, c1, modr0.rearrange("p (b n) -> p b n", n=1), sm("ada_b0", 16, 48), (13, 15))
        behind += steps
        modr1 = vec(48)
        steps, toks1 = ada("ada_w", 1, 0, 6144, c1, modr1.rearrange("p (b n) -> p b n", n=1), sm("ada_b1"), (1, 3))
        behind += steps
        modr2 = vec(48)
        steps, toks2 = ada("w_ada_2", None, 0, 6144, c2s.rearrange("p (n k) -> p n k", n=1),
                           modr2.rearrange("p (b n) -> p b n", n=1), sm("b_ada_2"), ())
        behind += steps
        t_mod = toks[-1]
        sh_x, sh_c = vec(8), vec(8)
        a_x, a_c = vec(8), vec(8)
        t1 = dve.op(lambda e: e.tensor_copy(sh_x, mod0[:, 0:8, 0]), t_mod)
        t2 = dve.op(lambda e: e.tensor_copy(sh_c, mod0[:, 0:8, 1]), t_mod)
        t3 = scale_vec(a_x, sm("norm1_g0"), mod0[:, 8:16, 0], t_mod)
        t4 = scale_vec(a_c, sm("norm1_g0"), mod0[:, 8:16, 1], t_mod)
        dve.wait(t4, t_cn)
        hcat = Pair(0, KD, 512)
        t_hx = norm_apply(xT[:, :, :], a_x, sh_x, hcat.part(256, 512), nr[:, :], t_sx, t_sc)

        qT = ar(0, KD, T)
        kT = ar(2048, KD, 512)
        vv = ar(6144, 4, 1024)
        pT = [work[:, i * 1024:(i + 1) * 1024].rearrange("p (k q) -> p k q", k=4) for i in range(2)]
        oT = nsq[:, :, :]
        pexp = [[work[:, 2048 + i * 1024 + m * 512:2560 + i * 1024 + m * 512] for m in range(2)] for i in range(2)]
        pcomb = [ar(10240 + i * 512, 512) for i in range(2)]
        SWAP = [i ^ 16 for i in range(32)]
        rt = [work[:, i * 512:i * 512 + 256] for i in range(4)]
        ru = [work[:, i * 512 + 256:i * 512 + 512] for i in range(4)]
        rt_used = [None] * 4
        n_rope = [0]

        two = []

        def rope(dst, src, t, done):
            i = n_rope[0] % 4
            n_rope[0] += 1
            t0 = act.op(lambda e: e.activation(rt[i], src, ACT.Copy), t, rt_used[i])
            two.append((i, dst, t0, done))
            if len(two) == 2:
                ts = [dve.op(lambda e, i=i: e.stream_shuffle(ru[i], rt[i], SWAP), t0) for i, _, t0, _ in two]
                ts = [dve.op(lambda e, i=i: e.tensor_tensor(ru[i], ru[i], cn("sin"), ALU.mult), t)
                      for (i, _, _, _), t in zip(two, ts)]
                ts = [dve.op(lambda e, i=i: e.tensor_tensor(rt[i], rt[i], cn("cos"), ALU.mult), t)
                      for (i, _, _, _), t in zip(two, ts)]
                for (i, o, _, f), t in zip(two, ts):
                    rt_used[i] = dve.op(lambda e, i=i, o=o: e.tensor_tensor(o, rt[i], ru[i], ALU.add), t)
                    f(rt_used[i])
                two.clear()
            return t0

        t_q = {}

        def take_q(n, b, t):
            free[b] = rope(qT[:, n, :], banks[b][:, 0:T], t, lambda t: t_q.__setitem__(n, t))

        t_hc = []
        for i in range(0, KD, 2):
            project("da_wqkv", None, hcat.part(256, 512), KD, lambda n, b, t, i=i: take_q(n + i, b, t), t_hx, i * P, 256,
                    n_behind=0, flush=False)
            t_hc += norm_apply(ctxT, a_c, sh_c, hcat.part(0, 256), nr_c, t_sc, t_hx[-1], ks=(i,))
        t_k = {}
        for cc in range(0, D, 256):
            bs = [bank(), bank()]
            for k0 in (0, 4):
                q, hi, lo, tw = tile("da_wqkv", None, k0, k0 + 4, D + cc, D + cc + 256)
                one_behind()
                t_n = []
                for j in range(2):
                    pairs = []
                    for k in range(4):
                        cs = slice(j * P, (j + 1) * P)
                        pairs += products((hi[:, k, cs], lo[:, k, cs]), hcat.at(k0 + k), tw, t_hc[k0 + k])
                    t_n.append(chain(banks[bs[j]][:, :], pairs, k0 == 0, k0 == 4))
                split_free[q] = t_n[1]
            for j in range(2):
                n, b, t = cc // P + j, bs[j], t_n[j]
                tc = act.op(lambda e, b=b, n=n: e.activation(kT[:, n, 0:256], banks[b][:, 0:256], ACT.Copy), t)
                free[b] = rope(kT[:, n, 256:512], banks[b][:, 256:512], t, lambda t, n=n: t_k.__setitem__(n, t))
        t_v = None
        for cc in range(0, D, 256):
            bs = [bank() for _ in range(4)]
            for k0 in (0, 4):
                q, hi, lo, tw = tile("da_wqkv", None, k0, k0 + 4, 2 * D + cc, 2 * D + cc + 256)
                one_behind()
                one_behind()
                t_n = []
                for m in range(4):
                    pairs = []
                    for k in range(4):
                        xh, xl = (v[:, k0 + k, m * P:(m + 1) * P] for v in (hcat.hi, hcat.lo))
                        pairs += products((xh, xl), (hi[:, k, :], lo[:, k, :]), tw, t_hc[k0 + k])
                    t_n.append(chain(banks[bs[m]][:, 0:256], pairs, k0 == 0, k0 == 4))
                split_free[q] = t_n[3]
            for m in range(4):
                b, t = bs[m], t_n[m]
                t_v = act.op(lambda e, b=b, m=m, cc=cc: e.activation(vv[:, m, cc:cc + 256], banks[b][:, 0:256], ACT.Copy), t)
                free[b] = t_v

        lam2 = vec(2)
        lamx = vec(2)
        lamn = vec(1)
        lp = ar(11264, 128).rearrange("p (a d) -> p a d", a=2)
        l4 = sm("lam").rearrange("p (a b d) -> p a b d", a=2, b=2)
        t = dve.op(lambda e: e.tensor_tensor(lp, l4[:, :, 0, :], l4[:, :, 1, :], ALU.mult), t_in)
        t = dve.op(lambda e: e.tensor_reduce(lam2, lp, AX, ALU.add), t)
        t = act.op(lambda e: e.activation(lamx, lam2, ACT.Exp), t)
        LAM_INIT = 0.8 - 0.6 * math.exp(-0.3 * 0)
        t = dve.op(lambda e: e.tensor_tensor(lamn, lamx[:, 1:2], lamx[:, 0:1], ALU.subtract), t)
        t_lam = dve.op(lambda e: e.tensor_scalar(lamn, lamn, -LAM_INIT, None, ALU.add), t)
        sub_g = vec(1)
        t_subg = dve.op(lambda e: e.tensor_scalar(sub_g, sm("subln"), 1.0 - LAM_INIT, None, ALU.mult), t_in)

        SCALE = 64 ** -0.5
        stat = vec(64)
        pe.wait(t_v)
        act.wait(t_k[7])
        t_o = {}
        units = [(h, qb) for h in range(8) for qb in range(2)]
        comb_tok = {}
        comb_free = [None, None]
        pT_free = [None, None]
        evac_tok = {}

        def scores(u):
            h, qb = units[u]
            pe.wait(t_q[h], t_k[h])
            st = stat[:, (u % 4) * 8:(u % 4) * 8 + 8]
            ends = []
            for m in range(2):
                b = bank()
                t = mm_end(banks[b][:, :], qT[m * 64:m * 64 + 64, h, qb * P:qb * P + P],
                           kT[m * 64:m * 64 + 64, h, :], True, True)
                t = dve.op(lambda e, b=b, m=m: e.tensor_reduce(st[:, m:m + 1], banks[b][:, :], AX, ALU.max), t)
                t = dve.op(lambda e, m=m: e.tensor_scalar(st[:, 2 + m:3 + m], st[:, m:m + 1], -SCALE, None, ALU.mult), t)
                t = act.op(lambda e, b=b, m=m: e.activation(pexp[u % 2][m], banks[b][:, :], ACT.Exp,
                                                            bias=st[:, 2 + m:3 + m], scale=SCALE,
                                                            accum_out=st[:, 4 + m:5 + m]), t, comb_free[u % 2])
                free[b] = t
                ends.append(t)
            return ends

        def combine(u, ends):
            st = stat[:, (u % 4) * 8:(u % 4) * 8 + 8]
            t = dve.op(lambda e: e.reciprocal(st[:, 6:8], st[:, 4:6]), *ends)
            t1 = dve.op(lambda e: e.tensor_tensor(st[:, 7:8], st[:, 7:8], lamn, ALU.mult), t, t_lam)
            t2 = dve.op(lambda e: e.tensor_scalar(pexp[u % 2][0], pexp[u % 2][0], st[:, 6:7], None, ALU.mult), t)
            comb_tok[u] = dve.op(lambda e: e.scalar_tensor_tensor(
                out=pcomb[u % 2], in0=pexp[u % 2][1], scalar=st[:, 7:8], in1=pexp[u % 2][0],
                op0=ALU.mult, op1=ALU.add), t1, t2, evac_tok.get(("tr", u - 2)))
            comb_free[u % 2] = comb_tok[u]

        def turn_p(u):
            h, qb = units[u]
            pe.wait(comb_tok[u], t_cn)
            b = bank()
            for kt in range(4):
                o = banks[b][:, kt * P:(kt + 1) * P]
                i = pcomb[u % 2][:, kt * P:(kt + 1) * P]
                if kt < 3:
                    pe.quiet(lambda e, o=o, i=i: e.transpose(o, i, ident))
                else:
                    t = pe.op(lambda e, o=o, i=i: e.transpose(o, i, ident))
            evac_tok[("tr", u)] = t
            t = act.op(lambda e: e.activation(pT[h % 2][:, :, qb * P:qb * P + P],
                                              banks[b][:, :].rearrange("p (k q) -> p k q", k=4), ACT.Copy),
                       t, pT_free[h % 2])
            free[b] = t
            evac_tok[u] = t

        def pv(h):
            pe.wait(evac_tok[2 * h], evac_tok[2 * h + 1])
            b = bank()
            t = chain(banks[b][:, 0:T], [(vv[:, kt, h * P:(h + 1) * P], pT[h % 2][:, kt, :]) for kt in range(4)])
            pT_free[h % 2] = t
            t_o[h] = act.op(lambda e: e.activation(oT[:, h, :], banks[b][:, 0:T], ACT.Copy), t)
            free[b] = t_o[h]

        ends = {}
        for u in range(len(units) + 4):
            if u < len(units):
                ends[u] = scores(u)
            if 1 <= u <= len(units):
                combine(u - 1, ends[u - 1])
            if 2 <= u < len(units) + 2:
                turn_p(u - 2)
            if u >= 4 and u % 2 == 0:
                pv((u - 4) // 2)
            one_behind()

        all_behind(96)
        t_modr = toks0[15]
        g1, sh2, sc2, g2 = (modr0[:, i * 8:i * 8 + 8] for i in range(4))
        a2 = vec(8)
        t_a2 = scale_vec(a2, sm("norm2_g0"), sc2, t_modr)

        osq = ar(0, KD, T)
        ors = ar(2048, KD, T)
        oru = ar(4096, KD, T)
        on = Pair(8192, KD, T)
        parts = [slice(h, h + 2) for h in range(0, 8, 2)]
        t_ln = []
        for p in parts:
            t = act.op(lambda e, p=p: e.activation(osq[:, p, :], oT[:, p, :], ACT.Square), t_o[7])
            for h in (p.start, p.start + 1):
                tm = mean_sq(osq[:, h, :], ones_h, 1, osq[:, h:h + 1, :], t)
            t_ln.append(tm)
        t_ln = [act.op(lambda e, p=p: e.activation(ors[:, p, :], osq[:, p, :], ACT.Ln), t) for p, t in zip(parts, t_ln)]
        t_y0 = [act.op(lambda e, p=p: e.activation(ors[:, p, :], ors[:, p, :], ACT.Exp, scale=-0.5), t)
                for p, t in zip(parts, t_ln)]
        t_on = []
        for h in range(0, 8, 2):
            p = parts[h // 2]
            t = newton(osq[:, p, :], ors[:, p, :], oru[:, p, :], t_y0[h // 2])
            t1 = dve.op(lambda e, h=h: e.scalar_tensor_tensor(out=ors[:, h:h + 2, :], in0=oT[:, h:h + 2, :], scalar=sub_g,
                                                              in1=ors[:, h:h + 2, :], op0=ALU.mult, op1=ALU.mult),
                        t, t_subg)
            q = Pair.__new__(Pair)
            q.hi, q.lo = on.hi[:, h:h + 2, :], on.lo[:, h:h + 2, :]
            t_on += split_into(q, ors[:, h:h + 2, :], t1)
        consume, t_res = add_gated(g1)
        dve.wait(t_modr)
        project("da_wo", None, on, KD, consume, t_on)

        h = Pair(0, KD, T)
        t_h = norm_apply(xT[:, :, :], a2, sh2, h, nr[:, :], t_res.rsqrt(nr[:, :]), t_a2)
        consume, t_res = add_gated(g2)
        ffn(0, h, t_h, consume)

        all_behind(48)
        t_mod = toks1[23]
        sh1, sc1, g1b, sh2b, sc2b, g2b = (modr1[:, i * 8:i * 8 + 8] for i in range(6))
        a1b, a2b = vec(8), vec(8)
        t_a = scale_vec(a1b, sm("norm1_g1"), sc1, t_mod)
        t_a2 = scale_vec(a2b, sm("norm2_g1"), sc2b, t_mod)
        t_h = norm_apply(xT[:, :, :], a1b, sh1, h, nr[:, :], t_res.rsqrt(nr[:, :]), t_a)
        zp = ar(0, KD, 258)
        cv = ar(2064, KD, T)
        bzf = ar(4112, KD, T)
        bz = Pair(4096, KD, T)
        t_z0 = dve.op(lambda e: e.memset(zp[:, :, 0:1], 0.0), t_h[-1])
        t_z0 = dve.op(lambda e: e.memset(zp[:, :, 257:258], 0.0), t_h[-1])
        t_cv = {}
        scw = sm("sc_conv")
        t_cg = {}

        def take_cgate(n, b, t):
            free[b] = t_cg[n] = act.op(lambda e: e.activation(bzf[:, n, :], banks[b][:, 0:T], ACT.Copy), t, t_h[-1])

        def take_u(n, b, t):
            t = dve.op(lambda e: e.tensor_tensor(zp[:, n, 1:257], banks[b][:, 0:T], bzf[:, n, :], ALU.mult), t, t_cg[n])
            free[b] = t
            t = dve.op(lambda e: e.tensor_scalar(cv[:, n, :], zp[:, n, 0:256], scw[:, n:n + 1], None,
                                                 ALU.mult), t, t_z0)
            for q in range(1, 3):
                t = dve.op(lambda e, q=q: e.scalar_tensor_tensor(
                    out=cv[:, n, :], in0=zp[:, n, q:q + 256], scalar=scw[:, q * 8 + n:q * 8 + n + 1],
                    in1=cv[:, n, :], op0=ALU.mult, op1=ALU.add), t)
            t_cv[n] = t

        t_bz = []

        def take_b(n, b, t):
            t = dve.op(lambda e: e.tensor_tensor(bzf[:, n, :], banks[b][:, 0:T], cv[:, n, :], ALU.mult), t, t_cv[n])
            free[b] = t
            q = Pair.__new__(Pair)
            q.hi, q.lo = bz.hi[:, n:n + 1, :], bz.lo[:, n:n + 1, :]
            t_bz.extend(split_into(q, bzf[:, n:n + 1, :], t))

        project("sc_w_in", None, h, KD, take_cgate, t_h, D, n_behind=2, flush=False)
        project("sc_w_in", None, h, KD, take_u, t_h, 2 * D, n_behind=0, flush=False)
        project("sc_w_in", None, h, KD, take_b, t_h, 0, flush=False)
        consume, t_res = add_gated(g1b)
        project("sc_w_out", None, bz, KD, consume, t_bz)
        t_h = norm_apply(xT[:, :, :], a2b, sh2b, h, nr[:, :], t_res.rsqrt(nr[:, :]), t_a2)
        consume, t_res = add_gated(g2b)
        ffn(1, h, t_h, consume)

        all_behind()
        t_mod = toks2[23]
        sh1, sc1, g1c, sh2c, sc2c, g2c = (modr2[:, i * 8:i * 8 + 8] for i in range(6))
        a1c, a2c = vec(8), vec(8)
        t_a = scale_vec(a1c, sm("norm_mix"), sc1, t_mod)
        t_a2 = scale_vec(a2c, sm("norm_ffn"), sc2c, t_mod)
        t = norm_apply(xT[:, :, :], sm("final_g"), None, xT[:, :, :], nr[:, :], t_res.rsqrt(nr[:, :]))
        ms = MeanSq()
        for n in range(KD):
            ms.add(n, xT[:, n, :], t[n])
        t_h = norm_apply(xT[:, :, :], a1c, sh1, h, nr[:, :], ms.rsqrt(nr[:, :]), t_a)

        DTC, XPC, GTC = 6144, 6176, 7200
        xbc = ar(0, 32, T)
        xdt = ar(8192, 2, 2048)
        lt = ar(12288, 192)

        praw = [work[:, i * 1024:i * 1024 + 259] for i in range(4)]
        pacc = [work[:, i * 1024 + 260:i * 1024 + 516] for i in range(4)]
        t_pad = [dve.op(lambda e, i=i: e.memset(praw[i][:, 0:3], 0.0), t_h[-1]) for i in range(4)]
        p_used = [t_pad[3]] * 4
        cw, cb = sm("conv_w"), sm("conv_b")
        t_xbc = {}

        def take_xbc(n, b, t):
            i = n % 4
            raw, acc = praw[i], pacc[i]
            t = act.op(lambda e: e.activation(raw[:, 3:259], banks[b][:, 0:T], ACT.Copy), t, p_used[i])
            free[b] = t
            both.append((n, raw, acc, t))
            if len(both) == 2:
                ts = [dve.op(lambda e, n=n, raw=raw, acc=acc: e.tensor_scalar(
                    acc, raw[:, 0:256], cw[:, n:n + 1], cb[:, n:n + 1], ALU.mult, ALU.add), t) for n, raw, acc, t in both]
                for q in range(1, 4):
                    ts = [dve.op(lambda e, n=n, raw=raw, acc=acc, q=q: e.scalar_tensor_tensor(
                        out=acc, in0=raw[:, q:q + 256], scalar=cw[:, q * 32 + n:q * 32 + n + 1], in1=acc,
                        op0=ALU.mult, op1=ALU.add), t) for (n, raw, acc, _), t in zip(both, ts)]
                finish_xbc()
                for (n, _, acc, _), t in zip(both, ts):
                    todo_xbc.append(lambda n=n, acc=acc, t=t: t_xbc.__setitem__(n, silu_into(xbc[:, n, :], acc, t)))
                both.clear()

        both = []
        todo_xbc = []

        def finish_xbc():
            while todo_xbc:
                todo_xbc.pop(0)()
            for n, t in t_xbc.items():
                p_used[n % 4] = t

        project("w_in_2", None, h, KD, take_xbc, t_h, 2048, 512, flush=False)

        r, vdt, tok = tile("w_in_2", None, 0, KD, DTC, DTC + 32, "raw")
        pe.wait(tok, t_h[-1])
        b = bank()
        for m in range(2):
            t = chain(banks[b][:, m * 32:m * 32 + 32], [(nsq[:, k, m * P:(m + 1) * P], vdt[:, k, :]) for k in range(KD)])
        raw_free[r] = (t,)
        u_, dt_, a_ = (lt[:, i * 64:i * 64 + 64] for i in range(3))
        e_, w_, q_ = (nr[:, i * 64:i * 64 + 64] for i in range(3))
        b3 = lambda v: v.rearrange("p (c h) -> p c h", c=2)
        bc = lambda v: v.rearrange("p (o h) -> p o h", o=1).to_broadcast([P, 2, 32])
        pb = banks[b][:, 0:64].rearrange("p (c h) -> p c h", c=2)
        t = dve.op(lambda e: e.tensor_tensor(b3(u_), pb, bc(sm("dt_bias")), ALU.add), t)
        free[b] = t
        t = dve.op(lambda e: e.scalar_tensor_tensor(out=e_, in0=u_, scalar=-1.0, in1=u_, op0=ALU.mult, op1=ALU.max), t)
        t = act.op(lambda e: e.activation(e_, e_, ACT.Exp, scale=-1.0), t)
        t = dve.op(lambda e: e.tensor_scalar(w_, e_, 1.0, None, ALU.add), t)
        t = act.op(lambda e: e.activation(q_, w_, ACT.Ln), t)
        t = dve.op(lambda e: e.tensor_scalar(dt_, w_, 1.0, None, ALU.is_equal), t)
        t = dve.op(lambda e: e.tensor_tensor(q_, q_, dt_, ALU.add), t)
        t = dve.op(lambda e: e.scalar_tensor_tensor(out=w_, in0=w_, scalar=-1.0, in1=dt_, op0=ALU.add, op1=ALU.add), t)
        t = dve.op(lambda e: e.reciprocal(w_, w_), t)
        t = dve.op(lambda e: e.tensor_tensor(q_, q_, w_, ALU.mult), t)
        t = dve.op(lambda e: e.tensor_tensor(q_, q_, e_, ALU.mult), t)
        t_dt = dve.op(lambda e: e.scalar_tensor_tensor(out=dt_, in0=u_, scalar=0.0, in1=q_, op0=ALU.max, op1=ALU.add), t)
        A_ = vec(32)
        t = act.op(lambda e: e.activation(A_, sm("a_log"), ACT.Exp))
        t = dve.op(lambda e: e.tensor_scalar(A_, A_, -1.0, None, ALU.mult), t)
        t_av = dve.op(lambda e: e.tensor_tensor(b3(a_), b3(dt_), bc(A_), ALU.mult), t, t_dt)

        project("w_in_2", None, h, KD, lambda n, b, t: take_xbc(n + 4, b, t), t_h, 2560, 3584)
        finish_xbc()

        cs_ = u_
        b = bank()
        pe.wait(t_av)
        for c in range(2):
            t = mm_end(banks[b][:, c * 32:c * 32 + 32], triu, a_[:, c * 32:c * 32 + 32], True, True)
        t_cs = act.op(lambda e, b=b: e.activation(cs_, banks[b][:, 0:64], ACT.Copy), t)
        free[b] = t_cs

        nsf = nsq[:, :, :].rearrange("p k t -> p (k t)")
        Bt = nsf[:, 0:1024].rearrange("p (g n) -> p g n", g=8)
        t_xdt = {}
        for c in range(2):
            for q in range(4):
                b = bank()
                for j in range(4):
                    n = 4 * q + j
                    pe.wait(t_xbc[n])
                    o, i = banks[b][:, j * P:(j + 1) * P], xbc[:, n, c * P:(c + 1) * P]
                    t = pe.op(lambda e, o=o, i=i: e.transpose(o, i, ident))
                src = banks[b][:, :].rearrange("p (h d) -> p h d", d=64)
                dst = xdt[:, c, q * 512:(q + 1) * 512].rearrange("p (h d) -> p h d", d=64)
                dtb = dt_[:, c * 32 + q * 8:c * 32 + q * 8 + 8].rearrange("p (h o) -> p h o", o=1).to_broadcast([P, 8, 64])
                t_xdt[c, q] = dve.op(lambda e, src=src, dst=dst, dtb=dtb: e.tensor_tensor(dst, src, dtb, ALU.mult),
                                     t, t_dt)
                free[b] = t_xdt[c, q]
        for q in range(2):
            b = bank()
            for j in range(4):
                g = 4 * q + j
                pe.wait(t_xbc[16 + g])
                o, i = banks[b][:, j * P:(j + 1) * P], xbc[:, 16 + g, 0:P]
                t = pe.op(lambda e, o=o, i=i: e.transpose(o, i, ident))
            t_Bt = act.op(lambda e, b=b, q=q: e.activation(
                Bt[:, 4 * q:4 * q + 4, :], banks[b][:, :].rearrange("p (g n) -> p g n", g=4), ACT.Copy), t)
            free[b] = t_Bt

        Rs = [work[:, i * 2048:i * 2048 + 512].rearrange("p (r l) -> p r l", r=4) for i in range(2)]
        Ex = [work[:, i * 2048 + 512:i * 2048 + 1024].rearrange("p (r l) -> p r l", r=4) for i in range(2)]
        Ce = [work[:, i * 2048 + 1024:i * 2048 + 1536].rearrange("p (r l) -> p r l", r=4) for i in range(2)]
        CBm = [work[:, i * 2048 + 1536:i * 2048 + 1664] for i in range(2)]
        xdec = [work[:, i * 2048 + 1664:i * 2048 + 1920] for i in range(2)]
        dec = vec(8)
        Sg = [nsf[:, 1024 + i * 256:1280 + i * 256] for i in range(2)]
        buf_free = [list(p_used), list(p_used)]
        sg_free = [None, None]
        y_tok = {}
        dsk = sm("dskip")

        def decays(u):
            g, c = divmod(u, 2)
            i = u % 2
            b = bank()
            for r in range(4):
                h = c * 32 + 4 * g + r
                t = mm_end(banks[b][:, r * P:(r + 1) * P], a_[:, h:h + 1].to_broadcast([P, P]), triu, True, True)
            tR = act.op(lambda e: e.activation(Rs[i], banks[b][:, :].rearrange("p (r l) -> p r l", r=4), ACT.Copy),
                        t, *buf_free[i])
            free[b] = tR
            pe.wait(t_xbc[16 + g], t_xbc[24 + g])
            b2 = bank()
            t = mm_end(banks[b2][:, 0:P], xbc[:, 16 + g, c * P:(c + 1) * P], xbc[:, 24 + g, c * P:(c + 1) * P], True, True)
            tCB = dve.op(lambda e: e.tensor_tensor(CBm[i], banks[b2][:, 0:P], triu, ALU.mult), t, *buf_free[i])
            free[b2] = tCB
            if c == 0:
                h0 = 4 * g
                d4 = dec[:, 4 * (g % 2):4 * (g % 2) + 4]
                t = dve.op(lambda e: e.tensor_tensor(d4, Rs[i][:, :, 127], cs_[:, h0:h0 + 4], ALU.subtract), tR, t_cs)
                t = act.op(lambda e: e.activation(d4, d4, ACT.Exp), t)
                xv = xdt[:, 0, h0 * 64:h0 * 64 + 256].rearrange("p (r d) -> p r d", r=4)
                db = d4.rearrange("p (r o) -> p r o", o=1).to_broadcast([P, 4, 64])
                xd = xdec[i].rearrange("p (r d) -> p r d", r=4)
                tX = dve.op(lambda e: e.tensor_tensor(xd, xv, db, ALU.mult), t, t_xdt[0, g // 2])
                tC = None
            else:
                t = act.op(lambda e: e.activation(Ce[i], Rs[i], ACT.Exp), tR)
                cb_ = xbc[:, 24 + g, P:2 * P].rearrange("p (o l) -> p o l", o=1).to_broadcast([P, 4, P])
                tC = dve.op(lambda e: e.tensor_tensor(Ce[i], Ce[i], cb_, ALU.mult), t)
                tX = None
            for r in range(4):
                h = c * 32 + 4 * g + r
                t = dve.op(lambda e, r=r, h=h: e.tensor_scalar(Ex[i][:, r, :], Rs[i][:, r, :], cs_[:, h:h + 1], 0.0,
                                                               ALU.subtract, ALU.min), tR, t_cs)
            t = act.op(lambda e: e.activation(Ex[i], Ex[i], ACT.Exp), t)
            mb = CBm[i].rearrange("p (o l) -> p o l", o=1).to_broadcast([P, 4, P])
            tE = dve.op(lambda e: e.tensor_tensor(Ex[i], Ex[i], mb, ALU.mult), t, tCB)
            return tE, tX, tC

        y_bank = {}

        def outputs(u, toks):
            g, c = divmod(u, 2)
            i = u % 2
            tE, tX, tC = toks
            if c == 0:
                y_bank[g] = (bank(), bank())
                bs = bank()
                pe.wait(tX, t_Bt)
                t = mm_end(banks[bs][:, 0:256], Bt[:, g, :], xdec[i], True, True)
                t_S = act.op(lambda e: e.activation(Sg[g % 2], banks[bs][:, 0:256], ACT.Copy), t, sg_free[g % 2])
                free[bs] = t_S
                y_tok["S", g] = t_S
            pe.wait(tE, t_xdt[c, g // 2], tC, y_tok["S", g] if c else None)
            for r in range(4):
                bk = banks[y_bank[g][r // 2]]
                o = bk[64 * (r % 2):64 * (r % 2) + 64, c * P:(c + 1) * P]
                h = 4 * g + r
                t = mm_end(o, xdt[:, c, h * 64:h * 64 + 64], Ex[i][:, r, :], True, c == 0)
                if c:
                    t = mm_end(o, Sg[g % 2][:, r * 64:r * 64 + 64], Ce[i][:, r, :], False, True)
            buf_free[i] = [t]
            if c:
                sg_free[g % 2] = t
                for j in range(2):
                    n = 2 * g + j
                    bb = y_bank[g][j]
                    free[bb] = y_tok[n] = dve.op(lambda e, n=n, bb=bb: e.scalar_tensor_tensor(
                        out=xbc[:, n, :], in0=xbc[:, n, :], scalar=dsk[:, n:n + 1], in1=banks[bb][:, 0:T],
                        op0=ALU.mult, op1=ALU.add), t)

        yf = xbc[:, 0:16, :]
        flat = new_top("top_2", F32)
        zs = flat[:, 0:4096].rearrange("p (k t) -> p k t", k=16)
        gv_ = flat[:, 9216:11264].rearrange("p (k t) -> p k t", k=8)
        t_z = {}

        def take_z(n, b, t):
            free[b] = t_z[n] = act.op(lambda e: e.activation(zs[:, n, :], banks[b][:, 0:T], ACT.Copy), t)

        prev = None
        for u in range(17):
            cur = decays(u) if u < 16 else None
            if u % 2 == 0 and u < 16:
                g = u // 2
                project("w_in_2", None, h, KD, lambda n, b, t, g=g: take_z(2 * g + n, b, t), t_h, 256 * g, 256, flush=False)
            if u % 2 or u == 16:
                run_pend()
            if prev is not None:
                outputs(u - 1, prev)
            prev = cur

        t_scan = y_tok[15]
        ysq = ar(8192, 16, T)
        gy_ = ar(8192, 8, T)
        gu_ = ar(10240, 8, T)
        gg = sm("ssd_g")
        new_top("top_3", F32R)
        yT = Pair(4096, 16, T)
        t_y = []
        gn = {}

        def gate_y():
            for n in range(0, 16, 4):
                ns = slice(n, n + 4)
                t = act.op(lambda e, ns=ns: e.activation(zs[:, ns, :], zs[:, ns, :], ACT.Silu), t_z[n + 3])
                t = dve.op(lambda e, ns=ns: e.tensor_tensor(yf[:, ns, :], yf[:, ns, :], zs[:, ns, :], ALU.mult), t, t_scan)
                gn["sq", n // 4] = act.op(lambda e, ns=ns: e.activation(ysq[:, ns, :], yf[:, ns, :], ACT.Square), t)

        def group_means():
            for g in range(8):
                gn["mean"] = mean_sq(gv_[:, g, :], ones_g, 2, ysq[:, 2 * g:2 * g + 2, :], gn["sq", g // 2])
            gn["rsqrt"] = rsqrt(gv_, gy_, gu_, gn["mean"])

        def norm_y(half):
            for n in range(8 * half, 8 * half + 8, 2):
                for j in (n, n + 1):
                    t2 = dve.op(lambda e, j=j: e.scalar_tensor_tensor(out=yf[:, j, :], in0=yf[:, j, :],
                                                                      scalar=gg[:, j:j + 1], in1=gy_[:, j // 2, :],
                                                                      op0=ALU.mult, op1=ALU.mult), gn["rsqrt"])
                p = Pair.__new__(Pair)
                p.hi, p.lo = yT.hi[:, n:n + 2, :], yT.lo[:, n:n + 2, :]
                t_y.extend(split_into(p, yf[:, n:n + 2, :], t2))

        pp = [work[:, 512 + i * 1024:512 + i * 1024 + 272] for i in range(2)]
        pq = [[work[:, 512 + i * 1024 + 272:512 + i * 1024 + 544], work[:, 512 + i * 1024 + 544:512 + i * 1024 + 816]]
              for i in range(2)]
        pooled = ar(4096, KD, T)
        mixf = ar(6144, KD, T)
        mixp = Pair(0, KD, T)
        pz = [pool.op(lambda e, i=i: e.memset(pp[i][:, 0:16], 0.0), t_scan) for i in range(2)]
        pp_used = [pz[1], pz[1]]
        t_pool = {}

        def take_xp(n, b, t):
            i = n % 2
            t = act.op(lambda e: e.activation(pp[i][:, 16:272], banks[b][:, 0:T], ACT.Copy), t, pp_used[i])
            free[b] = t
            src, w, q = pp[i], 1, 0
            for step in range(n // 2 + 1):
                dst = pq[i][q]
                t = pool.op(lambda e, src=src, dst=dst, w=w: e.tensor_tensor(
                    dst[:, 2 * w:272], src[:, 2 * w:272], src[:, w:272 - w], ALU.add), t)
                src, w, q = dst, 2 * w, 1 - q
            g = n // 2
            iw = cn("invw", g * 16, g * 16 + 16)
            dst = pq[i][q]
            t0 = pool.op(lambda e: e.tensor_tensor(dst[:, 16:32], src[:, 16:32], iw, ALU.mult), t, t_cn)
            t = pool.op(lambda e: e.tensor_scalar(dst[:, 32:272], src[:, 32:272], 0.5 ** (g + 1), None, ALU.mult), t)
            t = pool.op(lambda e: e.tensor_tensor(pooled[:, n, :], dst[:, 16:272], pp[i][:, 16:272], ALU.subtract),
                        t0, t, t_scan)
            pp_used[i] = t_pool[n] = t

        for q in range(4):
            project("w_in_2", None, h, KD, lambda n, b, t, q=q: take_xp(2 * q + n, b, t), t_h, XPC + 256 * q, 256,
                    flush=False)
            (gate_y, group_means, lambda: norm_y(0), lambda: norm_y(1))[q]()

        gts = ar(8192, 16, T)
        t_gt = {}

        def take_gt(n, b, t):
            v = gts[:, n, :]
            free[b] = t_gt[n] = act.op(lambda e: e.activation(v, banks[b][:, 0:T], ACT.Sigmoid), t, t_y[-1])

        project("w_in_2", None, h, KD, take_gt, t_h, GTC, 2048, flush=False)

 
        psc = sm("pool_scale")
        t_mx = []
        for n in range(8):
            g, j = divmod(n, 2)
            if n % 4 == 0:
                r, vp, tok = tile("pool_w_2", None, n, n + 4, 0, 256, "raw")
                pe.wait(tok)
            pe.wait(t_pool[2 * g], t_pool[2 * g + 1])
            b = bank()
            t = chain(banks[b][:, 0:T], [(vp[:, 2 * g + k - n // 4 * 4, j * P:(j + 1) * P], pooled[:, 2 * g + k, :]) for k in range(2)])
            t1 = dve.op(lambda e, n=n, b=b: e.tensor_scalar(mixf[:, n, :], banks[b][:, 0:T], psc[:, n:n + 1], None,
                                                            ALU.mult), t)
            free[b] = t1
            q = Pair.__new__(Pair)
            q.hi, q.lo = mixp.hi[:, n:n + 1, :], mixp.lo[:, n:n + 1, :]
            t_mx += split_into(q, mixf[:, n:n + 1, :], t1)
            raw_free[r] = (t,)

        t_m1 = {}

        def take_ssd(n, b, t):
            free[b] = t_m1[n] = dve.op(lambda e: e.tensor_tensor(gts[:, n, :], banks[b][:, 0:T], gts[:, n, :], ALU.mult),
                                       t, t_gt[n])

        project("w_br_ssd_2", None, yT, 16, take_ssd, t_y, flush=False)
        t_m2 = []
        mix = Pair(4096, KD, T)

        def take_pool(n, b, t):
            t = dve.op(lambda e: e.tensor_tensor(gts[:, 8 + n, :], banks[b][:, 0:T], gts[:, 8 + n, :], ALU.mult),
                       t, t_gt[8 + n])
            free[b] = t
            t = dve.op(lambda e: e.tensor_tensor(gts[:, n, :], gts[:, n, :], gts[:, 8 + n, :], ALU.add), t, t_m1[n])
            q = Pair.__new__(Pair)
            q.hi, q.lo = mix.hi[:, n:n + 1, :], mix.lo[:, n:n + 1, :]
            t_m2.extend(split_into(q, gts[:, n:n + 1, :], t))

        project("w_br_pool_2", None, mixp, KD, take_pool, t_mx, flush=False)
        consume, t_res = add_gated(g1c)
        project("w_out_2", None, mix, KD, consume, t_m2)

        active[0] = [0, 1, 2, 3]
        t_u = norm_apply(xT[:, :, :], a2c, sh2c, h, nr[:, :], t_res.rsqrt(nr[:, :]), t_a2)
        wT = ar(1024, T)[0:64, :]
        scs = ar(0, 128)
        cho = ar(128, 128)
        msk = ar(256, 128)
        m8 = ar(384, 2, 64)
        gsc = ar(512, 16)
        gv = ar(528, 16)
        rpl = ar(544, 128)
        gmk = ar(672, 16)
        top = ar(688, 16)
        den = ar(704, 2)
        wts = ar(706, 128)
        three = lambda v, a: v.rearrange("p (a b) -> p a b", a=a)
        def logits():
            r, vr, tok = tile("w_router_2", None, 0, KD, 0, 64, "raw")
            pe.wait(tok, t_u[-1])
            b = bank()
            for m in range(2):
                t = chain(banks[b][:, m * 64:m * 64 + 64], [(nsq[:, k, m * P:(m + 1) * P], vr[:, k, :]) for k in range(KD)])
            raw_free[r] = (t,)
            lg = banks[b][:, 0:128]
            t = act.op(lambda e: e.activation(scs, lg, ACT.Exp, scale=-1.0), t)
            free[b] = t
            t = dve.op(lambda e: e.tensor_scalar(scs, scs, 1.0, None, ALU.add), t)
            t = dve.op(lambda e: e.reciprocal(scs, scs), t)
            rb = sm("router_bias").rearrange("p (o n) -> p o n", o=1).to_broadcast([P, 2, 64])
            t = dve.op(lambda e: e.tensor_tensor(three(cho, 2), three(scs, 2), rb, ALU.add), t)
            return bank(), t

        def route(m, t, bw):
            cm = cho[:, m * 64:m * 64 + 64]
            sm_ = scs[:, m * 64:m * 64 + 64]
            mk = msk[:, m * 64:m * 64 + 64]
            wm = wts[:, m * 64:m * 64 + 64]
            for g in range(8):
                tg = dve.op(lambda e, g=g: e.max(m8[:, m, g * 8:g * 8 + 8], cm[:, g * 8:g * 8 + 8]), t)
            m3 = three(m8[:, m, :], 8)
            gs, gvm, gmm, tp = (v[:, m * 8:m * 8 + 8] for v in (gsc, gv, gmk, top))
            t2 = dve.op(lambda e: e.tensor_tensor(gs, m3[:, :, 0], m3[:, :, 1], ALU.add), tg)
            t2 = dve.op(lambda e: e.max(gvm, gs), t2)
            t2 = dve.op(lambda e: e.memset(gvm[:, 4:8], BIG), t2)
            t2 = dve.op(lambda e: e.match_replace(gmm, gvm, gs, -BIG), t2)
            t2 = dve.op(lambda e: e.tensor_tensor(gmm, gmm, gs, ALU.not_equal), t2)
            gb = gmm.rearrange("p (g o) -> p g o", o=1).to_broadcast([P, 8, 8])
            t3 = dve.op(lambda e: e.tensor_scalar(gs, gmm, 1.0, BIG, ALU.subtract, ALU.mult), t2)
            t2 = dve.op(lambda e: e.tensor_tensor(three(mk, 8), three(cm, 8), gb, ALU.mult), t2)
            gsb = gs.rearrange("p (g o) -> p g o", o=1).to_broadcast([P, 8, 8])
            t2 = dve.op(lambda e: e.tensor_tensor(three(mk, 8), three(mk, 8), gsb, ALU.add), t2, t3)
            t2 = dve.op(lambda e: e.max(tp, mk), t2)
            rp = rpl[:, m * 64:m * 64 + 64]
            t2 = dve.op(lambda e: e.match_replace(rp, tp, mk, -3e30), t2)
            t2 = dve.op(lambda e: e.tensor_tensor(rp, rp, mk, ALU.not_equal), t2)
            t2 = dve.op(lambda e: e.tensor_tensor(wm, rp, sm_, ALU.mult), t2)
            dm = den[:, m:m + 1]
            t2 = dve.op(lambda e: e.tensor_reduce(dm, wm, AX, ALU.add), t2)
            t2 = dve.op(lambda e: e.reciprocal(dm, dm), t2)
            t2 = dve.op(lambda e: e.tensor_scalar(wm, wm, dm, 2.5, ALU.mult, ALU.mult), t2)
            pe.wait(t2)
            return pe.op(lambda e: e.transpose(banks[bw][0:64, m * P:(m + 1) * P], wm, ident))

        t_wT = []
        routing = []

        def route_first():
            routing.extend(logits())
            route(0, routing[1], routing[0])

        def route_second():
            bw = routing[0]
            t = route(1, routing[1], bw)
            t_wT.append(act.op(lambda e: e.activation(wT, banks[bw][0:64, 0:T], ACT.Copy), t))
            free[bw] = t_wT[0]

        for b in range(4, 8):
            pe.wait(free[b])
        hidE = [Pair(4096 + i * 1024, 2, T) for i in range(2)]
        wrow = [ar(1280 + i * 256, T) for i in range(2)]
        hid_used = [t_u[-1], t_u[-1]]
        wrow_used = [None, None]
        acc = [banks[4 + n // 2][:, (n % 2) * T:(n % 2) * T + T] for n in range(8)]

        def shared_bank(todo):
            for n, (o, l, x, st, en, w) in enumerate(todo):
                pe.wait(*w)
                (pe.op if n == len(todo) - 1 else pe.quiet)(
                    lambda e, o=o, l=l, x=x, st=st, en=en: e.matmul(o, l, x, start=st, stop=en, skip_group_check=True))
            return (pe.sem, pe.count)

        def expert_in(i):
            q = i % 2
            extra = None
            names = ("ws_gate_2", "ws_up_2") if i == 0 else ("we_gate_2", "we_up_2")
            lead = None if i == 0 else i - 1

            def weights():
                bw = bank()
                pe.wait(t_wT[0])
                t = mm_end(banks[bw][:, 0:T], ident[0:64, lead:lead + 1].to_broadcast([64, P]), wT, True, True)
                t = act.op(lambda e: e.activation(wrow[q], banks[bw][:, 0:T], ACT.Copy), t, wrow_used[q])
                free[bw] = t
                return wrow[q].rearrange("p (o t) -> p o t", o=1).to_broadcast([P, 2, T]), t

            if i > 1:
                extra = weights()
            fin = None
            for name in names:
                b = bank()
                for k0 in (0, 4):
                    sq, hi, lo, tw = tile(name, lead, k0, k0 + 4, 0, 256)
                    todo = []
                    for j in range(2):
                        for k in range(4):
                            cs = slice(j * P, (j + 1) * P)
                            for m, (l, x, *w) in enumerate(products((hi[:, k, cs], lo[:, k, cs]), h.at(k0 + k),
                                                                    tw, t_u[k0 + k])):
                                todo.append((banks[b][:, j * T:(j + 1) * T], l, x, k0 + k + j + m == 0,
                                             k0 + k == 7 and m == 2, w))
                    t = split_free[sq] = shared_bank(todo)
                ps = three(banks[b][:, :], 2)
                if fin is None:
                    act.wait(hid_used[q])
                    dve.wait(hid_used[q])
                    if i == 0:
                        route_first()
                    free[b], fin = gated(hidE[q], 0, ps, None, t, None)
                else:
                    if i == 0:
                        route_second()
                    elif i == 1:
                        extra = weights()
                    free[b], toks = fin(ps, t, extra)
            wrow_used[q] = toks[-1]
            return toks

        def expert_out(i, t_hid, first, last):
            q = i % 2
            for n0 in (0, 4):
                sq, hi, lo, tw = tile("ws_down_2" if i == 0 else "we_down_2", None if i == 0 else i - 1, 0, 2,
                                      n0 * P, n0 * P + 512)
                todo = []
                for n in range(n0, n0 + 4):
                    for k in range(2):
                        cs = slice((n - n0) * P, (n - n0 + 1) * P)
                        for m, (l, x, *w) in enumerate(products((hi[:, k, cs], lo[:, k, cs]), hidE[q].at(k), tw, t_hid[k])):
                            todo.append((acc[n], l, x, first and k == 0 and m == 0 and n % 2 == 0,
                                         last and k == 1 and m == 2, w))
                t = split_free[sq] = shared_bank(todo)
            hid_used[q] = t
            return t

        prev = None
        for i in range(NE + 2):
            cur = expert_in(i) if i <= NE else None
            if prev is not None:
                t_acc = expert_out(i - 1, prev, i == 1, i == NE + 1)
            prev = cur

        ms = MeanSq()
        for n in range(8):
            t = dve.op(lambda e, n=n: e.scalar_tensor_tensor(out=xT[:, n, :], in0=acc[n], scalar=g2c[:, n:n + 1],
                                                             in1=xT[:, n, :], op0=ALU.mult, op1=ALU.add), t_acc)
            ms.add(n, xT[:, n, :], t)
        t = norm_apply(xT[:, :, :], sm("final_g2"), None, None, nr[:, :], ms.rsqrt(nr[:, :]))
        s_out = sem("s_out")
        for k in range(0, KD, 2):
            sp.quiet(lambda e, k=k: e.dma_start(out[k * P:(k + 2) * P, :].rearrange("(k p) t -> p k t", p=P),
                                                nsq[:, k:k + 2, :]).then_inc(s_out, 16), t[k + 1])
        sp.wait((s_out, 64))
        if plan is None:
            return order

        block = ctx.enter_context(nc.Block())
        block.sync(sp.run)
        block.scalar(act.run)
        block.vector(dve.run)
        block.gpsimd(pool.run)
        block.tensor(pe.run)


def _cols(v):
    return np.ascontiguousarray(v.reshape(-1, P).T)


def _constants():
    f = np.float32
    tok = np.arange(T)
    inv = (1.0 / (f(10000.0) ** (np.arange(0, 32, 2, dtype=f) / f(32)))).astype(f)
    ang = np.concatenate([(tok // 64).astype(f)[:, None] * inv, (tok % 64).astype(f)[:, None] * inv], axis=-1)
    d = np.arange(P) % 64
    idx = (d // 32) * 16 + d % 16
    sign = np.where(d % 32 < 16, -1.0, 1.0).astype(f)
    cos = np.cos(ang).astype(f)[:, idx].T
    sin = np.sin(ang).astype(f)[:, idx].T * sign[:, None]
    invw = np.stack([1.0 / np.minimum(tok + 1, w) for w in (2, 4, 8, 16)]).astype(f)[:, 0:16].reshape(1, -1)
    return np.concatenate([np.eye(P, dtype=f), np.triu(np.ones((P, P), f)), cos, sin,
                           np.broadcast_to(invw, (P, 64))], axis=1).astype(f)


def kernel(**inputs):
    import concourse.bacc as bacc
    from concourse.bass_utils import run_bass_kernel_spmd

    a = {k: np.asarray(v) for k, v in inputs.items()}
    row = lambda v: np.broadcast_to(v.reshape(1, -1), (P, v.size))
    small = np.concatenate([
        _cols(a["c"]), _cols(a["c_ctx"]), _cols(a["c_2"]), _cols(a["ada_b"][0]), _cols(a["ada_b"][1]),
        _cols(a["b_ada_2"]), _cols(a["norm1_g"][0]), _cols(a["norm1_g"][1]), _cols(a["norm2_g"][0]),
        _cols(a["norm2_g"][1]), _cols(a["final_g"]), _cols(a["da_subln_g"]), _cols(a["sc_conv_w"]),
        _cols(a["norm_mix_g_2"]), _cols(a["conv_w_2"]), _cols(a["conv_b_2"]),
        _cols(np.repeat(a["D_skip_2"][0], 64)), _cols(a["ssd_norm_g_2"]), _cols(a["pool_scale_2"]),
        _cols(a["norm_ffn_g_2"]), _cols(a["final_norm_g_2"]), row(a["dt_bias_2"]), row(a["A_log_2"]),
        row(a["router_bias_2"]), row(a["da_lambda"]),
    ], axis=1)
    arrays = {
        "small": np.ascontiguousarray(small), "const": _constants(),
        "xT": np.ascontiguousarray(a["x"][0].T), "ctxT": np.ascontiguousarray(a["ctx"][0].T),
    }
    for name in ("ada_w", "ffn_w_in", "ffn_w_out"):
        arrays[name] = np.ascontiguousarray(a[name])
    for name in ("da_wqkv", "da_wo", "sc_w_in", "sc_w_out", "w_ada_2", "w_in_2", "pool_w_2", "w_br_ssd_2",
                 "w_br_pool_2", "w_out_2", "w_router_2", "we_gate_2", "we_up_2", "we_down_2",
                 "ws_gate_2", "ws_up_2", "ws_down_2"):
        arrays[name] = np.ascontiguousarray(a[name][0])
    plan = None
    for _ in range(2):
        nc = bacc.Bacc("TRN2", target_bir_lowering=False, num_devices=1)
        I = {k: nc.dram_tensor(f"in_{k}", v.shape, F32, kind="ExternalInput").ap() for k, v in arrays.items()}
        out = nc.dram_tensor("out_0", (D, T), F32, kind="ExternalOutput").ap()
        plan = program(nc, I, out, plan)
    r = run_bass_kernel_spmd(nc, [{f"in_{k}": v for k, v in arrays.items()}], core_ids=[0])
    return np.ascontiguousarray(r.results[0]["out_0"].T)[None]
```
